# Optimizing a Trainium2 kernel written in Bass

```python
import math
import jax
import jax.numpy as jnp
from jax import lax
import numpy as np

D_MODEL = 1024
BATCH = 1
SEQ = 256
DEPTH = 2

N_A = DEPTH // 2
N_B = DEPTH - N_A
N_DENSE = (DEPTH + 1) // 2
N_MOE = DEPTH // 2
N_MOD = 6

MLA_HEADS = 16
MLA_Q_RANK = 384
MLA_KV_RANK = 256
MLA_NOPE = 64
MLA_ROPE = 32
MLA_V = 64
MLA_QK = MLA_NOPE + MLA_ROPE
MLA_IN = MLA_Q_RANK + MLA_KV_RANK + MLA_ROPE
ROPE_THETA = 10000.0
Q_BLOCK = 128

DIL_PATTERNS = ((128, 1), (512, 4), (2048, 16))
DIL_GROUPS = len(DIL_PATTERNS)
DIL_HEADS = 8
DIL_HEAD_DIM = 64
DIL_BLOCK = 128
DIL_Q = DIL_GROUPS * DIL_HEADS * DIL_HEAD_DIM
DIL_KV = 2 * DIL_Q
DIL_OUT = DIL_HEADS * DIL_HEAD_DIM

RPB_BUCKETS = 32
RPB_MAX_DIST = 2048

D_FF = 2816
N_EXPERTS = 8
TOP_K = 2
EPS = 1e-6

kernel_name = "yoco_mla_dilated_moe_hybrid"

def rmsnorm(x, g):
    xf = x.astype(jnp.float32)
    y = xf * lax.rsqrt(jnp.mean(xf * xf, axis=-1, keepdims=True) + EPS)
    return (y * g.astype(jnp.float32)).astype(x.dtype)

def modulate(h, shift, scale):
    return h * (1 + scale[:, None, :]) + shift[:, None, :]

def apply_rope(x, cos, sin):
    xf = x.astype(jnp.float32)
    x1, x2 = jnp.split(xf, 2, axis=-1)
    return jnp.concatenate([x1 * cos - x2 * sin, x1 * sin + x2 * cos], axis=-1).astype(x.dtype)

def swiglu(h, w_gu, w_down):
    gate, up = jnp.split(h @ w_gu, 2, axis=-1)
    return (jax.nn.silu(gate) * up) @ w_down

def causal_attention(q, k, v, scale):
    B, S, H, Dk = q.shape
    nb = S // Q_BLOCK
    qb = q.reshape(B, nb, Q_BLOCK, H, Dk).transpose(1, 0, 2, 3, 4)
    k_pos = jnp.arange(S)

    def one_block(args):
        i, qi = args
        s = jnp.einsum('bqhd,bkhd->bhqk', qi, k, preferred_element_type=jnp.float32) * scale
        q_pos = i * Q_BLOCK + jnp.arange(Q_BLOCK)
        s = jnp.where(k_pos[None, :] <= q_pos[:, None], s, -jnp.inf)
        p = jax.nn.softmax(s, axis=-1)
        return jnp.einsum('bhqk,bkhd->bqhd', p.astype(v.dtype), v)

    o = lax.map(one_block, (jnp.arange(nb), qb))
    return o.transpose(1, 0, 2, 3, 4).reshape(B, S, H, v.shape[-1])

def mla(hn, positions, w_in, g_q, w_q_up, g_kv, w_kv_up, w_out):
    B, S, _ = hn.shape
    q_lat, kv_lat, k_rope = jnp.split(hn @ w_in, [MLA_Q_RANK, MLA_Q_RANK + MLA_KV_RANK], axis=-1)
    q = (rmsnorm(q_lat, g_q) @ w_q_up).reshape(B, S, MLA_HEADS, MLA_QK)
    kv = (rmsnorm(kv_lat, g_kv) @ w_kv_up).reshape(B, S, MLA_HEADS, MLA_NOPE + MLA_V)
    q_nope, q_rope = jnp.split(q, [MLA_NOPE], axis=-1)
    k_nope, v = jnp.split(kv, [MLA_NOPE], axis=-1)
    inv_freq = ROPE_THETA ** (-jnp.arange(0, MLA_ROPE, 2, dtype=jnp.float32) / MLA_ROPE)
    ang = positions.astype(jnp.float32)[..., None] * inv_freq
    cos, sin = jnp.cos(ang), jnp.sin(ang)
    q_rope = apply_rope(q_rope, cos[:, :, None], sin[:, :, None])
    k_rope = apply_rope(k_rope, cos, sin)
    q = jnp.concatenate([q_nope, q_rope], axis=-1)
    k = jnp.concatenate([k_nope, jnp.broadcast_to(k_rope[:, :, None], (B, S, MLA_HEADS, MLA_ROPE))], axis=-1)
    o = causal_attention(q, k, v, MLA_QK ** -0.5)
    return o.reshape(B, S, MLA_HEADS * MLA_V) @ w_out

def rpb_bucket(dist):
    exact = RPB_BUCKETS // 2
    d = jnp.maximum(dist, 0)
    d_f = jnp.maximum(d, 1).astype(jnp.float32)
    large = exact + (jnp.log(d_f / exact) / math.log(RPB_MAX_DIST / exact)
                     * (RPB_BUCKETS - exact)).astype(jnp.int32)
    return jnp.where(d < exact, d, jnp.minimum(large, RPB_BUCKETS - 1))

def dilated_group(q, k, v, table, span, dil):
    B, S, H, Dh = q.shape
    n = S // dil
    nb = -(-n // DIL_BLOCK)
    n_pad = nb * DIL_BLOCK

    def to_sub(t):
        t = t.reshape(B, n, dil, H, Dh).transpose(0, 2, 1, 3, 4)
        return jnp.pad(t, ((0, 0), (0, 0), (0, n_pad - n), (0, 0), (0, 0)))

    def band(t):
        t = jnp.pad(t, ((0, 0), (0, 0), (DIL_BLOCK, 0), (0, 0), (0, 0)))
        prev = t[:, :, :n_pad].reshape(B, dil, nb, DIL_BLOCK, H, Dh)
        cur = t[:, :, DIL_BLOCK:].reshape(B, dil, nb, DIL_BLOCK, H, Dh)
        return jnp.concatenate([prev, cur], axis=3)

    qs = to_sub(q).reshape(B, dil, nb, DIL_BLOCK, H, Dh)
    ks = band(to_sub(k))
    vs = band(to_sub(v))

    dist = jnp.arange(DIL_BLOCK)[:, None] + DIL_BLOCK - jnp.arange(2 * DIL_BLOCK)[None, :]
    key_idx = (jnp.arange(nb)[:, None] - 1) * DIL_BLOCK + jnp.arange(2 * DIL_BLOCK)[None, :]
    mask = ((dist >= 0) & (dist <= span))[None] & (key_idx >= 0)[:, None, :]
    bias = jnp.transpose(table[rpb_bucket(dist * dil)], (2, 0, 1)).astype(jnp.float32)

    s = jnp.einsum('brnqhd,brnkhd->brnhqk', qs, ks, preferred_element_type=jnp.float32)
    s = s * (DIL_HEAD_DIM ** -0.5) + bias
    s = jnp.where(mask[None, None, :, None], s, -jnp.inf)
    m = jnp.max(s, axis=-1, keepdims=True)
    p = jnp.exp(s - m)
    l = jnp.sum(p, axis=-1, keepdims=True)
    o = jnp.einsum('brnhqk,brnkhd->brnqhd', p.astype(v.dtype), vs, preferred_element_type=jnp.float32)
    o = o / jnp.transpose(l, (0, 1, 2, 4, 3, 5))
    lse = jnp.transpose((m + jnp.log(l))[..., 0], (0, 1, 2, 4, 3))

    def from_sub(t):
        t = t.reshape((B, dil, n_pad) + t.shape[4:])[:, :, :n]
        t = jnp.swapaxes(t, 1, 2)
        return t.reshape((B, S) + t.shape[3:])

    return from_sub(o), from_sub(lse)

def shared_kv(h, c_act, g, w_ada_kv, b_ada_kv, w_kv):
    B, S, _ = h.shape
    shift, scale = jnp.split(c_act @ w_ada_kv + b_ada_kv, 2, axis=-1)
    hn = modulate(rmsnorm(h, g), shift, scale)
    return (hn @ w_kv).reshape(B, S, DIL_GROUPS, 2, DIL_HEADS, DIL_HEAD_DIM)

def dilated_attention(hn, kv_b, w_q, w_o, rpb_table):
    B, S, _ = hn.shape
    q = (hn @ w_q).reshape(B, S, DIL_GROUPS, DIL_HEADS, DIL_HEAD_DIM)
    outs, lses = [], []
    for g, (window, dil) in enumerate(DIL_PATTERNS):
        table = rpb_table[:, g * DIL_HEADS:(g + 1) * DIL_HEADS]
        o, lse = dilated_group(q[:, :, g], kv_b[:, :, g, 0], kv_b[:, :, g, 1], table, window // dil, dil)
        outs.append(o)
        lses.append(lse)
    wts = jax.nn.softmax(jnp.stack(lses, axis=0), axis=0)
    o = jnp.sum(jnp.stack(outs, axis=0) * wts[..., None], axis=0)
    return o.reshape(B, S, DIL_OUT).astype(hn.dtype) @ w_o

def moe(h, w_router, w_gu, w_down):
    logits = (h @ w_router).astype(jnp.float32)
    top_val, top_idx = lax.top_k(logits, TOP_K)
    gates = jax.nn.softmax(top_val, axis=-1)
    dense_gates = jnp.sum(jax.nn.one_hot(top_idx, N_EXPERTS, dtype=jnp.float32) * gates[..., None], axis=-2)
    out = jnp.zeros_like(h)
    for e in range(N_EXPERTS):
        out = out + dense_gates[..., e:e + 1].astype(h.dtype) * swiglu(h, w_gu[e], w_down[e])
    return out

def setup_inputs(seed: int = 0) -> dict:
    key = jax.random.key(seed)
    kit = iter(jax.random.split(key, 40))

    def w(shape, fan_in, scale=1.0):
        return (scale * fan_in ** -0.5) * jax.random.normal(next(kit), shape, jnp.float32)

    def gain(shape):
        return 1.0 + 0.05 * jax.random.normal(next(kit), shape, jnp.float32)

    def small(shape, s=0.02):
        return s * jax.random.normal(next(kit), shape, jnp.float32)

    D = D_MODEL
    x = jax.random.normal(next(kit), (BATCH, SEQ, D), jnp.float32)
    c = jax.random.normal(next(kit), (BATCH, D), jnp.float32)
    positions = (jax.random.randint(next(kit), (BATCH, 1), 0, 4096, dtype=jnp.int32)
                 + jnp.arange(SEQ, dtype=jnp.int32)[None, :])
    return {
        "x": x,
        "c": c,
        "positions": positions,
        "g_mix": gain((DEPTH, D)),
        "g_ffn": gain((DEPTH, D)),
        "w_ada": w((DEPTH, D, N_MOD * D), D, 0.5),
        "b_ada": small((DEPTH, N_MOD * D)),
        "w_mla_in": w((N_A, D, MLA_IN), D),
        "g_mla_q": gain((N_A, MLA_Q_RANK)),
        "w_mla_q_up": w((N_A, MLA_Q_RANK, MLA_HEADS * MLA_QK), MLA_Q_RANK),
        "g_mla_kv": gain((N_A, MLA_KV_RANK)),
        "w_mla_kv_up": w((N_A, MLA_KV_RANK, MLA_HEADS * (MLA_NOPE + MLA_V)), MLA_KV_RANK),
        "w_mla_out": w((N_A, MLA_HEADS * MLA_V, D), MLA_HEADS * MLA_V),
        "g_kv_b": gain((D,)),
        "w_ada_kv": w((D, 2 * D), D, 0.5),
        "b_ada_kv": small((2 * D,)),
        "w_kv_b": w((D, DIL_KV), D),
        "rpb_table": small((RPB_BUCKETS, DIL_GROUPS * DIL_HEADS), 0.2),
        "w_q_b": w((N_B, D, DIL_Q), D),
        "w_o_b": w((N_B, DIL_OUT, D), DIL_OUT),
        "w_ffn_gu": w((N_DENSE, D, 2 * D_FF), D),
        "w_ffn_down": w((N_DENSE, D_FF, D), D_FF),
        "w_router": w((N_MOE, D, N_EXPERTS), D),
        "w_exp_gu": w((N_MOE, N_EXPERTS, D, 2 * D_FF), D),
        "w_exp_down": w((N_MOE, N_EXPERTS, D_FF, D), D_FF),
        "g_final": gain((D,)),
    }

def reference(x, c, positions, g_mix, g_ffn, w_ada, b_ada,
              w_mla_in, g_mla_q, w_mla_q_up, g_mla_kv, w_mla_kv_up, w_mla_out,
              g_kv_b, w_ada_kv, b_ada_kv, w_kv_b, rpb_table, w_q_b, w_o_b,
              w_ffn_gu, w_ffn_down, w_router, w_exp_gu, w_exp_down, g_final):
    c_act = jax.nn.silu(c)
    h = x
    kv_b = None
    for layer in range(DEPTH):
        if layer == N_A:
            kv_b = shared_kv(h, c_act, g_kv_b, w_ada_kv, b_ada_kv, w_kv_b)
        mod = c_act @ w_ada[layer] + b_ada[layer]
        sh_m, sc_m, gt_m, sh_f, sc_f, gt_f = jnp.split(mod, N_MOD, axis=-1)
        hn = modulate(rmsnorm(h, g_mix[layer]), sh_m, sc_m)
        if layer < N_A:
            y = mla(hn, positions, w_mla_in[layer], g_mla_q[layer], w_mla_q_up[layer],
                    g_mla_kv[layer], w_mla_kv_up[layer], w_mla_out[layer])
        else:
            j = layer - N_A
            y = dilated_attention(hn, kv_b, w_q_b[j], w_o_b[j], rpb_table)
        h = h + gt_m[:, None, :] * y
        hn = modulate(rmsnorm(h, g_ffn[layer]), sh_f, sc_f)
        if layer % 2 == 0:
            y = swiglu(hn, w_ffn_gu[layer // 2], w_ffn_down[layer // 2])
        else:
            y = moe(hn, w_router[layer // 2], w_exp_gu[layer // 2], w_exp_down[layer // 2])
        h = h + gt_f[:, None, :] * y
    return rmsnorm(h, g_final)


_drawn_inputs = setup_inputs


def setup_inputs(seed=0):
    import zlib

    import numpy as np

    out = dict(_drawn_inputs(seed))
    spreads = {}
    factors = {'g_mix': 7.045,
     'g_mla_q': 7.918,
     'g_mla_kv': 4.374,
     'g_kv_b': 6.866,
     'b_ada_kv': 4.823,
     'rpb_table': 3.389}
    for name, (base, spread) in spreads.items():
        noise = np.random.default_rng([zlib.crc32(name.encode()), seed]).standard_normal(out[name].shape)
        drawn = base * np.exp(spread * noise) if base else spread * noise
        out[name] = jnp.asarray(drawn.astype(out[name].dtype))
    for name, factor in factors.items():
        out[name] = (out[name] * factor).astype(out[name].dtype)
    return out
```

```python
from contextlib import ExitStack

import concourse.bass as bass
from concourse import mybir

F32 = mybir.dt.float32
BF16 = mybir.dt.bfloat16
I32 = mybir.dt.int32
ALU = mybir.AluOpType
ACT = mybir.ActivationFunctionType
AX_X = mybir.AxisListType.X

P = 128
D = 1024
T = 256
TB = T // P
KT = D // P
FF = 2816
HALF = FF // 2
JT = HALF // P
NCH = (JT + 1) // 2
NE = 8
HEADS = 16
NOPE, ROPE, VD = 64, 32, 64
QK = NOPE + ROPE
QR, KVR = 384, 256
QRT, KVT = QR // P, KVR // P
GROUPS, SLOTS, HD = 3, 8, 64
DILATIONS = (1, 4, 16)
SPANS = (128, 128, 128)
BUCKETS = 32
DQ = SLOTS * HD
NREL = 384
EPS = 1e-6
BIG = 1e30
HUGE = 3e38
WIDTHS = (64, 96, 128, T)
RING, SLOT = 9, 2048
ADAS, BLOCKS = 4, 14
TWO_PI_HI, TWO_PI_MID = 6.28125, 0.0019350051879882812
ROUND = 12582912.0

C_ID, C_PERM, C_OPEN, C_CAUSAL, C_BEFORE, C_IOTA, C_FREQ, NCONST = 0, 128, 160, 288, 416, 544, 800, 801
V_C, V_MIX, V_FFN, V_KV, V_FINAL, V_LQ, V_LKV, NVEC = 0, 8, 24, 40, 48, 56, 59, 61
SH_M, SC_M, GT_M, SH_F, SC_F, GT_F = range(6)
KV_SH, KV_SC, L1 = 6, 7, 8


def trunk(nc, x, c, positions, g_mix, g_ffn, w_ada, b_ada, w_mla_in, g_mla_q, w_mla_q_up, g_mla_kv,
          w_mla_kv_up, w_mla_out, g_kv_b, w_ada_kv, b_ada_kv, w_kv_b, rpb_table, w_q_b, w_o_b,
          w_ffn_gu, w_ffn_down, w_router, w_exp_gu, w_exp_down, g_final, consts, onehot, relmask, out):
    ctx = ExitStack()
    with ctx:
        def sb(name, shape, dt=F32):
            return ctx.enter_context(nc.sbuf_tensor(name, shape, dt))

        def sem(name):
            return ctx.enter_context(nc.semaphore(name))

        bank = [ctx.enter_context(nc.psum_tensor(f"bank{i}", [P, 512], F32)) for i in range(4)]
        wide = ctx.enter_context(nc.psum_tensor("wide", [P, 2048], F32))
        upper = [wide[:, 512 * i:512 * (i + 1)] for i in range(4)]

        hT = sb("hT", [P, KT, T])
        nT = sb("nT", [P, KT, T])
        sqT = sb("sqT", [P, KT, T])
        ring = sb("ring", [P, RING, SLOT])
        strip = sb("strip", [P, ADAS, D])
        adasum = sb("adasum", [P, 2, D])
        arena = sb("arena", [P, 18432])
        con = sb("con", [P, NCONST])
        ones = sb("ones", [P, P])
        zeros = sb("zeros", [1, 512], BF16)
        vrows = sb("vrows", [NVEC, P])
        brows = sb("brows", [BLOCKS * KT, P])
        vec = sb("vec", [P, NVEC])
        bcol = sb("bcol", [P, BLOCKS * KT])
        mod = sb("mod", [P, BLOCKS * KT])
        cact = sb("cact", [P, KT])
        ascale = sb("ascale", [P, 5, KT])
        eps = sb("eps", [P, 1])
        std = sb("std", [P, 2, T])
        rstd = sb("rstd", [P, 2, T])
        trig = sb("trig", [P, 2, T])
        rsum = sb("rsum", [P, TB, HEADS])
        rinv = sb("rinv", [P, TB, HEADS])
        nmax = sb("nmax", [P, TB, HEADS])
        npart = sb("npart", [P, SLOTS])
        wrout = sb("wrout", [P, KT, NE])
        table = sb("table", [BUCKETS, GROUPS * SLOTS])
        small = sb("small", [P, 12, TB, NE + 1])
        counts = sb("counts", [1, NE], I32)
        scratch = nc.dram_tensor("relbias", [SLOTS, GROUPS, P, NREL], F32, kind="Internal").ap()

        def area(at, *shape):
            size = 1
            for n in shape:
                size *= n
            a = arena[:, at:at + size]
            if len(shape) == 2:
                a = a.rearrange("p (a b) -> p a b", b=shape[1])
            if len(shape) == 3:
                a = a.rearrange("p (a b c) -> p a b c", b=shape[1], c=shape[2])
            return a

        oh = area(0, GROUPS, NREL)
        rmask = area(1152, GROUPS, NREL)
        relb = area(2304, GROUPS, NREL)
        xtok = area(16384, TB, D)
        posi = area(12288, T).bitcast(I32)
        ang = area(12544, 2, T)
        turns = area(13056, 2, T)
        lat = sqT[:, 0:5, :]
        Q = area(0, HEADS, T)
        K = area(4096, HEADS, T)
        V = area(8192, TB, D)
        O = area(10240, TB, D)
        latsq = area(10240, 5, T)
        latn = area(12288, 5, T)
        prob = area(12288, 2, 3 * P)
        probT = area(13056, 2, 3 * P)
        rt = area(14336, 2, 2 * T)
        krot = area(15360, 2, T)
        Qd = area(0, 12, T)
        Kd = area(3072, 12, T)
        Vd = area(6144, TB, 3 * DQ)
        Od = area(9216, TB, DQ)
        n2T = area(10240, KT, T)
        pd = area(12288, 9 * P)
        pdT = area(13440, 2, 3 * P)
        relT = area(14208, 2, GROUPS, 2 * P)
        sg = area(16384, 2, T)
        hid = area(16896, 2, T)
        xg = area(0, KT * T)
        yT = area(2048, KT * T)
        yslot = area(4096, TB, D)
        ntok = area(6144, TB, D)
        moe = area(8192, KT, T)
        sel = area(10240, TB, T)
        selg = area(10752, TB, T)
        selgT = area(11264, TB, T)
        otok = area(0, TB, D)

        ident = con[:, C_ID:C_ID + P]
        perm = con[NOPE:QK, C_PERM:C_PERM + ROPE]
        causal = con[:, C_CAUSAL:C_CAUSAL + P]
        before = con[:, C_BEFORE:C_BEFORE + P]
        iota = con[:, C_IOTA:C_IOTA + T]
        freq = con[NOPE:QK, C_FREQ:C_FREQ + 1]

        names = """in_vec in_con in_x in_misc in_pos pool_const rel_stored rel_in vecT vec_sb c_ready xT x_act x_dve
            relmm rel_ready trig_step trig_done ada_step ada_reduced mod_ready
            sq stat std_ready dve_own norm_mul norm_ready scaled
            latmm lat_sb latsq_done latstat latstd latn_ready krmm k_rot k_bcast
            qmm q_sb ropemm rope_mul rope_done kmm k_sb vmm v_sb
            mscore masked expd mprobT mprobT_sb mpv o_norm oT oT_sb omm h_ready
            gumm silu_done hid_ready downmm
            kvmm kv_sb qdmm qd_sb dscore dmask dexp dprobT dprobT_sb dpv od_norm odT odT_sb odmm
            logit ntokT ntok_sb routed routed_gap gap_exp rankmm rank_sb count_sb
            selmade gathermm xg_sb selT selT_sb y_sb yslotT yslot_sb scatmm moe_sum
            finT fin_act fin_dve out_done""".split()
        s = {n: sem(n) for n in names}
        landed = [sem(f"landed{i}") for i in range(RING)]
        strip_in = [sem(f"strip_in{i}") for i in range(ADAS)]
        rel_in = [sem(f"rel_in{i}") for i in range(2)]

        freed = []
        freed += [(s["latmm"], 2 * i + 2) for i in range(3)]
        freed += [(s["qmm"], HEADS)] * QRT
        freed += [(s["vmm"], 4)] * KVT
        freed += [(s["omm"], 2 * i + 2) for i in range(4)]
        T_QUP, T_KVUP, T_OUT, T_FFN = 3, 6, 8, 12

        def tiles_through(c):
            return min(2 * c + 2, JT)
        for half in range(2):
            for ch in range(NCH):
                n = JT * half + tiles_through(ch)
                freed += [(s["gumm"], n), (s["gumm"], n), (s["downmm"], n)]
        T_KVB = len(freed)
        freed += [(s["kvmm"], 2 * i + 2) for i in range(12)]
        T_QB = len(freed)
        freed += [(s["qdmm"], 2 * i + 2) for i in range(6)]
        T_OB = len(freed)
        freed += [(s["odmm"], 4 * i + 4) for i in range(2)]
        T_MOE = len(freed)

        def tile_in(eng, t):
            eng.wait_ge(landed[t % RING], 16 * (t // RING + 1))

        def half_tile_in(eng, base, half, k):
            t = base + k
            eng.wait_ge(landed[t % RING], half * (16 * 3 * NCH // RING) + 16 * (t // RING + 1))

        def slot(t):
            return ring[:, t % RING, :]

        def cols(t, kt=KT, n=None):
            n = n or SLOT // kt
            return slot(t)[:, 0:kt * n].rearrange("p (k n) -> p k n", n=n)

        def by_width(eng, count, body):
            def choose(ws):
                if len(ws) == 1:
                    body(ws[0])
                    return
                with eng.If(count < ws[0] + 1):
                    body(ws[0])
                with eng.Else():
                    choose(ws[1:])
                    eng.nop()
            choose(WIDTHS)
            eng.nop()

        def tiles_in_bank(n):
            return {64: 8, 96: 4, 128: 4, 256: 2}[n]

        def sums(d, n):
            m = tiles_in_bank(n)
            at = 512 * (d // m) + n * (d % m)
            return wide[:, at:at + n]

        block = ctx.enter_context(nc.Block())

        @block.sync
        def _(sp):
            def rows(ap, r0, n):
                return ap[r0:r0 + n, :]

            vlist = [(V_C, c.rearrange("a (j p) -> (a j) p", p=P)), (V_MIX, g_mix.rearrange("a (j p) -> (a j) p", p=P)),
                     (V_FFN, g_ffn.rearrange("a (j p) -> (a j) p", p=P)),
                     (V_KV, g_kv_b.rearrange("(j p) -> j p", p=P)), (V_FINAL, g_final.rearrange("(j p) -> j p", p=P)),
                     (V_LQ, g_mla_q.rearrange("a (j p) -> (a j) p", p=P)),
                     (V_LKV, g_mla_kv.rearrange("a (j p) -> (a j) p", p=P))]
            for at, ap in vlist:
                sp.dma_start(vrows[at:at + ap.shape[0], :], ap).then_inc(s["in_vec"], 16)
            ba = b_ada.rearrange("l (j p) -> (l j) p", p=P)
            sp.dma_start(brows[0:48, :], ba[0:48, :]).then_inc(s["in_vec"], 16)
            sp.dma_start(brows[48:64, :], b_ada_kv.rearrange("(j p) -> j p", p=P)).then_inc(s["in_vec"], 16)
            sp.dma_start(brows[64:112, :], ba[48:96, :]).then_inc(s["in_vec"], 16)

            def load(t, dst, src):
                if t >= RING:
                    sp.wait_ge(*freed[t - RING])
                sp.dma_start(dst, src).then_inc(landed[t % RING], 16)

            strips = "(k p) n -> p k n"
            for i, (a, b) in enumerate(((0, 256), (256, 512), (512, 672))):
                load(i, cols(i, KT, b - a), w_mla_in[0][:, a:b].rearrange(strips, p=P))
            for k in range(QRT):
                load(T_QUP + k, slot(T_QUP + k)[:, 0:HEADS * QK], w_mla_q_up[0][k * P:(k + 1) * P, :])
            for k in range(KVT):
                load(T_KVUP + k, slot(T_KVUP + k), w_mla_kv_up[0][k * P:(k + 1) * P, :])
            for i in range(4):
                load(T_OUT + i, cols(T_OUT + i), w_mla_out[0][:, 256 * i:256 * (i + 1)].rearrange(strips, p=P))
            for half in range(2):
                for ch in range(NCH):
                    t = T_FFN + 3 * (NCH * half + ch)
                    f0, n = half * HALF + ch * 256, min(256, HALF - ch * 256)
                    load(t, cols(t, KT, n), w_ffn_gu[0][:, f0:f0 + n].rearrange(strips, p=P))
                    load(t + 1, cols(t + 1, KT, n), w_ffn_gu[0][:, FF + f0:FF + f0 + n].rearrange(strips, p=P))
                    load(t + 2, cols(t + 2, n // P, D), w_ffn_down[0][f0:f0 + n, :].rearrange(strips, p=P))
            for i in range(12):
                load(T_KVB + i, cols(T_KVB + i), w_kv_b[:, 256 * i:256 * (i + 1)].rearrange(strips, p=P))
            for i in range(6):
                load(T_QB + i, cols(T_QB + i), w_q_b[0][:, 256 * i:256 * (i + 1)].rearrange(strips, p=P))
            for i in range(2):
                load(T_OB + i, cols(T_OB + i, 4), w_o_b[0][:, 512 * i:512 * (i + 1)].rearrange(strips, p=P))

            gu_rows = w_exp_gu[0].rearrange("e d n -> (e d) n")
            down_rows = w_exp_down[0].rearrange("e f n -> (e f) n")
            for t in range(T_MOE - RING, T_MOE):
                sp.wait_ge(*freed[t])
            with sp.Fori(0, NE) as e:
                with sp.Fori(0, 2) as hf:
                    hh = e * 2 + hf
                    for ch in range(NCH):
                        t = T_MOE + 3 * ch
                        n = min(256, HALF - ch * 256)
                        used = JT * 2 + (tiles_through(ch - 3) if ch >= 3 else tiles_through(ch + 3) - JT)
                        col = hf * HALF + ch * 256
                        sp.wait_ge(s["gumm"], hh * JT + used)
                        for k, c0 in ((0, 0), (1, FF)):
                            src = gu_rows[bass.ds(e * D, D), bass.ds(col + c0, n)].rearrange(strips, p=P)
                            sp.dma_start(cols(t + k, KT, n), src).then_inc(landed[(t + k) % RING], 16)
                        sp.wait_ge(s["downmm"], hh * JT + used)
                        src = down_rows[bass.ds(e * FF + col, n), :].rearrange(strips, p=P)
                        sp.dma_start(cols(t + 2, n // P, D), src).then_inc(landed[(t + 2) % RING], 16)
            ov = out[0].rearrange("(b p) d -> p b d", p=P)
            for b in range(TB):
                sp.wait_ge(s["fin_act"], b + 1)
                sp.wait_ge(s["fin_dve"], b + 1)
                sp.dma_start(ov[:, b, :], otok[:, b, :]).then_inc(s["out_done"], 16)
            sp.wait_ge(s["out_done"], 16 * TB)

        @block.gpsimd
        def _(pool):
            nc.gpsimd.memset(ones[:, :], 1.0).then_inc(s["pool_const"], 1)
            nc.gpsimd.memset(eps[:, :], EPS).then_inc(s["pool_const"], 1)
            nc.gpsimd.memset(zeros[:, :], 0.0).then_inc(s["pool_const"], 1)
            nc.gpsimd.memset(small[:, :, :, :], 0.0).then_inc(s["pool_const"], 1)

            def blocks(first, w, col):
                for k in range(KT):
                    n = first * KT + k
                    if not (isinstance(n, int) and n < ADAS):
                        pool.wait_ge(s["ada_step"], n - ADAS + 1)
                    pool.dma_start(strip[:, k % ADAS, :], w[k * P:(k + 1) * P, col])\
                        .then_inc(strip_in[k % ADAS], 16)

            blocks(0, w_ada[0], slice(0, D))
            pool.wait_ge(s["rel_ready"], GROUPS)
            for g in range(GROUPS):
                pool.dma_start(scratch[:, g, :, :], relb[0:SLOTS, g:g + 1, :].broadcast_to([SLOTS, P, NREL]))\
                    .then_inc(s["rel_stored"], 16)
            with pool.Fori(1, 4) as b:
                blocks(b, w_ada[0], bass.ds(b * D, D))
            pool.wait_ge(s["k_rot"], 1)
            nc.gpsimd.tensor_copy(K[NOPE:QK, :, :], krot[NOPE:QK, 1:2, :].broadcast_to([ROPE, HEADS, T]))\
                .then_inc(s["k_bcast"], 1)
            with pool.Fori(4, 6) as b:
                blocks(b, w_ada[0], bass.ds(b * D, D))
            with pool.Fori(0, 2) as b:
                blocks(b + KV_SH, w_ada_kv, bass.ds(b * D, D))
            with pool.Fori(0, 6) as b:
                blocks(b + L1, w_ada[1], bass.ds(b * D, D))
            pool.wait_ge(s["rel_stored"], 16 * GROUPS)
            pool.wait_ge(s["mpv"], HEADS)
            pool.wait_ge(s["rope_done"], SLOTS)
            for h in range(SLOTS):
                if h >= 2:
                    pool.wait_ge(s["dmask"], 2 * (h - 1))
                src = bass.AP(scratch.tensor, h * GROUPS * P * NREL + P - 1,
                              [[NREL - 1, P], [P * NREL, GROUPS], [1, 2 * P]])
                pool.dma_start(relT[:, h % 2, :, :], src).then_inc(rel_in[h % 2], 16)
            pool.wait_ge(s["odT"], 4)
            nc.gpsimd.memset(moe[:, :, :], 0.0).then_inc(s["moe_sum"], 1)

        @block.tensor
        def _(pe):
            mm, tr = nc.tensor.matmul, nc.tensor.transpose

            def turn(o, a, first):
                return mm(o, a, ident, start=True, stop=True) if first else tr(o, a, ident)

            def product(o, pairs):
                n = len(pairs)
                for i, (w, r) in enumerate(pairs):
                    last = mm(o, w, r, start=(i == 0), stop=(i == n - 1))
                return last

            def ada_reduce(b, i=None, dyn=0):
                i = b if i is None else i
                pe.wait_ge(s["ada_step"], dyn * KT + KT * (b + 1))
                if b >= 1:
                    pe.wait_ge(s["mod_ready"], dyn + b)
                for j in range(KT):
                    last = mm(bank[3][:, KT * i + j:KT * i + j + 1], adasum[:, b % 2, j * P:(j + 1) * P],
                              ones[:, 0:1], start=True, stop=True)
                last.then_inc(s["ada_reduced"], 1)

            def norm_stat(k):
                for j in range(KT):
                    pe.wait_ge(s["sq"], KT * k + j + 1)
                    last = mm(bank[2][:, 0:T], ones[:, :], sqT[:, j, :], start=(j == 0), stop=(j == KT - 1))
                last.then_inc(s["stat"], 1)

            pe.wait_ge(s["in_vec"], 16 * 10)
            pe.wait_ge(s["in_con"], 16)
            tr(bank[0][:, 0:NVEC], vrows[:, :], ident[0:NVEC, 0:NVEC]).then_inc(s["vecT"], 1)
            nb = BLOCKS * KT
            tr(bank[1][:, 0:nb], brows[:, :], ident[0:nb, 0:nb]).then_inc(s["vecT"], 1)
            pe.wait_ge(s["in_x"], 16)
            for d in range(KT):
                if d >= 4:
                    pe.wait_ge(s["x_act"] if d % 2 == 0 else s["x_dve"], (d - 4) // 2 + 1)
                for b in range(TB):
                    last = tr(upper[d % 4][:, b * P:(b + 1) * P], xtok[:, b, d * P:(d + 1) * P], ident)
                last.then_inc(s["xT"], 1)
            pe.wait_ge(s["in_misc"], 16 * 4)
            pe.wait_ge(s["vec_sb"], 2)
            for g in range(GROUPS):
                mm(bank[g][0:SLOTS, 0:NREL], table[:, g * SLOTS:(g + 1) * SLOTS], oh[0:BUCKETS, g, :],
                   start=True, stop=True).then_inc(s["relmm"], 1)
            pe.wait_ge(s["rel_ready"], GROUPS)
            pe.wait_ge(s["pool_const"], 4)
            norm_stat(0)
            ada_reduce(0)
            ada_reduce(1)

            for i in range(6):
                if i % 2 == 0:
                    tile_in(pe, i // 2)
                if i >= 4:
                    pe.wait_ge(s["latsq_done"], i - 3)
                w = cols(i // 2, KT, 256 if i < 4 else 160)
                o = upper[i % 4][:, 0:T] if i < 5 else upper[1][NOPE:QK, 0:T]
                n = P if i < 5 else ROPE
                for k in range(KT):
                    if i == 0:
                        pe.wait_ge(s["norm_ready"], k + 1)
                    last = mm(o, w[:, k, (i % 2) * P:(i % 2) * P + n], nT[:, k, :], start=(k == 0), stop=(k == KT - 1))
                last.then_inc(s["latmm"], 1)
            pe.wait_ge(s["latsq_done"], 5)
            product(bank[2][:, 0:T], [(ones[:, :], latsq[:, i, :]) for i in range(QRT)]).then_inc(s["latstat"], 1)
            product(bank[1][:, 0:T], [(ones[:, :], latsq[:, QRT + i, :]) for i in range(KVT)])\
                .then_inc(s["latstat"], 1)
            pe.wait_ge(s["lat_sb"], 6)
            mm(bank[0][NOPE:QK, 0:T], perm, krot[NOPE:QK, 0, :], start=True, stop=True).then_inc(s["krmm"], 1)

            for k in range(QRT):
                tile_in(pe, T_QUP + k)
            for h in range(HEADS):
                if h >= 4:
                    pe.wait_ge(s["q_sb"], h - 3)
                if h == 0:
                    pe.wait_ge(s["latn_ready"], QRT)
                product(upper[h % 4][0:QK, 0:T], [(slot(T_QUP + k)[:, h * QK:(h + 1) * QK], latn[:, k, :])
                                                  for k in range(QRT)]).then_inc(s["qmm"], 1)
            pe.wait_ge(s["latn_ready"], 5)
            pe.wait_ge(s["k_rot"], 1)
            for k in range(KVT):
                tile_in(pe, T_KVUP + k)
            for p in range(HEADS // 2):
                if p >= 2:
                    pe.wait_ge(s["rope_mul"], p - 1)
                pe.wait_ge(s["q_sb"], min(2 * p + 6, HEADS))
                mm(bank[p % 2][NOPE:QK, 0:2 * T], perm, Q[NOPE:QK, 2 * p:2 * p + 2, :],
                   start=True, stop=True).then_inc(s["ropemm"], 1)
                for h in (2 * p, 2 * p + 1):
                    if h >= 4:
                        pe.wait_ge(s["k_sb"], h - 3)
                    if h == 0:
                        pe.wait_ge(s["q_sb"], HEADS)
                    product(upper[h % 4][0:NOPE, 0:T], [(slot(T_KVUP + k)[:, h * P:h * P + NOPE], latn[:, QRT + k, :])
                                                        for k in range(KVT)]).then_inc(s["kmm"], 1)
            for i in range(4):
                b, half = i // 2, i % 2
                pe.wait_ge(s["k_sb"], HEADS - 3 + i)
                product(upper[i], [(latn[:, QRT + k, b * P:(b + 1) * P],
                                    slot(T_KVUP + k).rearrange("p (h c) -> p h c", c=P)[:, half * 8:half * 8 + 8, NOPE:P])
                                   for k in range(KVT)]).then_inc(s["vmm"], 1)
            ada_reduce(2)
            ada_reduce(3)

            pe.wait_ge(s["rope_done"], HEADS // 2)
            pe.wait_ge(s["k_bcast"], 1)
            pe.wait_ge(s["v_sb"], 4)
            pe.wait_ge(s["mod_ready"], 4)
            for i in range(HEADS + 2):
                if i < HEADS:
                    h = i
                    if h >= 2:
                        pe.wait_ge(s["masked"], 2 * (h - 1))
                    mm(bank[h % 2][:, 0:P], Q[0:QK, h, 0:P], K[0:QK, h, 0:P], start=True, stop=True)
                    mm(bank[h % 2][:, P:3 * P], Q[0:QK, h, P:T], K[0:QK, h, :], start=True, stop=True)\
                        .then_inc(s["mscore"], 1)
                if 1 <= i <= HEADS:
                    h = i - 1
                    pe.wait_ge(s["expd"], 2 * (h + 1))
                    if h >= 2:
                        pe.wait_ge(s["mprobT_sb"], h - 1)
                    for j in range(3):
                        last = tr(bank[2 + h % 2][:, j * P:(j + 1) * P], prob[:, h % 2, j * P:(j + 1) * P], ident)
                    last.then_inc(s["mprobT"], 1)
                if i >= 2:
                    h = i - 2
                    pe.wait_ge(s["mprobT_sb"], h + 1)
                    o = upper[2 * (h // 8)][:, (h % 8) * VD:(h % 8 + 1) * VD]
                    mm(o, probT[:, h % 2, 0:P], V[:, 0, h * VD:(h + 1) * VD], start=True, stop=True)
                    o = upper[2 * (h // 8) + 1][:, (h % 8) * VD:(h % 8 + 1) * VD]
                    product(o, [(probT[:, h % 2, (b + 1) * P:(b + 2) * P], V[:, b, h * VD:(h + 1) * VD])
                                for b in range(TB)]).then_inc(s["mpv"], 1)
            for d in range(KT):
                pe.wait_ge(s["o_norm"], 2 * (d // 4 + 1))
                if d >= 2:
                    pe.wait_ge(s["oT_sb"], d - 1)
                for b in range(TB):
                    last = tr(bank[d % 2][:, b * P:(b + 1) * P], O[:, b, d * P:(d + 1) * P], ident)
                last.then_inc(s["oT"], 1)
            pe.wait_ge(s["oT_sb"], KT)
            for d in range(KT):
                if d % 2 == 0:
                    tile_in(pe, T_OUT + d // 2)
                if d >= 4:
                    pe.wait_ge(s["h_ready"], d - 3)
                product(upper[d % 4][:, 0:T], [(cols(T_OUT + d // 2)[:, k, (d % 2) * P:(d % 2 + 1) * P], nT[:, k, :])
                                               for k in range(KT)]).then_inc(s["omm"], 1)
            norm_stat(1)
            ada_reduce(4)
            ada_reduce(5)

            def open_sums(n):
                for i in range(KT // tiles_in_bank(n)):
                    mm(upper[i], zeros[:, 0:P], zeros[:, :], start=True, stop=False, skip_group_check=True)

            def ffn_half(base, half, n, src, before=0, extra=None):
                job0 = half * JT

                def down(j):
                    k = 3 * (j // 2) + 2
                    if j % 2 == 0:
                        half_tile_in(pe, base, half, k)
                    pe.wait_ge(s["hid_ready"], before + job0 + j + 1)
                    w = cols(base + k, 2 if j < JT - 1 else 1, D)
                    for d in range(KT):
                        last = mm(sums(d, n), w[:, j % 2, d * P:(d + 1) * P],
                                  hid[:, j % 2, 0:n], start=False, stop=False, skip_group_check=True)
                    last.then_inc(s["downmm"], 1)

                for j in range(JT):
                    k = 3 * (j // 2)
                    if j % 2 == 0:
                        half_tile_in(pe, base, half, k)
                        half_tile_in(pe, base, half, k + 1)
                    if j >= 2:
                        pe.wait_ge(s["hid_ready"], before + job0 + j - 1)
                    m = 256 if j < JT - 1 else P
                    for i in range(2):
                        w = cols(base + k + i, KT, m)
                        for kt in range(KT):
                            last = mm(bank[j % 2][:, i * T:i * T + n], w[:, kt, (j % 2) * P:(j % 2 + 1) * P],
                                      src(kt), start=(kt == 0), stop=(kt == KT - 1))
                    last.then_inc(s["gumm"], 1)
                    if j >= 1:
                        down(j - 1)
                    if extra:
                        extra(j)
                down(JT - 1)

            pe.wait_ge(s["h_ready"], KT)
            pe.wait_ge(s["oT_sb"], KT)
            open_sums(T)
            pe.wait_ge(s["norm_ready"], 2 * KT)
            with pe.Fori(0, 2) as half:
                def extra(j):
                    if j in (4, 7, 9):
                        i = (4, 7, 9).index(j)
                        ada_reduce(6 + i, i, half * 4)
                ffn_half(T_FFN, half, T, lambda kt: nT[:, kt, :], 0, extra)
                ada_reduce(9, 3, half * 4)

            norm_stat(2)
            for i in range(24):
                t = T_KVB + i // 2
                if i % 2 == 0:
                    tile_in(pe, t)
                if i == 0:
                    pe.wait_ge(s["norm_ready"], 3 * KT)
                    pe.wait_ge(s["h_ready"], 2 * KT)
                if i >= 4:
                    pe.wait_ge(s["kv_sb"], i - 3)
                if (i // 2) % 4 < 2:
                    pairs = [(cols(t)[:, k, (i % 2) * P:(i % 2 + 1) * P], nT[:, k, :]) for k in range(KT)]
                else:
                    pairs = [(nT[:, k, (i % 2) * P:(i % 2 + 1) * P], cols(t)[:, k, :]) for k in range(KT)]
                product(upper[i % 4][:, 0:T], pairs).then_inc(s["kvmm"], 1)
            pe.wait_ge(s["norm_ready"], 4 * KT)
            for i in range(12):
                t = T_QB + i // 2
                if i % 2 == 0:
                    tile_in(pe, t)
                if i < 4:
                    pe.wait_ge(s["kv_sb"], 21 + i)
                else:
                    pe.wait_ge(s["qd_sb"], i - 3)
                product(upper[i % 4][:, 0:T], [(cols(t)[:, k, (i % 2) * P:(i % 2 + 1) * P], n2T[:, k, :])
                                               for k in range(KT)]).then_inc(s["qdmm"], 1)

            pe.wait_ge(s["qd_sb"], 12)

            def dscores(u):
                h, b = divmod(u, 2)
                if u >= 2:
                    pe.wait_ge(s["dmask"], u - 1)
                p0 = (h % 2) * HD
                for g in range(GROUPS):
                    t = 4 * g + h // 2
                    n = (b + 1) * P
                    o = bank[0][:, g * P:(g + 1) * P] if b == 0 else bank[1 + g // 2][:, (g % 2) * T:(g % 2) * T + T]
                    last = mm(o, Qd[p0:p0 + HD, t, b * P:(b + 1) * P], Kd[p0:p0 + HD, t, 0:n], start=True, stop=True)
                last.then_inc(s["dscore"], 1)

            def dtranspose(q):
                h, r = divmod(q, 3)
                pe.wait_ge(s["dexp"], 2 * h + (1 if r == 0 else 2))
                if q >= 2:
                    pe.wait_ge(s["dprobT_sb"], q - 1)
                o = bank[3] if q % 2 == 0 else upper[0]
                for j in range(3):
                    last = tr(o[:, j * P:(j + 1) * P], pd[:, (3 * r + j) * P:(3 * r + j + 1) * P], ident)
                last.then_inc(s["dprobT"], 1)

            def dvalues(q):
                h, r = divmod(q, 3)
                pe.wait_ge(s["dprobT_sb"], q + 1)
                o = upper[1 if r == 0 else 2][:, h * HD:(h + 1) * HD]
                for j in range(3):
                    g, kb = (j, 0) if r == 0 else divmod(3 * (r - 1) + j, 2)
                    first = j == 0 and r < 2
                    last = mm(o, pdT[:, q % 2, j * P:(j + 1) * P], Vd[:, kb, g * DQ + h * HD:g * DQ + (h + 1) * HD],
                              start=first, stop=(j == 2 and r != 1))
                last.then_inc(s["dpv"], 1)

            dscores(0)
            dscores(1)
            for h in range(SLOTS):
                for r in range(3):
                    q = 3 * h + r
                    dtranspose(q)
                    if q >= 1:
                        dvalues(q - 1)
                    if h + 1 < SLOTS and r in (0, 1):
                        dscores(2 * h + 2 + r)
            dvalues(3 * SLOTS - 1)
            for d in range(4):
                pe.wait_ge(s["od_norm"], TB)
                if d >= 2:
                    pe.wait_ge(s["odT_sb"], d - 1)
                for b in range(TB):
                    last = tr(bank[d % 2][:, b * P:(b + 1) * P], Od[:, b, d * P:(d + 1) * P], ident)
                last.then_inc(s["odT"], 1)
            pe.wait_ge(s["odT_sb"], 4)
            for d in range(KT):
                if d % 4 == 0:
                    tile_in(pe, T_OB + d // 4)
                if d >= 4:
                    pe.wait_ge(s["h_ready"], 2 * KT + d - 3)
                product(upper[d % 4][:, 0:T], [(cols(T_OB + d // 4, 4)[:, k, (d % 4) * P:(d % 4 + 1) * P], nT[:, k, :])
                                               for k in range(4)]).then_inc(s["odmm"], 1)
            norm_stat(3)

            pe.wait_ge(s["norm_ready"], 5 * KT)
            for b in range(TB):
                last = product(bank[3][:, b * NE:(b + 1) * NE],
                               [(nT[:, k, b * P:(b + 1) * P], wrout[:, k, :]) for k in range(KT)])
            last.then_inc(s["logit"], 1)
            for i in range(4):
                b, half = i // 2, i % 2
                for j in range(4):
                    d = 4 * half + j
                    last = tr(upper[i][:, j * P:(j + 1) * P], nT[:, d, b * P:(b + 1) * P], ident)
                last.then_inc(s["ntokT"], 1)
            pe.wait_ge(s["routed"], 1)
            chosen = small[:, 0, :, 0:NE]
            mm(bank[2][:, 0:NE], before, chosen[:, 0, :], start=True, stop=True)
            product(bank[2][:, NE:2 * NE], [(ones[:, :], chosen[:, 0, :]), (before, chosen[:, 1, :])])
            product(bank[2][:, 2 * NE:3 * NE], [(ones[:, :], chosen[:, 0, :]), (ones[:, :], chosen[:, 1, :])])\
                .then_inc(s["rankmm"], 1)
            pe.wait_ge(s["count_sb"], 1)
            pe.wait_ge(s["ntok_sb"], 4)

            def expert(e, n):
                nb, w = max(1, n // P), min(n, P)
                pe.wait_ge(s["selmade"], e + 1)
                for d in range(KT):
                    last = product(sums(d, n), [(ntok[:, b, d * P:(d + 1) * P], sel[:, b, 0:n]) for b in range(TB)])
                last.then_inc(s["gathermm"], 1)
                pe.wait_ge(s["moe_sum"], e + 1)
                for k in range(nb):
                    for b in range(TB):
                        last = turn(bank[3][0:w, k * T + b * P:k * T + (b + 1) * P], selg[:, b, k * P:k * P + w],
                                    k + b == 0)
                last.then_inc(s["selT"], 1)
                pe.wait_ge(s["xg_sb"], e + 1)
                open_sums(n)
                with pe.Fori(0, 2) as hf:
                    ffn_half(T_MOE, e * 2 + hf, n, lambda kt: xg[:, kt * n:(kt + 1) * n], 2 * JT)
                pe.wait_ge(s["y_sb"], e + 1)
                for k in range(nb):
                    for d in range(KT):
                        last = turn(wide[0:w, k * D + d * P:k * D + (d + 1) * P],
                                    yT[:, d * n + k * P:d * n + k * P + w], k + d == 0)
                last.then_inc(s["yslotT"], 1)
                pe.wait_ge(s["yslot_sb"], e + 1)
                pe.wait_ge(s["selT_sb"], e + 1)
                for d in range(KT):
                    last = product(bank[d // 2][:, (d % 2) * T:(d % 2 + 1) * T],
                                   [(yslot[0:w, k, d * P:(d + 1) * P], selgT[0:w, k, :]) for k in range(nb)])
                last.then_inc(s["scatmm"], 1)

            with pe.Fori(0, NE) as e:
                count = pe.value_load(counts[0:1, bass.ds(e, 1)], min_val=0, max_val=T)
                by_width(pe, count, lambda n: expert(e, n))

            norm_stat(4)
            pe.wait_ge(s["scaled"], KT)
            for i in range(4):
                b, half = i // 2, i % 2
                for j in range(4):
                    last = tr(upper[i][:, j * P:(j + 1) * P], nT[:, 4 * half + j, b * P:(b + 1) * P], ident)
                last.then_inc(s["finT"], 1)

        @block.scalar
        def _(act):
            go = nc.scalar.activation
            act.dma_start(con[:, :], consts).then_inc(s["in_con"], 16)
            act.dma_start(xtok, x[0].rearrange("(b p) d -> p b d", p=P)).then_inc(s["in_x"], 16)
            act.dma_start(oh[0:BUCKETS, :, :], onehot.rearrange("b (g m) -> b g m", g=GROUPS)).then_inc(s["in_misc"], 16)
            act.dma_start(rmask[0:SLOTS, :, :], relmask.rearrange("b (g m) -> b g m", g=GROUPS)).then_inc(s["in_misc"], 16)
            act.dma_start(table[:, :], rpb_table).then_inc(s["in_misc"], 16)
            act.dma_start(wrout[:, :, :], w_router[0].rearrange("(k p) e -> p k e", p=P)).then_inc(s["in_misc"], 16)
            pos_all = bass.AP(positions.tensor, 0, [[0, ROPE], [1, T]])
            act.dma_start(posi[NOPE:QK, :], pos_all).then_inc(s["in_pos"], 16)

            act.wait_ge(s["vec_sb"], 1)
            go(cact[:, :], vec[:, V_C:V_C + KT], ACT.Silu).then_inc(s["c_ready"], 1)
            for d in range(0, KT, 2):
                act.wait_ge(s["xT"], d + 1)
                go(hT[:, d, :], upper[d % 4][:, 0:T], ACT.Copy).then_inc(s["x_act"], 1)

            act.wait_ge(s["trig_step"], 1)
            go(trig[NOPE:QK, :, :], ang[NOPE:QK, :, :], ACT.Sin).then_inc(s["trig_done"], 1)

            def squares(k, ready):
                for j in range(KT):
                    ready(j)
                    go(sqT[:, j, :], hT[:, j, :], ACT.Square).then_inc(s["sq"], 1)
                act.wait_ge(s["stat"], k + 1)
                go(std[:, 0, :], bank[2][:, 0:T], ACT.Sqrt, bias=eps[:, 0:1], scale=1.0 / D)\
                    .then_inc(s["std_ready"], 1)

            def shifts(m, b, dst):
                act.wait_ge(s["mod_ready"], b + 1)
                for j in range(KT):
                    act.wait_ge(s["norm_mul"], m * KT + j + 1)
                    go(dst[:, j, :], dst[:, j, :], ACT.Identity, bias=mod[:, b * KT + j:b * KT + j + 1])\
                        .then_inc(s["norm_ready"], 1)

            act.wait_ge(s["pool_const"], 4)

            def x_ready(j):
                act.wait_ge(*((s["x_act"], j // 2 + 1) if j % 2 == 0 else (s["x_dve"], j // 2 + 1)))
            squares(0, x_ready)
            shifts(0, SH_M, nT)

            act.wait_ge(s["stat"], 1)
            for i in range(6):
                act.wait_ge(s["latmm"], i + 1)
                if i < 5:
                    go(lat[:, i, :], upper[i % 4][:, 0:T], ACT.Copy).then_inc(s["lat_sb"], 1)
                    go(latsq[:, i, :], upper[i % 4][:, 0:T], ACT.Square).then_inc(s["latsq_done"], 1)
                else:
                    go(krot[NOPE:QK, 0, :], upper[1][NOPE:QK, 0:T], ACT.Copy).then_inc(s["lat_sb"], 1)
            act.wait_ge(s["latstat"], 1)
            go(std[:, 0, :], bank[2][:, 0:T], ACT.Sqrt, bias=eps[:, 0:1], scale=1.0 / QR).then_inc(s["latstd"], 1)
            act.wait_ge(s["latstat"], 2)
            go(std[:, 1, :], bank[1][:, 0:T], ACT.Sqrt, bias=eps[:, 0:1], scale=1.0 / KVR).then_inc(s["latstd"], 1)
            act.wait_ge(s["rel_stored"], 16 * GROUPS)
            for h in range(HEADS):
                act.wait_ge(s["qmm"], h + 1)
                go(Q[0:QK, h, :], upper[h % 4][0:QK, 0:T], ACT.Copy).then_inc(s["q_sb"], 1)
            for h in range(HEADS):
                act.wait_ge(s["kmm"], h + 1)
                go(K[0:NOPE, h, :], upper[h % 4][0:NOPE, 0:T], ACT.Copy).then_inc(s["k_sb"], 1)
            for i in range(4):
                act.wait_ge(s["vmm"], i + 1)
                go(V[:, i // 2, (i % 2) * 512:(i % 2 + 1) * 512], upper[i], ACT.Copy).then_inc(s["v_sb"], 1)
            for h in range(HEADS):
                for b in range(TB):
                    act.wait_ge(s["masked"], 2 * h + b + 1)
                    pr = prob[:, h % 2, 0:P] if b == 0 else prob[:, h % 2, P:3 * P]
                    go(pr, pr, ACT.Exp, bias=nmax[:, b, h:h + 1], scale=-1.0,
                       accum_out=rsum[:, b, h:h + 1]).then_inc(s["expd"], 1)
            for d in range(KT):
                act.wait_ge(s["oT"], d + 1)
                go(nT[:, d, :], bank[d % 2][:, 0:T], ACT.Copy).then_inc(s["oT_sb"], 1)

            def h_ready(base):
                return lambda j: act.wait_ge(s["h_ready"], base + j + 1)
            squares(1, h_ready(0))
            shifts(1, SH_F, nT)

            def gates(j, n, job):
                act.wait_ge(s["gumm"], job + j + 1)
                if isinstance(job, int) and job + j < 2:
                    pass
                else:
                    act.wait_ge(s["hid_ready"], job + j - 1)
                go(sg[:, j % 2, 0:n], bank[j % 2][:, 0:n], ACT.Silu).then_inc(s["silu_done"], 1)

            for half in range(2):
                for j in range(JT):
                    gates(j, T, half * JT)
            squares(2, h_ready(KT))
            shifts(2, KV_SH, nT)
            shifts(3, L1 + SH_M, n2T)
            for i in range(24):
                act.wait_ge(s["kvmm"], i + 1)
                m, r = divmod(i, 2)
                g, q = divmod(m, 4)
                dst = Kd[:, 4 * g + 2 * q + r, :] if q < 2 else Vd[:, r, g * DQ + (q - 2) * T:g * DQ + (q - 1) * T]
                go(dst, upper[i % 4][:, 0:T], ACT.Copy).then_inc(s["kv_sb"], 1)
            for i in range(12):
                act.wait_ge(s["qdmm"], i + 1)
                go(Qd[:, i, :], upper[i % 4][:, 0:T], ACT.Copy).then_inc(s["qd_sb"], 1)
            for u in range(2 * SLOTS):
                h, b = divmod(u, 2)
                act.wait_ge(s["dmask"], u + 1)
                pr = pd[:, 0:3 * P] if b == 0 else pd[:, 3 * P:9 * P]
                go(pr, pr, ACT.Exp, bias=nmax[:, b, h:h + 1], scale=-1.0,
                   accum_out=rsum[:, b, h:h + 1]).then_inc(s["dexp"], 1)
            for d in range(4):
                act.wait_ge(s["odT"], d + 1)
                go(nT[:, d, :], bank[d % 2][:, 0:T], ACT.Copy).then_inc(s["odT_sb"], 1)
            squares(3, h_ready(2 * KT))
            shifts(4, L1 + SH_F, nT)
            act.wait_ge(s["logit"], 1)
            act.wait_ge(s["dexp"], 2 * SLOTS)
            for i in range(4):
                act.wait_ge(s["ntokT"], i + 1)
                go(ntok[:, i // 2, (i % 2) * 512:(i % 2 + 1) * 512], upper[i], ACT.Copy).then_inc(s["ntok_sb"], 1)
            act.wait_ge(s["routed_gap"], 1)
            go(small[:, 8, :, 0:1], small[:, 8, :, 1:2], ACT.Exp).then_inc(s["gap_exp"], 1)
            act.wait_ge(s["count_sb"], 1)

            def copy_sums(dst, n):
                m = tiles_in_bank(n) * n
                return go(dst[:, 0:KT * n].rearrange("p (b c) -> p b c", c=m),
                          wide[:, :].rearrange("p (b c) -> p b c", c=512)[:, 0:KT * n // m, 0:m], ACT.Copy)

            def expert(e, n):
                nb, w = max(1, n // P), min(n, P)
                act.wait_ge(s["gathermm"], e + 1)
                copy_sums(xg, n).then_inc(s["xg_sb"], 1)
                act.wait_ge(s["selT"], e + 1)
                go(selgT[0:w, 0:nb, :], bank[3][0:w, 0:nb * T].rearrange("p (k t) -> p k t", t=T), ACT.Copy)\
                    .then_inc(s["selT_sb"], 1)
                with act.Fori(0, 2) as hf:
                    for j in range(JT):
                        gates(j, n, 2 * JT + (e * 2 + hf) * JT)
                act.wait_ge(s["downmm"], 2 * JT + (e + 1) * (2 * JT))
                copy_sums(yT, n).then_inc(s["y_sb"], 1)
                act.wait_ge(s["yslotT"], e + 1)
                go(yslot[0:w, 0:nb, :], wide[0:w, 0:nb * D].rearrange("p (k d) -> p k d", d=D), ACT.Copy)\
                    .then_inc(s["yslot_sb"], 1)

            with act.Fori(0, NE) as e:
                count = act.value_load(counts[0:1, bass.ds(e, 1)], min_val=0, max_val=T)
                by_width(act, count, lambda n: expert(e, n))
            squares(4, h_ready(3 * KT))
            for i in range(0, 4, 2):
                act.wait_ge(s["finT"], i + 1)
                go(otok[:, i // 2, 0:512], upper[i], ACT.Copy).then_inc(s["fin_act"], 1)

        @block.vector
        def _(dve):
            v = nc.vector
            own = [0]

            def link(ins):
                own[0] += 1
                ins.then_inc(s["dve_own"], 1)
                dve.wait_ge(s["dve_own"], own[0])

            def ada_strip(b, k, dyn=0):
                n = KT * b + k
                m = n % ADAS
                turn = n // ADAS + 1
                dve.wait_ge(strip_in[m], dyn * (16 * KT // ADAS) + 16 * turn)
                if k == 0:
                    if b >= 2:
                        dve.wait_ge(s["ada_reduced"], dyn + b - 1)
                    v.tensor_scalar(adasum[:, b % 2, :], strip[:, m, :], cact[:, 0:1], None, ALU.mult)\
                        .then_inc(s["ada_step"], 1)
                else:
                    dve.wait_ge(s["ada_step"], dyn * KT + n)
                    v.scalar_tensor_tensor(out=adasum[:, b % 2, :], in0=strip[:, m, :], scalar=cact[:, k:k + 1],
                                           in1=adasum[:, b % 2, :], op0=ALU.mult, op1=ALU.add)\
                        .then_inc(s["ada_step"], 1)

            def ada(b):
                for k in range(KT):
                    ada_strip(b, k)

            def mod_out(b):
                dve.wait_ge(s["ada_reduced"], b + 1)
                v.tensor_tensor(mod[:, b * KT:(b + 1) * KT], bank[3][:, b * KT:(b + 1) * KT],
                                bcol[:, b * KT:(b + 1) * KT], ALU.add).then_inc(s["mod_ready"], 1)

            def scale_of(m, b, g):
                dve.wait_ge(s["mod_ready"], b + 1)
                link(v.scalar_tensor_tensor(out=ascale[:, m, :], in0=mod[:, b * KT:(b + 1) * KT], scalar=1.0,
                                            in1=vec[:, g:g + KT], op0=ALU.add, op1=ALU.mult))

            def norm(m, dst):
                for j in range(KT):
                    v.scalar_tensor_tensor(out=dst[:, j, :], in0=hT[:, j, :], scalar=ascale[:, m, j:j + 1],
                                           in1=rstd[:, 0, :], op0=ALU.mult, op1=ALU.mult)\
                        .then_inc(s["norm_mul"], 1)

            def inverse(k):
                dve.wait_ge(s["std_ready"], k + 1)
                link(v.reciprocal(rstd[:, 0, :], std[:, 0, :]))

            def residual(j, src, b):
                v.scalar_tensor_tensor(out=hT[:, j, :], in0=src, scalar=mod[:, b * KT + j:b * KT + j + 1],
                                       in1=hT[:, j, :], op0=ALU.mult, op1=ALU.add).then_inc(s["h_ready"], 1)

            dve.wait_ge(s["vecT"], 1)
            v.tensor_copy(vec[:, :], bank[0][:, 0:NVEC]).then_inc(s["vec_sb"], 1)
            dve.wait_ge(s["vecT"], 2)
            v.tensor_copy(bcol[:, :], bank[1][:, 0:BLOCKS * KT]).then_inc(s["vec_sb"], 1)
            for d in range(1, KT, 2):
                dve.wait_ge(s["xT"], d + 1)
                v.tensor_copy(hT[:, d, :], upper[d % 4][:, 0:T]).then_inc(s["x_dve"], 1)
            dve.wait_ge(s["in_misc"], 64)
            for g in range(GROUPS):
                dve.wait_ge(s["relmm"], g + 1)
                v.scalar_tensor_tensor(out=relb[0:SLOTS, g, :], in0=bank[g][0:SLOTS, 0:NREL], scalar=HD ** 0.5,
                                       in1=rmask[0:SLOTS, g, :], op0=ALU.mult, op1=ALU.add)\
                    .then_inc(s["rel_ready"], 1)
            R = slice(NOPE, QK)
            dve.wait_ge(s["in_pos"], 16)
            dve.wait_ge(s["in_con"], 16)
            link(v.tensor_copy(ang[R, 1, :], posi[R, :]))
            link(v.tensor_scalar(ang[R, 0, :], ang[R, 1, :], freq, None, ALU.mult))
            link(v.tensor_scalar(turns[R, 0, :], ang[R, 0, :], 0.15915494309189535, 0.25, ALU.mult, ALU.add))
            link(v.tensor_scalar(turns[R, 1, :], ang[R, 0, :], 0.15915494309189535, None, ALU.mult))
            link(v.tensor_copy(ang[R, 1, :], ang[R, 0, :]))
            link(v.tensor_scalar(turns[R, :, :], turns[R, :, :], ROUND, None, ALU.add))
            link(v.tensor_scalar(turns[R, :, :], turns[R, :, :], ROUND, None, ALU.subtract))
            two_pi_lo = 6.283185307179586 - TWO_PI_HI - TWO_PI_MID
            for part in (TWO_PI_HI, TWO_PI_MID, two_pi_lo):
                link(v.scalar_tensor_tensor(out=ang[R, :, :], in0=turns[R, :, :], scalar=-part, in1=ang[R, :, :],
                                            op0=ALU.mult, op1=ALU.add))
            link(v.tensor_scalar(ang[R, 0, :], ang[R, 0, :], 1.5707963267948966, None, ALU.add))
            v.tensor_scalar(ang[R, :, :], ang[R, :, :], 3.1415925, -3.1415925, ALU.min, ALU.max)\
                .then_inc(s["trig_step"], 1)

            dve.wait_ge(s["c_ready"], 1)
            ada(0)
            ada(1)
            mod_out(0)
            mod_out(1)
            scale_of(0, SC_M, V_MIX)
            inverse(0)
            norm(0, nT)

            for i, (a, n, g) in enumerate(((0, QRT, V_LQ), (QRT, KVT, V_LKV))):
                dve.wait_ge(s["latstd"], i + 1)
                dve.wait_ge(s["lat_sb"], 5)
                link(v.reciprocal(rstd[:, i, :], std[:, i, :]))
                if i == 0:
                    dve.wait_ge(s["trig_done"], 1)
                for j in range(n):
                    v.scalar_tensor_tensor(out=latn[:, a + j, :], in0=lat[:, a + j, :], scalar=vec[:, g + j:g + j + 1],
                                           in1=rstd[:, i, :], op0=ALU.mult, op1=ALU.mult)\
                        .then_inc(s["latn_ready"], 1)
            cos, sin = trig[R, 0:1, :], trig[R, 1:2, :]
            dve.wait_ge(s["krmm"], 1)
            dve.wait_ge(s["lat_sb"], 6)
            link(v.tensor_tensor(rt[R, 0, 0:T], bank[0][R, 0:T], trig[R, 1, :], ALU.mult))
            link(v.tensor_tensor(rt[R, 1, 0:T], krot[R, 0, :], trig[R, 0, :], ALU.mult))
            v.tensor_tensor(krot[R, 1, :], rt[R, 0, 0:T], rt[R, 1, 0:T], ALU.add).then_inc(s["k_rot"], 1)
            ada(2)
            ada(3)
            dve.wait_ge(s["k_rot"], 1)
            for p in range(HEADS // 2):
                two = [ROPE, 2, T]
                dve.wait_ge(s["ropemm"], p + 1)
                q2 = Q[R, 2 * p:2 * p + 2, :]
                r0 = rt[R, 0, :].rearrange("p (a t) -> p a t", t=T)
                r1 = rt[R, 1, :].rearrange("p (a t) -> p a t", t=T)
                if p:
                    dve.wait_ge(s["rope_done"], p)
                v.tensor_tensor(r0, bank[p % 2][R, :].rearrange("p (a t) -> p a t", t=T), sin.broadcast_to(two),
                                ALU.mult).then_inc(s["rope_mul"], 1)
                dve.wait_ge(s["rope_mul"], p + 1)
                link(v.tensor_tensor(r1, q2, cos.broadcast_to(two), ALU.mult))
                v.tensor_tensor(q2, r0, r1, ALU.add).then_inc(s["rope_done"], 1)
            mod_out(2)
            mod_out(3)

            scale = QK ** -0.5
            dve.wait_ge(s["v_sb"], 4)

            def divide(parts, heads, o, sums, rn):
                for b, src in enumerate(parts):
                    v.tensor_tensor(o[:, b, :].rearrange("p (h c) -> p h c", c=HD),
                                    src.rearrange("p (h c) -> p h c", c=HD),
                                    rn[:, b, heads].unsqueeze(2).broadcast_to([P, 8, HD]), ALU.mult).then_inc(sums, 1)

            for h in range(HEADS + 1):
                if h < HEADS:
                    dve.wait_ge(s["mscore"], h + 1)
                    if h >= 2:
                        dve.wait_ge(s["mprobT"], h - 1)
                    k = bank[h % 2]
                    pr = prob[:, h % 2, :]
                    v.tensor_tensor_reduce(out=pr[:, 0:P], in0=k[:, 0:P], in1=causal, scale=-scale, scalar=HUGE,
                                           op0=ALU.add, op1=ALU.min, accum_out=nmax[:, 0, h:h + 1])\
                        .then_inc(s["masked"], 1)
                    v.tensor_tensor_reduce(out=pr[:, P:3 * P], in0=k[:, P:3 * P], in1=con[:, C_OPEN:C_OPEN + 2 * P],
                                           scale=-scale, scalar=HUGE, op0=ALU.add, op1=ALU.min,
                                           accum_out=nmax[:, 1, h:h + 1]).then_inc(s["masked"], 1)
                if h >= 1:
                    g = h - 1
                    dve.wait_ge(s["mprobT"], g + 1)
                    if g >= 2:
                        dve.wait_ge(s["mpv"], g - 1)
                    v.tensor_copy(probT[:, g % 2, :], bank[2 + g % 2][:, 0:3 * P]).then_inc(s["mprobT_sb"], 1)
                if h in (9, HEADS):
                    a = 0 if h == 9 else 8
                    if h == HEADS:
                        dve.wait_ge(s["mpv"], HEADS)
                    dve.wait_ge(s["mpv"], a + 8 if h == HEADS else 8)
                    dve.wait_ge(s["expd"], 2 * (a + 8))
                    link(v.reciprocal(rinv[:, :, a:a + 8], rsum[:, :, a:a + 8]))
                    divide([upper[2 * (a // 8)], upper[2 * (a // 8) + 1]], slice(a, a + 8),
                           O[:, :, a * VD:(a + 8) * VD], s["o_norm"], rinv)
            for d in range(KT):
                dve.wait_ge(s["omm"], d + 1)
                residual(d, upper[d % 4][:, 0:T], GT_M)
                ada_strip(4 + d // 4, 2 * (d % 4))
                ada_strip(4 + d // 4, 2 * (d % 4) + 1)
            mod_out(4)
            mod_out(5)
            scale_of(1, SC_F, V_FFN)
            inverse(1)
            norm(1, nT)

            def gated(j, n, job):
                dve.wait_ge(s["silu_done"], job + j + 1)
                if not (isinstance(job, int) and job + j < 2):
                    dve.wait_ge(s["downmm"], job + j - 1)
                v.tensor_tensor(hid[:, j % 2, 0:n], bank[j % 2][:, T:T + n], sg[:, j % 2, 0:n], ALU.mult)\
                    .then_inc(s["hid_ready"], 1)

            for half in range(2):
                done = 0
                for j in range(JT):
                    gated(j, T, half * JT)
                    for i in range(3 if j < JT - 1 else 2):
                        ada_strip(6 + 4 * half + done // KT, done % KT)
                        done += 1
                    if j in (4, 7, 9):
                        i = (4, 7, 9).index(j)
                        b = 6 + 4 * half + i
                        dve.wait_ge(s["ada_reduced"], b + 1)
                        v.tensor_tensor(mod[:, b * KT:(b + 1) * KT], bank[3][:, i * KT:(i + 1) * KT],
                                        bcol[:, b * KT:(b + 1) * KT], ALU.add).then_inc(s["mod_ready"], 1)
                b = 9 + 4 * half
                dve.wait_ge(s["ada_reduced"], b + 1)
                v.tensor_tensor(mod[:, b * KT:(b + 1) * KT], bank[3][:, 3 * KT:4 * KT],
                                bcol[:, b * KT:(b + 1) * KT], ALU.add).then_inc(s["mod_ready"], 1)
            dve.wait_ge(s["downmm"], 2 * JT)
            for d in range(KT):
                residual(d, wide[:, d * T:(d + 1) * T], GT_F)
            scale_of(2, KV_SC, V_KV)
            scale_of(3, L1 + SC_M, V_MIX + KT)
            scale_of(4, L1 + SC_F, V_FFN + KT)
            inverse(2)
            norm(2, nT)
            norm(3, n2T)

            for u in range(2 * SLOTS + 1):
                if u < 2 * SLOTS:
                    h, b = divmod(u, 2)
                    dve.wait_ge(s["dscore"], u + 1)
                    if b == 0:
                        dve.wait_ge(rel_in[h % 2], 16 * (h // 2 + 1))
                    if h >= 1:
                        dve.wait_ge(s["dprobT"], 3 * (h - 1) + (1 if b == 0 else 3))
                    n = (b + 1) * P
                    if b == 0:
                        src, dst = bank[0][:, 0:3 * P], pd[:, 0:3 * P]
                        parts = [(src.rearrange("p (g n) -> p g n", n=n), dst.rearrange("p (g n) -> p g n", n=n),
                                  relT[:, h % 2, :, P:2 * P])]
                    else:
                        parts = []
                        parts.append((bank[1][:, :].rearrange("p (g n) -> p g n", n=n),
                                      pd[:, 3 * P:7 * P].rearrange("p (g n) -> p g n", n=n), relT[:, h % 2, 0:2, :]))
                        parts.append((bank[2][:, 0:T], pd[:, 7 * P:9 * P], relT[:, h % 2, 2, :]))
                    for i, (a, o, bias) in enumerate(parts):
                        start = HUGE if i == 0 else npart[:, h:h + 1]
                        acc = nmax[:, b, h:h + 1] if i == len(parts) - 1 else npart[:, h:h + 1]
                        ins = v.tensor_tensor_reduce(out=o, in0=a, in1=bias, scale=-HD ** -0.5, scalar=start,
                                                     op0=ALU.add, op1=ALU.min, accum_out=acc)
                        if i < len(parts) - 1:
                            link(ins)
                    ins.then_inc(s["dmask"], 1)
                for q in {0: (), 1: (0,)}.get(u, ((3 * (u // 2) - 2, 3 * (u // 2) - 1) if u % 2 == 0
                                                  else (3 * (u // 2),))):
                    dve.wait_ge(s["dprobT"], q + 1)
                    if q >= 2:
                        dve.wait_ge(s["dpv"], q - 1)
                    v.tensor_copy(pdT[:, q % 2, :], (bank[3] if q % 2 == 0 else upper[0])[:, 0:3 * P])\
                        .then_inc(s["dprobT_sb"], 1)
            dve.wait_ge(s["dpv"], 3 * SLOTS)
            dve.wait_ge(s["dexp"], 2 * SLOTS)
            link(v.reciprocal(rinv[:, :, 0:SLOTS], rsum[:, :, 0:SLOTS]))
            divide([upper[1], upper[2]], slice(0, SLOTS), Od, s["od_norm"], rinv)
            for d in range(KT):
                dve.wait_ge(s["odmm"], d + 1)
                residual(d, upper[d % 4][:, 0:T], L1 + GT_M)
            inverse(3)
            norm(4, nT)

            dve.wait_ge(s["logit"], 1)
            sm = [small[:, i, :, 0:NE] for i in range(12)]
            chosen, gate, lg, first, second, rest, eq, tmp = sm[:8]
            one = [P, TB, NE]
            link(v.tensor_copy(lg, bank[3][:, 0:TB * NE].rearrange("p (b e) -> p b e", e=NE)))
            down_count = con[:, C_IOTA + 1:C_IOTA + 1 + NE]
            for vals, hot, best in ((lg, first, sm[9][:, :, 0:1]), (rest, second, sm[9][:, :, 1:2])):
                link(v.tensor_reduce(best, vals, AX_X, ALU.max))
                link(v.tensor_tensor(eq, vals, best.broadcast_to(one), ALU.is_equal))
                for b in range(TB):
                    link(v.scalar_tensor_tensor(out=tmp[:, b, :], in0=down_count, scalar=-9.0, in1=eq[:, b, :],
                                                op0=ALU.add, op1=ALU.mult))
                link(v.tensor_reduce(sm[9][:, :, 2:3], tmp, AX_X, ALU.min))
                link(v.tensor_tensor(hot, tmp, sm[9][:, :, 2:3].broadcast_to(one), ALU.is_equal))
                if hot is first:
                    link(v.scalar_tensor_tensor(out=rest, in0=first, scalar=-HUGE, in1=lg, op0=ALU.mult, op1=ALU.add))
            v.tensor_tensor(chosen, first, second, ALU.add).then_inc(s["routed"], 1)
            v.tensor_tensor(sm[8][:, :, 1:2], sm[9][:, :, 1:2], sm[9][:, :, 0:1], ALU.subtract)\
                .then_inc(s["routed_gap"], 1)
            dve.wait_ge(s["gap_exp"], 1)
            link(v.tensor_scalar(sm[9][:, :, 3:4], sm[8][:, :, 0:1], 1.0, None, ALU.add))
            link(v.reciprocal(sm[9][:, :, 4:5], sm[9][:, :, 3:4]))
            link(v.tensor_tensor(sm[9][:, :, 5:6], sm[9][:, :, 4:5], sm[8][:, :, 0:1], ALU.mult))
            link(v.tensor_tensor(gate, first, sm[9][:, :, 4:5].broadcast_to(one), ALU.mult))
            link(v.tensor_tensor(tmp, second, sm[9][:, :, 5:6].broadcast_to(one), ALU.mult))
            link(v.tensor_tensor(gate, gate, tmp, ALU.add))
            dve.wait_ge(s["rankmm"], 1)
            rank = sm[10]
            link(v.tensor_copy(rank, bank[2][:, 0:TB * NE].rearrange("p (b e) -> p b e", e=NE)))
            v.tensor_copy(counts[:, :], bank[2][0:1, 2 * NE:3 * NE]).then_inc(s["count_sb"], 1)
            dve.wait_ge(s["count_sb"], 1)

            def select_tokens(e):
                for b in range(TB):
                    r = small[:, 10, b, bass.ds(e, 1)]
                    v.tensor_scalar(sel[:, b, :], iota, r, small[:, 0, b, bass.ds(e, 1)], ALU.is_equal, ALU.mult)
                    ins = v.tensor_scalar(selg[:, b, :], iota, r, small[:, 1, b, bass.ds(e, 1)], ALU.is_equal, ALU.mult)
                ins.then_inc(s["selmade"], 1)

            dve.wait_ge(s["moe_sum"], 1)
            select_tokens(0)
            with dve.Fori(0, NE) as e:
                count = dve.value_load(counts[0:1, bass.ds(e, 1)], min_val=0, max_val=T)

                def expert(n):
                    with dve.Fori(0, 2) as hf:
                        for j in range(JT):
                            gated(j, n, 2 * JT + (e * 2 + hf) * JT)
                by_width(dve, count, expert)
                dve.wait_ge(s["selT"], e + 1)
                select_tokens(e + 1)
                dve.wait_ge(s["scatmm"], e + 1)
                for i in range(4):
                    m = moe[:, 2 * i:2 * i + 2, :]
                    ins = v.tensor_tensor(m, bank[i][:, :].rearrange("p (a t) -> p a t", t=T), m, ALU.add)
                ins.then_inc(s["moe_sum"], 1)
            dve.wait_ge(s["moe_sum"], NE + 1)
            for d in range(KT):
                residual(d, moe[:, d, :], L1 + GT_F)
            inverse(4)
            for j in range(KT):
                v.scalar_tensor_tensor(out=nT[:, j, :], in0=hT[:, j, :], scalar=vec[:, V_FINAL + j:V_FINAL + j + 1],
                                       in1=rstd[:, 0, :], op0=ALU.mult, op1=ALU.mult).then_inc(s["scaled"], 1)
            for i in range(1, 4, 2):
                dve.wait_ge(s["finT"], i + 1)
                v.tensor_copy(otok[:, i // 2, 512:D], upper[i]).then_inc(s["fin_dve"], 1)


def constants():
    import numpy as np
    con = np.zeros((P, NCONST), np.float32)
    con[:, C_ID:C_ID + P] = np.eye(P)
    i = np.arange(ROPE // 2)
    con[NOPE + ROPE // 2 + i, C_PERM + i] = -1.0
    con[NOPE + i, C_PERM + ROPE // 2 + i] = 1.0
    q, k = np.arange(P)[:, None], np.arange(P)[None, :]
    con[:, C_CAUSAL:C_CAUSAL + P] = np.where(k <= q, 0.0, -BIG)
    con[:, C_BEFORE:C_BEFORE + P] = q < k
    con[:, C_IOTA:C_IOTA + T] = np.arange(T)
    freq = np.float32(10000.0) ** (-np.arange(0, ROPE, 2, dtype=np.float32) / np.float32(ROPE))
    con[NOPE:QK, C_FREQ] = np.concatenate([freq, freq])
    onehot = np.zeros((BUCKETS, GROUPS, NREL), np.float32)
    relmask = np.zeros((SLOTS, GROUPS, NREL), np.float32)
    exact = BUCKETS // 2
    for g, (dil, span) in enumerate(zip(DILATIONS, SPANS)):
        for m in range(NREL):
            d = T - 1 - m
            if d < 0 or d % dil or d // dil > span:
                relmask[:, g, m] = -BIG
                continue
            big = exact + int(np.log(np.float32(max(d, 1)) / np.float32(exact)) / np.float32(np.log(2048 / exact))
                              * np.float32(BUCKETS - exact))
            onehot[d if d < exact else min(big, BUCKETS - 1), g, m] = 1.0
    return con, onehot.reshape(BUCKETS, -1), relmask.reshape(SLOTS, -1)


_INS = ['x', 'c', 'positions', 'g_mix', 'g_ffn', 'w_ada', 'b_ada', 'w_mla_in', 'g_mla_q', 'w_mla_q_up', 'g_mla_kv',
        'w_mla_kv_up', 'w_mla_out', 'g_kv_b', 'w_ada_kv', 'b_ada_kv', 'w_kv_b', 'rpb_table', 'w_q_b', 'w_o_b',
        'w_ffn_gu', 'w_ffn_down', 'w_router', 'w_exp_gu', 'w_exp_down', 'g_final']


def kernel(**inputs):
    import numpy as _np
    import concourse.bacc as _bacc
    from concourse import mybir as _mybir
    from concourse.bass_utils import run_bass_kernel_spmd as _run

    nc = _bacc.Bacc("TRN2", target_bir_lowering=False, num_devices=1)
    arrays, args = {}, []
    given = [(name, _np.ascontiguousarray(inputs[name])) for name in _INS]
    given += list(zip(("consts", "onehot", "relmask"), constants()))
    for name, a in given:
        arrays[f"in_{name}"] = a
        args.append(nc.dram_tensor(f"in_{name}", a.shape, _mybir.dt.from_np(a.dtype), kind="ExternalInput").ap())
    args.append(nc.dram_tensor("out_0", (1, T, D), _mybir.dt.float32, kind="ExternalOutput").ap())
    trunk(nc, *args)
    r = _run(nc, [arrays], core_ids=[0])
    return r.results[0]["out_0"]
```

```python
from contextlib import ExitStack

import concourse.bass as bass
from concourse import mybir

F32 = mybir.dt.float32
F32R = mybir.dt.float32r
BF16 = mybir.dt.bfloat16
I32 = mybir.dt.int32
ALU = mybir.AluOpType
ACT = mybir.ActivationFunctionType
AX_X = mybir.AxisListType.X

P = 128
D = 1024
T = 256
TB = T // P
KT = D // P
FF = 2816
HALF = FF // 2
JT = HALF // P
NCH = (JT + 1) // 2
NE = 8
HEADS = 16
NOPE, ROPE, VD = 64, 32, 64
QK = NOPE + ROPE
QR, KVR = 384, 256
QRT, KVT = QR // P, KVR // P
GROUPS, SLOTS, HD = 3, 8, 64
DILATIONS = (1, 4, 16)
SPANS = (128, 128, 128)
BUCKETS = 32
DQ = SLOTS * HD
NREL = 384
EPS = 1e-6
BIG = 1e30
HUGE = 3e38
CHUNKS = 2 * NCH
LEAD = 3
RING, SLOT = 9, 2048
ADAS, BLOCKS = 4, 14
TWO_PI_HI, TWO_PI_MID = 6.28125, 0.0019350051879882812
ROUND = 12582912.0

C_ID, C_PERM, C_OPEN, C_CAUSAL, C_BEFORE, C_IOTA, C_FREQ, NCONST = 0, 128, 160, 288, 416, 544, 800, 801
V_C, V_MIX, V_FFN, V_KV, V_FINAL, V_LQ, V_LKV, NVEC = 0, 8, 24, 40, 48, 56, 59, 61
SH_M, SC_M, GT_M, SH_F, SC_F, GT_F = range(6)
KV_SH, KV_SC, L1 = 6, 7, 8


def trunk(nc, x, c, positions, g_mix, g_ffn, w_ada, b_ada, w_mla_in, g_mla_q, w_mla_q_up, g_mla_kv,
          w_mla_kv_up, w_mla_out, g_kv_b, w_ada_kv, b_ada_kv, w_kv_b, rpb_table, w_q_b, w_o_b,
          w_ffn_gu, w_ffn_down, w_router, w_exp_gu, w_exp_down, g_final, consts, onehot, relmask, out):
    ctx = ExitStack()
    with ctx:
        def sb(name, shape, dt=F32):
            return ctx.enter_context(nc.sbuf_tensor(name, shape, dt))

        def sem(name):
            return ctx.enter_context(nc.semaphore(name))

        bank = [ctx.enter_context(nc.psum_tensor(f"bank{i}", [P, 512], F32)) for i in range(4)]
        wide = ctx.enter_context(nc.psum_tensor("wide", [P, 2048], F32))
        upper = [wide[:, 512 * i:512 * (i + 1)] for i in range(4)]

        hT = sb("hT", [P, KT, T])
        ring = sb("ring", [P, RING, SLOT])
        KB = 1024
        region0 = nc.sbuf_base
        sb("region", [P, 112 * KB // 4])

        def at(name, start, shape, dt=F32):
            return nc.alloc_sbuf_tensor_at(name, shape, dt, offset=region0 + start)

        nT = at("nT", 0, [P, KT, T])
        sqT = at("sqT", 8 * KB, [P, KT, T])
        strip = at("strip", 16 * KB, [P, ADAS, D])
        adasum = at("adasum", 32 * KB, [P, 2, D])
        arena = at("arena", 40 * KB, [P, 18432])
        w_hi = at("w_hi", 0, [P, 3, SLOT], F32R)
        w_lo = at("w_lo", 24 * KB, [P, 3, SLOT], F32R)
        xg_hi = at("xg_hi", 48 * KB, [P, KT, T], F32R)
        xg_lo = at("xg_lo", 56 * KB, [P, KT, T], F32R)
        hT_hi = at("hT_hi", 64 * KB, [P, 2, T], F32R)
        hT_lo = at("hT_lo", 66 * KB, [P, 2, T], F32R)
        con = sb("con", [P, NCONST])
        ones = sb("ones", [P, P])
        zeros = sb("zeros", [1, 512], BF16)
        vrows = sb("vrows", [NVEC, P])
        brows = sb("brows", [BLOCKS * KT, P])
        vec = sb("vec", [P, NVEC])
        bcol = sb("bcol", [P, BLOCKS * KT])
        mod = sb("mod", [P, BLOCKS * KT])
        cact = sb("cact", [P, KT])
        ascale = sb("ascale", [P, 5, KT])
        eps = sb("eps", [P, 1])
        std = sb("std", [P, 2, T])
        rstd = sb("rstd", [P, 2, T])
        trig = sb("trig", [P, 2, T])
        rsum = sb("rsum", [P, TB, HEADS])
        rinv = sb("rinv", [P, TB, HEADS])
        nmax = sb("nmax", [P, TB, HEADS])
        npart = sb("npart", [P, SLOTS])
        wrout = sb("wrout", [P, KT, NE])
        table = sb("table", [BUCKETS, GROUPS * SLOTS])
        small = sb("small", [P, 12, TB, NE + 1])
        counts = sb("counts", [1, NE + 1], I32)
        scratch = nc.dram_tensor("relbias", [SLOTS, GROUPS, P, NREL], F32, kind="Internal").ap()

        def area(at, *shape):
            size = 1
            for n in shape:
                size *= n
            a = arena[:, at:at + size]
            if len(shape) == 2:
                a = a.rearrange("p (a b) -> p a b", b=shape[1])
            if len(shape) == 3:
                a = a.rearrange("p (a b c) -> p a b c", b=shape[1], c=shape[2])
            return a

        oh = area(0, GROUPS, NREL)
        rmask = area(1152, GROUPS, NREL)
        relb = area(16384, GROUPS, NREL)
        xtok = area(16384, TB, D)
        posi = area(12288, T).bitcast(I32)
        ang = area(12544, 2, T)
        turns = area(13056, 2, T)
        lat = sqT[:, 0:5, :]
        Q = area(0, HEADS, T)
        K = area(4096, HEADS, T)
        V = area(8192, TB, D)
        O = area(10240, TB, D)
        latsq = area(10240, 5, T)
        latn = area(12288, 5, T)
        prob = area(12288, 2, 3 * P)
        probT = area(13056, 2, 3 * P)
        rt = area(14336, 2, 2 * T)
        krot = area(15360, 2, T)
        Qd = area(0, 12, T)
        Kd = area(3072, 12, T)
        Vd = area(6144, TB, 3 * DQ)
        Od = area(9216, TB, DQ)
        n2T = area(10240, KT, T)
        pd = area(12288, 9 * P)
        pdT = area(13440, 2, 3 * P)
        relT = area(14208, 2, GROUPS, 2 * P)
        sg = area(12288, 2, T)
        hid = area(12800, 2, T)
        ntok = area(7168, TB, D)
        yslot = area(9216, TB, D)
        moe = area(11264, KT, T)
        sel = area(13312, TB, T)
        selg = area(13824, TB, T)
        selgT = area(14336, TB, T)
        gate_act = area(14848, TB, T)
        hidden = area(15360, TB, T)
        otok = area(0, TB, D)

        ident = con[:, C_ID:C_ID + P]
        perm = con[NOPE:QK, C_PERM:C_PERM + ROPE]
        causal = con[:, C_CAUSAL:C_CAUSAL + P]
        before = con[:, C_BEFORE:C_BEFORE + P]
        iota = con[:, C_IOTA:C_IOTA + T]
        freq = con[NOPE:QK, C_FREQ:C_FREQ + 1]

        names = """in_vec in_con in_x in_misc in_pos pool_const rel_stored rel_in vecT vec_sb c_ready xT x_act x_dve
            relmm rel_ready trig_step trig_done ada_step ada_reduced mod_ready
            sq stat std_ready dve_own norm_mul norm_ready scaled
            latmm lat_sb latsq_done latstat latstd latn_ready krmm k_rot k_bcast
            qmm q_sb ropemm rope_mul rope_done kmm k_sb vmm v_sb
            mscore masked expd mprobT mprobT_sb mpv o_norm oT oT_sb omm h_ready
            gumm silu_done hid_ready downmm
            kvmm kv_sb qdmm qd_sb dscore dmask dexp dprobT dprobT_sb dpv od_norm odT odT_sb odmm
            logit ntokT ntok_sb routed routed_gap gap_exp rankmm rank_sb count_sb
            selmade gather0 gather1 xg_hi0 xg_hi1 xg_lo0 xg_lo1 selT selT_sb scatmm moe_sum
            hi_a hi_b hi_d lo_a lo_b lo_d gua gub e_silu e_hid e_hT hT_hi_done hT_lo_done e_down y_sb
            finT fin_act fin_dve out_done""".split()
        s = {n: sem(n) for n in names}
        landed = [sem(f"landed{i}") for i in range(RING)]
        strip_in = [sem(f"strip_in{i}") for i in range(ADAS)]
        rel_in = [sem(f"rel_in{i}") for i in range(2)]

        freed = []
        freed += [(s["latmm"], 2 * i + 2) for i in range(3)]
        freed += [(s["qmm"], HEADS)] * QRT
        freed += [(s["vmm"], 4)] * KVT
        freed += [(s["omm"], 2 * i + 2) for i in range(4)]
        T_QUP, T_KVUP, T_OUT, T_FFN = 3, 6, 8, 12

        def tiles_through(c):
            return min(2 * c + 2, JT)
        for half in range(2):
            for ch in range(NCH):
                n = JT * half + tiles_through(ch)
                freed += [(s["gumm"], n), (s["gumm"], n), (s["downmm"], n)]
        T_KVB = len(freed)
        freed += [(s["kvmm"], 2 * i + 2) for i in range(12)]
        T_QB = len(freed)
        freed += [(s["qdmm"], 2 * i + 2) for i in range(6)]
        T_OB = len(freed)
        freed += [(s["odmm"], 4 * i + 4) for i in range(2)]
        T_MOE = len(freed)

        def tile_in(eng, t):
            eng.wait_ge(landed[t % RING], 16 * (t // RING + 1))

        def half_tile_in(eng, base, half, k):
            t = base + k
            eng.wait_ge(landed[t % RING], half * (16 * 3 * NCH // RING) + 16 * (t // RING + 1))

        def slot(t):
            return ring[:, t % RING, :]

        def cols(t, kt=KT, n=None):
            n = n or SLOT // kt
            return slot(t)[:, 0:kt * n].rearrange("p (k n) -> p k n", n=n)

        def by_blocks(eng, e, body):
            count = eng.value_load(counts[0:1, bass.ds(e, 1)], min_val=0, max_val=T)
            with eng.If(count < P + 1):
                body(1)
            with eng.Else():
                body(2)
            eng.nop()

        def unless_last(eng, e, body):
            with eng.If(e < NE - 1):
                body()
            with eng.Else():
                eng.nop()

        def width(c):
            return 2 * P if c % NCH < NCH - 1 else P

        UNITS = ("a", "b", "d")

        def landings(e, c, u):
            t = T_MOE + 3 * c + u
            per = 1 if u == 2 else 2
            before = len([x for x in range(T_MOE) if x % RING == t % RING])
            return e * (16 * per * CHUNKS // LEAD) + 16 * (before + per * (c // LEAD + 1))

        def unit_size(c, u):
            return width(c) * (2 * KT // 2 if u < 2 else D // P)

        block = ctx.enter_context(nc.Block())

        @block.sync
        def _(sp):
            def rows(ap, r0, n):
                return ap[r0:r0 + n, :]

            vlist = [(V_C, c.rearrange("a (j p) -> (a j) p", p=P)), (V_MIX, g_mix.rearrange("a (j p) -> (a j) p", p=P)),
                     (V_FFN, g_ffn.rearrange("a (j p) -> (a j) p", p=P)),
                     (V_KV, g_kv_b.rearrange("(j p) -> j p", p=P)), (V_FINAL, g_final.rearrange("(j p) -> j p", p=P)),
                     (V_LQ, g_mla_q.rearrange("a (j p) -> (a j) p", p=P)),
                     (V_LKV, g_mla_kv.rearrange("a (j p) -> (a j) p", p=P))]
            for at, ap in vlist:
                sp.dma_start(vrows[at:at + ap.shape[0], :], ap).then_inc(s["in_vec"], 16)
            ba = b_ada.rearrange("l (j p) -> (l j) p", p=P)
            sp.dma_start(brows[0:48, :], ba[0:48, :]).then_inc(s["in_vec"], 16)
            sp.dma_start(brows[48:64, :], b_ada_kv.rearrange("(j p) -> j p", p=P)).then_inc(s["in_vec"], 16)
            sp.dma_start(brows[64:112, :], ba[48:96, :]).then_inc(s["in_vec"], 16)

            def load(t, dst, src):
                if t >= RING:
                    sp.wait_ge(*freed[t - RING])
                sp.dma_start(dst, src).then_inc(landed[t % RING], 16)

            strips = "(k p) n -> p k n"
            sp.wait_ge(s["ada_step"], KT + 5)
            for i, (a, b) in enumerate(((0, 256), (256, 512), (512, 672))):
                load(i, cols(i, KT, b - a), w_mla_in[0][:, a:b].rearrange(strips, p=P))
            for k in range(QRT):
                load(T_QUP + k, slot(T_QUP + k)[:, 0:HEADS * QK], w_mla_q_up[0][k * P:(k + 1) * P, :])
            for k in range(KVT):
                load(T_KVUP + k, slot(T_KVUP + k), w_mla_kv_up[0][k * P:(k + 1) * P, :])
            for i in range(4):
                load(T_OUT + i, cols(T_OUT + i), w_mla_out[0][:, 256 * i:256 * (i + 1)].rearrange(strips, p=P))
            for half in range(2):
                for ch in range(NCH):
                    t = T_FFN + 3 * (NCH * half + ch)
                    f0, n = half * HALF + ch * 256, min(256, HALF - ch * 256)
                    load(t, cols(t, KT, n), w_ffn_gu[0][:, f0:f0 + n].rearrange(strips, p=P))
                    load(t + 1, cols(t + 1, KT, n), w_ffn_gu[0][:, FF + f0:FF + f0 + n].rearrange(strips, p=P))
                    load(t + 2, cols(t + 2, n // P, D), w_ffn_down[0][f0:f0 + n, :].rearrange(strips, p=P))
            for i in range(12):
                load(T_KVB + i, cols(T_KVB + i), w_kv_b[:, 256 * i:256 * (i + 1)].rearrange(strips, p=P))
            for i in range(6):
                load(T_QB + i, cols(T_QB + i), w_q_b[0][:, 256 * i:256 * (i + 1)].rearrange(strips, p=P))
            for i in range(2):
                load(T_OB + i, cols(T_OB + i, 4), w_o_b[0][:, 512 * i:512 * (i + 1)].rearrange(strips, p=P))

            gu_rows = w_exp_gu[0].rearrange("e d n -> (e d) n").rearrange("r (i f) -> r i f", i=2)
            down_rows = w_exp_down[0].rearrange("e f n -> (e f) n")
            for t in range(T_MOE - RING, T_MOE):
                sp.wait_ge(*freed[t])
            with sp.Fori(0, NE) as e:
                for ch in range(CHUNKS):
                    n = width(ch)
                    f0 = (ch // NCH) * HALF + (ch % NCH) * 2 * P
                    for u in range(3):
                        sp.wait_ge(s["lo_" + UNITS[u]], e * CHUNKS + ch + 1)
                        to = slot(T_MOE + 3 * ch + u)[:, 0:unit_size(ch, u)]
                        if u < 2:
                            src = gu_rows[bass.ds(e * D + u * (D // 2), D // 2), :, f0:f0 + n]
                            for i in range(2):
                                sp.dma_start(to.rearrange("p (k i n) -> p k i n", i=2, n=n)[:, :, i, :],
                                             src[:, i, :].rearrange(strips, p=P))\
                                    .then_inc(landed[(T_MOE + 3 * ch + u) % RING], 16)
                        else:
                            src = down_rows[bass.ds(e * FF + f0, n), :].rearrange(strips, p=P)
                            sp.dma_start(to.rearrange("p (k n) -> p k n", n=D), src)\
                                .then_inc(landed[(T_MOE + 3 * ch + u) % RING], 16)
            ov = out[0].rearrange("(b p) d -> p b d", p=P)
            for b in range(TB):
                sp.wait_ge(s["fin_act"], b + 1)
                sp.wait_ge(s["fin_dve"], b + 1)
                sp.dma_start(ov[:, b, :], otok[:, b, :]).then_inc(s["out_done"], 16)
            sp.wait_ge(s["out_done"], 16 * TB)

        @block.gpsimd
        def _(pool):
            nc.gpsimd.memset(ones[:, :], 1.0).then_inc(s["pool_const"], 1)
            nc.gpsimd.memset(eps[:, :], EPS).then_inc(s["pool_const"], 1)
            nc.gpsimd.memset(zeros[:, :], 0.0).then_inc(s["pool_const"], 1)
            nc.gpsimd.memset(small[:, :, :, :], 0.0).then_inc(s["pool_const"], 1)
            nc.gpsimd.memset(counts[:, :], 0).then_inc(s["pool_const"], 1)

            def blocks(first, w, col):
                for k in range(KT):
                    n = first * KT + k
                    if not (isinstance(n, int) and n < ADAS):
                        pool.wait_ge(s["ada_step"], n - ADAS + 1)
                    pool.dma_start(strip[:, k % ADAS, :], w[k * P:(k + 1) * P, col])\
                        .then_inc(strip_in[k % ADAS], 16)

            blocks(0, w_ada[0], slice(0, D))
            with pool.Fori(1, 4) as b:
                blocks(b, w_ada[0], bass.ds(b * D, D))
            pool.wait_ge(s["k_rot"], 1)
            nc.gpsimd.tensor_copy(K[NOPE:QK, :, :], krot[NOPE:QK, 1:2, :].broadcast_to([ROPE, HEADS, T]))\
                .then_inc(s["k_bcast"], 1)
            with pool.Fori(4, 6) as b:
                blocks(b, w_ada[0], bass.ds(b * D, D))
            pool.wait_ge(s["rel_ready"], GROUPS)
            for g in range(GROUPS):
                pool.dma_start(scratch[:, g, :, :], relb[0:SLOTS, g:g + 1, :].broadcast_to([SLOTS, P, NREL]))\
                    .then_inc(s["rel_stored"], 16)
            with pool.Fori(0, 2) as b:
                blocks(b + KV_SH, w_ada_kv, bass.ds(b * D, D))
            with pool.Fori(0, 6) as b:
                blocks(b + L1, w_ada[1], bass.ds(b * D, D))
            pool.wait_ge(s["rel_stored"], 16 * GROUPS)
            pool.wait_ge(s["mpv"], HEADS)
            pool.wait_ge(s["rope_done"], SLOTS)
            for h in range(SLOTS):
                if h >= 2:
                    pool.wait_ge(s["dmask"], 2 * (h - 1))
                src = bass.AP(scratch.tensor, h * GROUPS * P * NREL + P - 1,
                              [[NREL - 1, P], [P * NREL, GROUPS], [1, 2 * P]])
                pool.dma_start(relT[:, h % 2, :, :], src).then_inc(rel_in[h % 2], 16)
            for u in UNITS:
                pool.sem_inc(s["lo_" + u], LEAD)
            pool.wait_ge(s["odT"], 4)
            nc.gpsimd.memset(moe[:, :, :], 0.0).then_inc(s["moe_sum"], 1)

        @block.tensor
        def _(pe):
            mm, tr = nc.tensor.matmul, nc.tensor.transpose

            def turn(o, a, first):
                return mm(o, a, ident, start=True, stop=True) if first else tr(o, a, ident)

            def product(o, pairs):
                n = len(pairs)
                for i, (w, r) in enumerate(pairs):
                    last = mm(o, w, r, start=(i == 0), stop=(i == n - 1))
                return last

            def ada_reduce(b, i=None, dyn=0):
                i = b if i is None else i
                pe.wait_ge(s["ada_step"], dyn * KT + KT * (b + 1))
                if b >= 1:
                    pe.wait_ge(s["mod_ready"], dyn + b)
                for j in range(KT):
                    last = mm(bank[3][:, KT * i + j:KT * i + j + 1], adasum[:, b % 2, j * P:(j + 1) * P],
                              ones[:, 0:1], start=True, stop=True)
                last.then_inc(s["ada_reduced"], 1)

            def norm_stat(k):
                for j in range(KT):
                    pe.wait_ge(s["sq"], KT * k + j + 1)
                    last = mm(bank[2][:, 0:T], ones[:, :], sqT[:, j, :], start=(j == 0), stop=(j == KT - 1))
                last.then_inc(s["stat"], 1)

            pe.wait_ge(s["in_vec"], 16 * 10)
            pe.wait_ge(s["in_con"], 16)
            tr(bank[0][:, 0:NVEC], vrows[:, :], ident[0:NVEC, 0:NVEC]).then_inc(s["vecT"], 1)
            nb = BLOCKS * KT
            tr(bank[1][:, 0:nb], brows[:, :], ident[0:nb, 0:nb]).then_inc(s["vecT"], 1)
            pe.wait_ge(s["in_x"], 16)
            for d in range(KT):
                if d >= 4:
                    pe.wait_ge(s["x_act"] if d % 2 == 0 else s["x_dve"], (d - 4) // 2 + 1)
                for b in range(TB):
                    last = tr(upper[d % 4][:, b * P:(b + 1) * P], xtok[:, b, d * P:(d + 1) * P], ident)
                last.then_inc(s["xT"], 1)
            pe.wait_ge(s["in_misc"], 16 * 4)
            pe.wait_ge(s["vec_sb"], 2)
            for g in range(GROUPS):
                mm(bank[g][0:SLOTS, 0:NREL], table[:, g * SLOTS:(g + 1) * SLOTS], oh[0:BUCKETS, g, :],
                   start=True, stop=True).then_inc(s["relmm"], 1)
            pe.wait_ge(s["rel_ready"], GROUPS)
            pe.wait_ge(s["pool_const"], 5)
            norm_stat(0)
            ada_reduce(0)
            ada_reduce(1)

            for i in range(6):
                if i % 2 == 0:
                    tile_in(pe, i // 2)
                if i >= 4:
                    pe.wait_ge(s["latsq_done"], i - 3)
                w = cols(i // 2, KT, 256 if i < 4 else 160)
                o = upper[i % 4][:, 0:T] if i < 5 else upper[1][NOPE:QK, 0:T]
                n = P if i < 5 else ROPE
                for k in range(KT):
                    if i == 0:
                        pe.wait_ge(s["norm_ready"], k + 1)
                    last = mm(o, w[:, k, (i % 2) * P:(i % 2) * P + n], nT[:, k, :], start=(k == 0), stop=(k == KT - 1))
                last.then_inc(s["latmm"], 1)
            pe.wait_ge(s["latsq_done"], 5)
            product(bank[2][:, 0:T], [(ones[:, :], latsq[:, i, :]) for i in range(QRT)]).then_inc(s["latstat"], 1)
            product(bank[1][:, 0:T], [(ones[:, :], latsq[:, QRT + i, :]) for i in range(KVT)])\
                .then_inc(s["latstat"], 1)
            pe.wait_ge(s["lat_sb"], 6)
            mm(bank[0][NOPE:QK, 0:T], perm, krot[NOPE:QK, 0, :], start=True, stop=True).then_inc(s["krmm"], 1)

            for k in range(QRT):
                tile_in(pe, T_QUP + k)
            for h in range(HEADS):
                if h >= 4:
                    pe.wait_ge(s["q_sb"], h - 3)
                if h == 0:
                    pe.wait_ge(s["latn_ready"], QRT)
                product(upper[h % 4][0:QK, 0:T], [(slot(T_QUP + k)[:, h * QK:(h + 1) * QK], latn[:, k, :])
                                                  for k in range(QRT)]).then_inc(s["qmm"], 1)
            pe.wait_ge(s["latn_ready"], 5)
            pe.wait_ge(s["k_rot"], 1)
            for k in range(KVT):
                tile_in(pe, T_KVUP + k)
            for p in range(HEADS // 2):
                if p >= 2:
                    pe.wait_ge(s["rope_mul"], p - 1)
                pe.wait_ge(s["q_sb"], min(2 * p + 6, HEADS))
                mm(bank[p % 2][NOPE:QK, 0:2 * T], perm, Q[NOPE:QK, 2 * p:2 * p + 2, :],
                   start=True, stop=True).then_inc(s["ropemm"], 1)
                for h in (2 * p, 2 * p + 1):
                    if h >= 4:
                        pe.wait_ge(s["k_sb"], h - 3)
                    if h == 0:
                        pe.wait_ge(s["q_sb"], HEADS)
                    product(upper[h % 4][0:NOPE, 0:T], [(slot(T_KVUP + k)[:, h * P:h * P + NOPE], latn[:, QRT + k, :])
                                                        for k in range(KVT)]).then_inc(s["kmm"], 1)
            for i in range(4):
                b, half = i // 2, i % 2
                pe.wait_ge(s["k_sb"], HEADS - 3 + i)
                product(upper[i], [(latn[:, QRT + k, b * P:(b + 1) * P],
                                    slot(T_KVUP + k).rearrange("p (h c) -> p h c", c=P)[:, half * 8:half * 8 + 8, NOPE:P])
                                   for k in range(KVT)]).then_inc(s["vmm"], 1)
            ada_reduce(2)
            ada_reduce(3)

            pe.wait_ge(s["rope_done"], HEADS // 2)
            pe.wait_ge(s["k_bcast"], 1)
            pe.wait_ge(s["v_sb"], 4)
            pe.wait_ge(s["mod_ready"], 4)
            for i in range(HEADS + 2):
                if i < HEADS:
                    h = i
                    if h >= 2:
                        pe.wait_ge(s["masked"], 2 * (h - 1))
                    mm(bank[h % 2][:, 0:P], Q[0:QK, h, 0:P], K[0:QK, h, 0:P], start=True, stop=True)
                    mm(bank[h % 2][:, P:3 * P], Q[0:QK, h, P:T], K[0:QK, h, :], start=True, stop=True)\
                        .then_inc(s["mscore"], 1)
                if 1 <= i <= HEADS:
                    h = i - 1
                    pe.wait_ge(s["expd"], 2 * (h + 1))
                    if h >= 2:
                        pe.wait_ge(s["mprobT_sb"], h - 1)
                    for j in range(3):
                        last = tr(bank[2 + h % 2][:, j * P:(j + 1) * P], prob[:, h % 2, j * P:(j + 1) * P], ident)
                    last.then_inc(s["mprobT"], 1)
                if i >= 2:
                    h = i - 2
                    pe.wait_ge(s["mprobT_sb"], h + 1)
                    o = upper[2 * (h // 8)][:, (h % 8) * VD:(h % 8 + 1) * VD]
                    mm(o, probT[:, h % 2, 0:P], V[:, 0, h * VD:(h + 1) * VD], start=True, stop=True)
                    o = upper[2 * (h // 8) + 1][:, (h % 8) * VD:(h % 8 + 1) * VD]
                    product(o, [(probT[:, h % 2, (b + 1) * P:(b + 2) * P], V[:, b, h * VD:(h + 1) * VD])
                                for b in range(TB)]).then_inc(s["mpv"], 1)
            for d in range(KT):
                pe.wait_ge(s["o_norm"], 2 * (d // 4 + 1))
                if d >= 2:
                    pe.wait_ge(s["oT_sb"], d - 1)
                for b in range(TB):
                    last = tr(bank[d % 2][:, b * P:(b + 1) * P], O[:, b, d * P:(d + 1) * P], ident)
                last.then_inc(s["oT"], 1)
            pe.wait_ge(s["oT_sb"], KT)
            for d in range(KT):
                if d % 2 == 0:
                    tile_in(pe, T_OUT + d // 2)
                if d >= 4:
                    pe.wait_ge(s["h_ready"], d - 3)
                product(upper[d % 4][:, 0:T], [(cols(T_OUT + d // 2)[:, k, (d % 2) * P:(d % 2 + 1) * P], nT[:, k, :])
                                               for k in range(KT)]).then_inc(s["omm"], 1)
            norm_stat(1)
            ada_reduce(4)
            ada_reduce(5)

            def open_sums(n):
                for i in range(n):
                    last = mm(upper[i], zeros[:, 0:P], zeros[:, :], start=True, stop=False, skip_group_check=True)
                return last

            def ffn_half(base, half, n, src, before=0, extra=None):
                job0 = half * JT

                def down(j):
                    k = 3 * (j // 2) + 2
                    if j % 2 == 0:
                        half_tile_in(pe, base, half, k)
                    pe.wait_ge(s["hid_ready"], before + job0 + j + 1)
                    w = cols(base + k, 2 if j < JT - 1 else 1, D)
                    for d in range(KT):
                        last = mm(wide[:, d * n:(d + 1) * n], w[:, j % 2, d * P:(d + 1) * P],
                                  hid[:, j % 2, 0:n], start=False, stop=False, skip_group_check=True)
                    last.then_inc(s["downmm"], 1)

                for j in range(JT):
                    k = 3 * (j // 2)
                    if j % 2 == 0:
                        half_tile_in(pe, base, half, k)
                        half_tile_in(pe, base, half, k + 1)
                    if j >= 2:
                        pe.wait_ge(s["hid_ready"], before + job0 + j - 1)
                    m = 256 if j < JT - 1 else P
                    for i in range(2):
                        w = cols(base + k + i, KT, m)
                        for kt in range(KT):
                            last = mm(bank[j % 2][:, i * T:i * T + n], w[:, kt, (j % 2) * P:(j % 2 + 1) * P],
                                      src(kt), start=(kt == 0), stop=(kt == KT - 1))
                    last.then_inc(s["gumm"], 1)
                    if j >= 1:
                        down(j - 1)
                    if extra:
                        extra(j)
                down(JT - 1)

            pe.wait_ge(s["h_ready"], KT)
            pe.wait_ge(s["oT_sb"], KT)
            open_sums(4)
            pe.wait_ge(s["norm_ready"], 2 * KT)
            with pe.Fori(0, 2) as half:
                def extra(j):
                    if j in (4, 7, 9):
                        i = (4, 7, 9).index(j)
                        ada_reduce(6 + i, i, half * 4)
                ffn_half(T_FFN, half, T, lambda kt: nT[:, kt, :], 0, extra)
                ada_reduce(9, 3, half * 4)

            norm_stat(2)
            for i in range(24):
                t = T_KVB + i // 2
                if i % 2 == 0:
                    tile_in(pe, t)
                if i == 0:
                    pe.wait_ge(s["norm_ready"], 3 * KT)
                    pe.wait_ge(s["h_ready"], 2 * KT)
                if i >= 4:
                    pe.wait_ge(s["kv_sb"], i - 3)
                if (i // 2) % 4 < 2:
                    pairs = [(cols(t)[:, k, (i % 2) * P:(i % 2 + 1) * P], nT[:, k, :]) for k in range(KT)]
                else:
                    pairs = [(nT[:, k, (i % 2) * P:(i % 2 + 1) * P], cols(t)[:, k, :]) for k in range(KT)]
                product(upper[i % 4][:, 0:T], pairs).then_inc(s["kvmm"], 1)
            pe.wait_ge(s["norm_ready"], 4 * KT)
            for i in range(12):
                t = T_QB + i // 2
                if i % 2 == 0:
                    tile_in(pe, t)
                if i < 4:
                    pe.wait_ge(s["kv_sb"], 21 + i)
                else:
                    pe.wait_ge(s["qd_sb"], i - 3)
                product(upper[i % 4][:, 0:T], [(cols(t)[:, k, (i % 2) * P:(i % 2 + 1) * P], n2T[:, k, :])
                                               for k in range(KT)]).then_inc(s["qdmm"], 1)

            pe.wait_ge(s["qd_sb"], 12)

            def dscores(u):
                h, b = divmod(u, 2)
                if u >= 2:
                    pe.wait_ge(s["dmask"], u - 1)
                p0 = (h % 2) * HD
                for g in range(GROUPS):
                    t = 4 * g + h // 2
                    n = (b + 1) * P
                    o = bank[0][:, g * P:(g + 1) * P] if b == 0 else bank[1 + g // 2][:, (g % 2) * T:(g % 2) * T + T]
                    last = mm(o, Qd[p0:p0 + HD, t, b * P:(b + 1) * P], Kd[p0:p0 + HD, t, 0:n], start=True, stop=True)
                last.then_inc(s["dscore"], 1)

            def dtranspose(q):
                h, r = divmod(q, 3)
                pe.wait_ge(s["dexp"], 2 * h + (1 if r == 0 else 2))
                if q >= 2:
                    pe.wait_ge(s["dprobT_sb"], q - 1)
                o = bank[3] if q % 2 == 0 else upper[0]
                for j in range(3):
                    last = tr(o[:, j * P:(j + 1) * P], pd[:, (3 * r + j) * P:(3 * r + j + 1) * P], ident)
                last.then_inc(s["dprobT"], 1)

            def dvalues(q):
                h, r = divmod(q, 3)
                pe.wait_ge(s["dprobT_sb"], q + 1)
                o = upper[1 if r == 0 else 2][:, h * HD:(h + 1) * HD]
                for j in range(3):
                    g, kb = (j, 0) if r == 0 else divmod(3 * (r - 1) + j, 2)
                    first = j == 0 and r < 2
                    last = mm(o, pdT[:, q % 2, j * P:(j + 1) * P], Vd[:, kb, g * DQ + h * HD:g * DQ + (h + 1) * HD],
                              start=first, stop=(j == 2 and r != 1))
                last.then_inc(s["dpv"], 1)

            dscores(0)
            dscores(1)
            for h in range(SLOTS):
                for r in range(3):
                    q = 3 * h + r
                    dtranspose(q)
                    if q >= 1:
                        dvalues(q - 1)
                    if h + 1 < SLOTS and r in (0, 1):
                        dscores(2 * h + 2 + r)
            dvalues(3 * SLOTS - 1)
            for d in range(4):
                pe.wait_ge(s["od_norm"], TB)
                if d >= 2:
                    pe.wait_ge(s["odT_sb"], d - 1)
                for b in range(TB):
                    last = tr(bank[d % 2][:, b * P:(b + 1) * P], Od[:, b, d * P:(d + 1) * P], ident)
                last.then_inc(s["odT"], 1)
            pe.wait_ge(s["odT_sb"], 4)
            for d in range(KT):
                if d % 4 == 0:
                    tile_in(pe, T_OB + d // 4)
                if d >= 4:
                    pe.wait_ge(s["h_ready"], 2 * KT + d - 3)
                product(upper[d % 4][:, 0:T], [(cols(T_OB + d // 4, 4)[:, k, (d % 4) * P:(d % 4 + 1) * P], nT[:, k, :])
                                               for k in range(4)]).then_inc(s["odmm"], 1)
            norm_stat(3)

            pe.wait_ge(s["norm_ready"], 5 * KT)
            for b in range(TB):
                last = product(bank[3][:, b * NE:(b + 1) * NE],
                               [(nT[:, k, b * P:(b + 1) * P], wrout[:, k, :]) for k in range(KT)])
            last.then_inc(s["logit"], 1)
            for i in range(4):
                b, half = i // 2, i % 2
                for j in range(4):
                    d = 4 * half + j
                    last = tr(upper[i][:, j * P:(j + 1) * P], nT[:, d, b * P:(b + 1) * P], ident)
                last.then_inc(s["ntokT"], 1)
            pe.wait_ge(s["routed"], 1)
            chosen = small[:, 0, :, 0:NE]
            mm(bank[2][:, 0:NE], before, chosen[:, 0, :], start=True, stop=True)
            product(bank[2][:, NE:2 * NE], [(ones[:, :], chosen[:, 0, :]), (before, chosen[:, 1, :])])
            product(bank[2][:, 2 * NE:3 * NE], [(ones[:, :], chosen[:, 0, :]), (ones[:, :], chosen[:, 1, :])])\
                .then_inc(s["rankmm"], 1)
            pe.wait_ge(s["count_sb"], 1)
            pe.wait_ge(s["ntok_sb"], 4)

            def gather(e, k, to):
                pe.wait_ge(s["selmade"], e + 1)
                for d in range(KT):
                    last = product(to[d // 4][:, (d % 4) * P:(d % 4 + 1) * P],
                                   [(ntok[:, b, d * P:(d + 1) * P], sel[:, b, k * P:(k + 1) * P]) for b in range(TB)])
                last.then_inc(s[f"gather{k}"], 1)

            def turn_gates(e, nb):
                pe.wait_ge(s[f"xg_lo{nb - 1}"], e + 1)
                for k in range(nb):
                    for b in range(TB):
                        last = tr(bank[3][:, k * T + b * P:k * T + (b + 1) * P], selg[:, b, k * P:(k + 1) * P], ident)
                last.then_inc(s["selT"], 1)

            def split_products(out, pairs, first, final):
                n = 3 * len(pairs)
                for i, ((xh, xl), (wh, wl)) in enumerate(pairs):
                    for j, (x_, w_) in enumerate(((xh, wh), (xh, wl), (xl, wh))):
                        at = 3 * i + j
                        last = mm(out, x_, w_, start=(first and at == 0), stop=(final and at == n - 1),
                                  skip_group_check=True)
                return last

            def gate_up(e, nb, c, u):
                n = 2 * width(c)
                pe.wait_ge(s["lo_" + UNITS[u]], e * CHUNKS + c + 1 + LEAD)
                if u == 0 and c > 2 - nb:
                    pe.wait_ge(s["e_hid"], e * CHUNKS + (c - 1 if nb == 1 else c))
                for k in range(nb):
                    o = bank[c % 2 if nb == 1 else k][:, 0:n]
                    xs = [(xg_hi[:, 4 * u + i, k * P:(k + 1) * P], xg_lo[:, 4 * u + i, k * P:(k + 1) * P])
                          for i in range(4)]
                    ws = [(w_hi[:, u, i * n:(i + 1) * n], w_lo[:, u, i * n:(i + 1) * n]) for i in range(4)]
                    last = split_products(o, list(zip(xs, ws)), u == 0, u == 1)
                last.then_inc(s["gua" if u == 0 else "gub"], 1)

            def start(e, nb, prior):
                pe.wait_ge(s["xg_lo0"], e + 1)
                if nb == 2:
                    if prior:
                        pe.wait_ge(s["selT_sb"], e)
                    gather(e, 1, bank[2:4])
                    pe.wait_ge(s["xg_lo1"], e + 1)
                else:
                    pe.sem_inc(s["gather1"], 1)
                gate_up(e, nb, 0, 0)
                gate_up(e, nb, 0, 1)

            def expert(e, nb):
                c0 = e * CHUNKS

                def turn_hidden(c):
                    pe.wait_ge(s["e_hid"], c0 + c + 1)
                    for f in range(width(c) // P):
                        for k in range(nb):
                            j = f * nb + k
                            last = tr(bank[2][:, j * P:(j + 1) * P], hidden[:, k, f * P:(f + 1) * P], ident)
                    last.then_inc(s["e_hT"], 1)

                def down(c):
                    if c == 0:
                        pe.wait_ge(s["moe_sum"], e + 2)
                        open_sums(2 * nb)
                    pe.wait_ge(s["lo_d"], c0 + c + 1 + LEAD)
                    pe.wait_ge(s["hT_lo_done"], c0 + c + 1)
                    for k in range(nb):
                        for half in range(2):
                            o = wide[:, k * D + half * 512:k * D + (half + 1) * 512]
                            at = [f * D + half * 512 for f in range(width(c) // P)]
                            last = split_products(o, [((hT_hi[:, f, k * P:(k + 1) * P], hT_lo[:, f, k * P:(k + 1) * P]),
                                                       (w_hi[:, 2, a:a + 512], w_lo[:, 2, a:a + 512]))
                                                      for f, a in enumerate(at)], False, False)
                    last.then_inc(s["e_down"], 1)

                for c in range(1, CHUNKS):
                    gate_up(e, nb, c, 0)
                    turn_hidden(c - 1)
                    gate_up(e, nb, c, 1)
                    down(c - 1)
                    if nb == 1 and c == CHUNKS - 2:
                        unless_last(pe, e, lambda: gather(e + 1, 0, upper[2:4]))
                turn_hidden(CHUNKS - 1)
                down(CHUNKS - 1)
                if nb == 2:
                    unless_last(pe, e, lambda: (pe.wait_ge(s["selT_sb"], e + 1),
                                                gather(e + 1, 0, bank[2:4])))

            def scatter(e, nb):
                pe.wait_ge(s["y_sb"], e + 1)
                for d in range(KT):
                    last = product(wide[:, d * T:(d + 1) * T],
                                   [(yslot[:, k, d * P:(d + 1) * P], selgT[:, k, :]) for k in range(nb)])
                last.then_inc(s["scatmm"], 1)

            open_sums(4).then_inc(s["scatmm"], 1)
            gather(0, 0, bank[2:4])
            by_blocks(pe, 0, lambda nb: start(0, nb, False))
            by_blocks(pe, 0, lambda nb: turn_gates(0, nb))
            with pe.Fori(0, NE) as e:
                by_blocks(pe, e, lambda nb: expert(e, nb))
                unless_last(pe, e, lambda: by_blocks(pe, e + 1, lambda nb: start(e + 1, nb, True)))
                by_blocks(pe, e, lambda nb: scatter(e, nb))
                unless_last(pe, e, lambda: by_blocks(pe, e + 1, lambda nb: turn_gates(e + 1, nb)))

            norm_stat(4)
            pe.wait_ge(s["scaled"], KT)
            for i in range(4):
                b, half = i // 2, i % 2
                for j in range(4):
                    last = tr(upper[i][:, j * P:(j + 1) * P], nT[:, 4 * half + j, b * P:(b + 1) * P], ident)
                last.then_inc(s["finT"], 1)

        @block.scalar
        def _(act):
            go = nc.scalar.activation
            act.dma_start(con[:, :], consts).then_inc(s["in_con"], 16)
            act.dma_start(xtok, x[0].rearrange("(b p) d -> p b d", p=P)).then_inc(s["in_x"], 16)
            act.dma_start(oh[0:BUCKETS, :, :], onehot.rearrange("b (g m) -> b g m", g=GROUPS)).then_inc(s["in_misc"], 16)
            act.dma_start(rmask[0:SLOTS, :, :], relmask.rearrange("b (g m) -> b g m", g=GROUPS)).then_inc(s["in_misc"], 16)
            act.dma_start(table[:, :], rpb_table).then_inc(s["in_misc"], 16)
            act.dma_start(wrout[:, :, :], w_router[0].rearrange("(k p) e -> p k e", p=P)).then_inc(s["in_misc"], 16)
            pos_all = bass.AP(positions.tensor, 0, [[0, ROPE], [1, T]])
            act.dma_start(posi[NOPE:QK, :], pos_all).then_inc(s["in_pos"], 16)

            act.wait_ge(s["vec_sb"], 1)
            go(cact[:, :], vec[:, V_C:V_C + KT], ACT.Silu).then_inc(s["c_ready"], 1)
            for d in range(0, KT, 2):
                act.wait_ge(s["xT"], d + 1)
                go(hT[:, d, :], upper[d % 4][:, 0:T], ACT.Copy).then_inc(s["x_act"], 1)

            act.wait_ge(s["trig_step"], 1)
            go(trig[NOPE:QK, :, :], ang[NOPE:QK, :, :], ACT.Sin).then_inc(s["trig_done"], 1)

            def squares(k, ready):
                for j in range(KT):
                    ready(j)
                    go(sqT[:, j, :], hT[:, j, :], ACT.Square).then_inc(s["sq"], 1)
                act.wait_ge(s["stat"], k + 1)
                go(std[:, 0, :], bank[2][:, 0:T], ACT.Sqrt, bias=eps[:, 0:1], scale=1.0 / D)\
                    .then_inc(s["std_ready"], 1)

            def shifts(m, b, dst):
                act.wait_ge(s["mod_ready"], b + 1)
                for j in range(KT):
                    act.wait_ge(s["norm_mul"], m * KT + j + 1)
                    go(dst[:, j, :], dst[:, j, :], ACT.Identity, bias=mod[:, b * KT + j:b * KT + j + 1])\
                        .then_inc(s["norm_ready"], 1)

            act.wait_ge(s["pool_const"], 5)

            def x_ready(j):
                act.wait_ge(*((s["x_act"], j // 2 + 1) if j % 2 == 0 else (s["x_dve"], j // 2 + 1)))
            squares(0, x_ready)
            shifts(0, SH_M, nT)

            act.wait_ge(s["stat"], 1)
            for i in range(6):
                act.wait_ge(s["latmm"], i + 1)
                if i < 5:
                    go(lat[:, i, :], upper[i % 4][:, 0:T], ACT.Copy).then_inc(s["lat_sb"], 1)
                    go(latsq[:, i, :], upper[i % 4][:, 0:T], ACT.Square).then_inc(s["latsq_done"], 1)
                else:
                    go(krot[NOPE:QK, 0, :], upper[1][NOPE:QK, 0:T], ACT.Copy).then_inc(s["lat_sb"], 1)
            act.wait_ge(s["latstat"], 1)
            go(std[:, 0, :], bank[2][:, 0:T], ACT.Sqrt, bias=eps[:, 0:1], scale=1.0 / QR).then_inc(s["latstd"], 1)
            act.wait_ge(s["latstat"], 2)
            go(std[:, 1, :], bank[1][:, 0:T], ACT.Sqrt, bias=eps[:, 0:1], scale=1.0 / KVR).then_inc(s["latstd"], 1)
            for h in range(HEADS):
                act.wait_ge(s["qmm"], h + 1)
                go(Q[0:QK, h, :], upper[h % 4][0:QK, 0:T], ACT.Copy).then_inc(s["q_sb"], 1)
            for h in range(HEADS):
                act.wait_ge(s["kmm"], h + 1)
                go(K[0:NOPE, h, :], upper[h % 4][0:NOPE, 0:T], ACT.Copy).then_inc(s["k_sb"], 1)
            for i in range(4):
                act.wait_ge(s["vmm"], i + 1)
                go(V[:, i // 2, (i % 2) * 512:(i % 2 + 1) * 512], upper[i], ACT.Copy).then_inc(s["v_sb"], 1)
            for h in range(HEADS):
                for b in range(TB):
                    act.wait_ge(s["masked"], 2 * h + b + 1)
                    pr = prob[:, h % 2, 0:P] if b == 0 else prob[:, h % 2, P:3 * P]
                    go(pr, pr, ACT.Exp, bias=nmax[:, b, h:h + 1], scale=-1.0,
                       accum_out=rsum[:, b, h:h + 1]).then_inc(s["expd"], 1)
            for d in range(KT):
                act.wait_ge(s["oT"], d + 1)
                go(nT[:, d, :], bank[d % 2][:, 0:T], ACT.Copy).then_inc(s["oT_sb"], 1)

            def h_ready(base):
                return lambda j: act.wait_ge(s["h_ready"], base + j + 1)
            squares(1, h_ready(0))
            shifts(1, SH_F, nT)

            def gates(j, n, job):
                act.wait_ge(s["gumm"], job + j + 1)
                if isinstance(job, int) and job + j < 2:
                    pass
                else:
                    act.wait_ge(s["hid_ready"], job + j - 1)
                go(sg[:, j % 2, 0:n], bank[j % 2][:, 0:n], ACT.Silu).then_inc(s["silu_done"], 1)

            for half in range(2):
                for j in range(JT):
                    gates(j, T, half * JT)
            squares(2, h_ready(KT))
            shifts(2, KV_SH, nT)
            shifts(3, L1 + SH_M, n2T)
            for i in range(24):
                act.wait_ge(s["kvmm"], i + 1)
                m, r = divmod(i, 2)
                g, q = divmod(m, 4)
                dst = Kd[:, 4 * g + 2 * q + r, :] if q < 2 else Vd[:, r, g * DQ + (q - 2) * T:g * DQ + (q - 1) * T]
                go(dst, upper[i % 4][:, 0:T], ACT.Copy).then_inc(s["kv_sb"], 1)
            for i in range(12):
                act.wait_ge(s["qdmm"], i + 1)
                go(Qd[:, i, :], upper[i % 4][:, 0:T], ACT.Copy).then_inc(s["qd_sb"], 1)
            for u in range(2 * SLOTS):
                h, b = divmod(u, 2)
                act.wait_ge(s["dmask"], u + 1)
                pr = pd[:, 0:3 * P] if b == 0 else pd[:, 3 * P:9 * P]
                go(pr, pr, ACT.Exp, bias=nmax[:, b, h:h + 1], scale=-1.0,
                   accum_out=rsum[:, b, h:h + 1]).then_inc(s["dexp"], 1)
            for d in range(4):
                act.wait_ge(s["odT"], d + 1)
                go(nT[:, d, :], bank[d % 2][:, 0:T], ACT.Copy).then_inc(s["odT_sb"], 1)
            squares(3, h_ready(2 * KT))
            shifts(4, L1 + SH_F, nT)
            act.wait_ge(s["logit"], 1)
            act.wait_ge(s["dexp"], 2 * SLOTS)
            for i in range(4):
                act.wait_ge(s["ntokT"], i + 1)
                go(ntok[:, i // 2, (i % 2) * 512:(i % 2 + 1) * 512], upper[i], ACT.Copy).then_inc(s["ntok_sb"], 1)
            act.wait_ge(s["routed_gap"], 1)
            go(small[:, 8, :, 0:1], small[:, 8, :, 1:2], ACT.Exp).then_inc(s["gap_exp"], 1)
            act.wait_ge(s["count_sb"], 1)

            def columns_hi(e, k, src):
                act.wait_ge(s[f"gather{k}"], e + 1)
                for i in range(2):
                    ins = go(xg_hi[:, 4 * i:4 * i + 4, k * P:(k + 1) * P],
                             src[i].rearrange("p (d n) -> p d n", n=P), ACT.Copy)
                ins.then_inc(s[f"xg_hi{k}"], 1)

            def second_block(e, nb):
                if nb == 2:
                    columns_hi(e, 1, bank23)
                else:
                    act.sem_inc(s["xg_hi1"], 1)

            def weight_hi(e, c, u):
                t = T_MOE + 3 * c + u
                act.wait_ge(landed[t % RING], landings(e, c, u))
                if c:
                    act.wait_ge(s[("gua", "gub", "e_down")[u]], e * CHUNKS + c)
                n = unit_size(c, u)
                go(w_hi[:, u, 0:n], slot(t)[:, 0:n], ACT.Copy).then_inc(s["hi_" + UNITS[u]], 1)

            def expert(e, nb):
                c0 = e * CHUNKS

                def silu(c):
                    w = width(c)
                    act.wait_ge(s["gub"], c0 + c + 1)
                    if c:
                        act.wait_ge(s["e_hid"], c0 + c)
                    for k in range(nb):
                        ins = go(gate_act[:, k, 0:w], bank[c % 2 if nb == 1 else k][:, 0:w], ACT.Silu)
                    ins.then_inc(s["e_silu"], 1)

                def hidden_hi(c):
                    nf = width(c) // P
                    act.wait_ge(s["e_hT"], c0 + c + 1)
                    go(hT_hi[:, 0:nf, 0:nb * P], bank[2][:, 0:nf * nb * P].rearrange("p (f n) -> p f n", f=nf), ACT.Copy)\
                        .then_inc(s["hT_hi_done"], 1)

                def results():
                    act.wait_ge(s["e_down"], c0 + CHUNKS)
                    go(yslot[:, 0:nb, :], wide[:, 0:nb * D].rearrange("p (k d) -> p k d", d=D), ACT.Copy)\
                        .then_inc(s["y_sb"], 1)

                for c in range(1, CHUNKS):
                    weight_hi(e, c, 0)
                    silu(c - 1)
                    weight_hi(e, c, 1)
                    if c == 1:
                        act.wait_ge(s["selT"], e + 1)
                        go(selgT[:, 0:nb, :], bank[3][:, 0:nb * T].rearrange("p (k t) -> p k t", t=T), ACT.Copy)\
                            .then_inc(s["selT_sb"], 1)
                    weight_hi(e, c - 1, 2)
                    hidden_hi(c - 1)

                def last_chunk_and_next():
                    weight_hi(e, CHUNKS, 0)
                    silu(CHUNKS - 1)
                    if nb == 1:
                        act.wait_ge(s["gub"], c0 + CHUNKS)
                        columns_hi(e + 1, 0, free23)
                    weight_hi(e, CHUNKS, 1)
                    weight_hi(e, CHUNKS - 1, 2)
                    hidden_hi(CHUNKS - 1)
                    results()
                    if nb == 2:
                        columns_hi(e + 1, 0, bank23)

                def last_chunk():
                    silu(CHUNKS - 1)
                    weight_hi(e, CHUNKS - 1, 2)
                    hidden_hi(CHUNKS - 1)
                    results()

                with act.If(e < NE - 1):
                    last_chunk_and_next()
                with act.Else():
                    last_chunk()

            bank23 = (bank[2][:, :], bank[3][:, :])
            free23 = (upper[2], upper[3])
            weight_hi(0, 0, 0)
            weight_hi(0, 0, 1)
            columns_hi(0, 0, bank23)
            by_blocks(act, 0, lambda nb: second_block(0, nb))
            with act.Fori(0, NE) as e:
                by_blocks(act, e, lambda nb: expert(e, nb))
                unless_last(act, e, lambda: by_blocks(act, e + 1, lambda nb: second_block(e + 1, nb)))
            squares(4, h_ready(3 * KT))
            for i in range(0, 4, 2):
                act.wait_ge(s["finT"], i + 1)
                go(otok[:, i // 2, 0:512], upper[i], ACT.Copy).then_inc(s["fin_act"], 1)

        @block.vector
        def _(dve):
            v = nc.vector
            own = [0]

            def link(ins):
                own[0] += 1
                ins.then_inc(s["dve_own"], 1)
                dve.wait_ge(s["dve_own"], own[0])

            def ada_strip(b, k, dyn=0):
                n = KT * b + k
                m = n % ADAS
                turn = n // ADAS + 1
                dve.wait_ge(strip_in[m], dyn * (16 * KT // ADAS) + 16 * turn)
                if k == 0:
                    if b >= 2:
                        dve.wait_ge(s["ada_reduced"], dyn + b - 1)
                    v.tensor_scalar(adasum[:, b % 2, :], strip[:, m, :], cact[:, 0:1], None, ALU.mult)\
                        .then_inc(s["ada_step"], 1)
                else:
                    dve.wait_ge(s["ada_step"], dyn * KT + n)
                    v.scalar_tensor_tensor(out=adasum[:, b % 2, :], in0=strip[:, m, :], scalar=cact[:, k:k + 1],
                                           in1=adasum[:, b % 2, :], op0=ALU.mult, op1=ALU.add)\
                        .then_inc(s["ada_step"], 1)

            def ada(b):
                for k in range(KT):
                    ada_strip(b, k)

            def mod_out(b):
                dve.wait_ge(s["ada_reduced"], b + 1)
                v.tensor_tensor(mod[:, b * KT:(b + 1) * KT], bank[3][:, b * KT:(b + 1) * KT],
                                bcol[:, b * KT:(b + 1) * KT], ALU.add).then_inc(s["mod_ready"], 1)

            def scale_of(m, b, g):
                dve.wait_ge(s["mod_ready"], b + 1)
                link(v.scalar_tensor_tensor(out=ascale[:, m, :], in0=mod[:, b * KT:(b + 1) * KT], scalar=1.0,
                                            in1=vec[:, g:g + KT], op0=ALU.add, op1=ALU.mult))

            def norm(m, dst):
                for j in range(KT):
                    v.scalar_tensor_tensor(out=dst[:, j, :], in0=hT[:, j, :], scalar=ascale[:, m, j:j + 1],
                                           in1=rstd[:, 0, :], op0=ALU.mult, op1=ALU.mult)\
                        .then_inc(s["norm_mul"], 1)

            def inverse(k):
                dve.wait_ge(s["std_ready"], k + 1)
                link(v.reciprocal(rstd[:, 0, :], std[:, 0, :]))

            def residual(j, src, b):
                v.scalar_tensor_tensor(out=hT[:, j, :], in0=src, scalar=mod[:, b * KT + j:b * KT + j + 1],
                                       in1=hT[:, j, :], op0=ALU.mult, op1=ALU.add).then_inc(s["h_ready"], 1)

            dve.wait_ge(s["vecT"], 1)
            v.tensor_copy(vec[:, :], bank[0][:, 0:NVEC]).then_inc(s["vec_sb"], 1)
            dve.wait_ge(s["vecT"], 2)
            v.tensor_copy(bcol[:, :], bank[1][:, 0:BLOCKS * KT]).then_inc(s["vec_sb"], 1)
            for d in range(1, KT, 2):
                dve.wait_ge(s["xT"], d + 1)
                v.tensor_copy(hT[:, d, :], upper[d % 4][:, 0:T]).then_inc(s["x_dve"], 1)
            dve.wait_ge(s["in_misc"], 64)
            for g in range(GROUPS):
                dve.wait_ge(s["relmm"], g + 1)
                v.scalar_tensor_tensor(out=relb[0:SLOTS, g, :], in0=bank[g][0:SLOTS, 0:NREL], scalar=HD ** 0.5,
                                       in1=rmask[0:SLOTS, g, :], op0=ALU.mult, op1=ALU.add)\
                    .then_inc(s["rel_ready"], 1)
            R = slice(NOPE, QK)
            dve.wait_ge(s["in_pos"], 16)
            dve.wait_ge(s["in_con"], 16)
            link(v.tensor_copy(ang[R, 1, :], posi[R, :]))
            link(v.tensor_scalar(ang[R, 0, :], ang[R, 1, :], freq, None, ALU.mult))
            link(v.tensor_scalar(turns[R, 0, :], ang[R, 0, :], 0.15915494309189535, 0.25, ALU.mult, ALU.add))
            link(v.tensor_scalar(turns[R, 1, :], ang[R, 0, :], 0.15915494309189535, None, ALU.mult))
            link(v.tensor_copy(ang[R, 1, :], ang[R, 0, :]))
            link(v.tensor_scalar(turns[R, :, :], turns[R, :, :], ROUND, None, ALU.add))
            link(v.tensor_scalar(turns[R, :, :], turns[R, :, :], ROUND, None, ALU.subtract))
            two_pi_lo = 6.283185307179586 - TWO_PI_HI - TWO_PI_MID
            for part in (TWO_PI_HI, TWO_PI_MID, two_pi_lo):
                link(v.scalar_tensor_tensor(out=ang[R, :, :], in0=turns[R, :, :], scalar=-part, in1=ang[R, :, :],
                                            op0=ALU.mult, op1=ALU.add))
            link(v.tensor_scalar(ang[R, 0, :], ang[R, 0, :], 1.5707963267948966, None, ALU.add))
            v.tensor_scalar(ang[R, :, :], ang[R, :, :], 3.1415925, -3.1415925, ALU.min, ALU.max)\
                .then_inc(s["trig_step"], 1)

            dve.wait_ge(s["c_ready"], 1)
            ada(0)
            ada(1)
            mod_out(0)
            mod_out(1)
            scale_of(0, SC_M, V_MIX)
            inverse(0)
            norm(0, nT)

            for i, (a, n, g) in enumerate(((0, QRT, V_LQ), (QRT, KVT, V_LKV))):
                dve.wait_ge(s["latstd"], i + 1)
                dve.wait_ge(s["lat_sb"], 5)
                link(v.reciprocal(rstd[:, i, :], std[:, i, :]))
                if i == 0:
                    dve.wait_ge(s["trig_done"], 1)
                for j in range(n):
                    v.scalar_tensor_tensor(out=latn[:, a + j, :], in0=lat[:, a + j, :], scalar=vec[:, g + j:g + j + 1],
                                           in1=rstd[:, i, :], op0=ALU.mult, op1=ALU.mult)\
                        .then_inc(s["latn_ready"], 1)
            cos, sin = trig[R, 0:1, :], trig[R, 1:2, :]
            dve.wait_ge(s["krmm"], 1)
            dve.wait_ge(s["lat_sb"], 6)
            link(v.tensor_tensor(rt[R, 0, 0:T], bank[0][R, 0:T], trig[R, 1, :], ALU.mult))
            link(v.tensor_tensor(rt[R, 1, 0:T], krot[R, 0, :], trig[R, 0, :], ALU.mult))
            v.tensor_tensor(krot[R, 1, :], rt[R, 0, 0:T], rt[R, 1, 0:T], ALU.add).then_inc(s["k_rot"], 1)
            ada(2)
            ada(3)
            dve.wait_ge(s["k_rot"], 1)
            for p in range(HEADS // 2):
                two = [ROPE, 2, T]
                dve.wait_ge(s["ropemm"], p + 1)
                q2 = Q[R, 2 * p:2 * p + 2, :]
                r0 = rt[R, 0, :].rearrange("p (a t) -> p a t", t=T)
                r1 = rt[R, 1, :].rearrange("p (a t) -> p a t", t=T)
                if p:
                    dve.wait_ge(s["rope_done"], p)
                v.tensor_tensor(r0, bank[p % 2][R, :].rearrange("p (a t) -> p a t", t=T), sin.broadcast_to(two),
                                ALU.mult).then_inc(s["rope_mul"], 1)
                dve.wait_ge(s["rope_mul"], p + 1)
                link(v.tensor_tensor(r1, q2, cos.broadcast_to(two), ALU.mult))
                v.tensor_tensor(q2, r0, r1, ALU.add).then_inc(s["rope_done"], 1)
            mod_out(2)
            mod_out(3)

            scale = QK ** -0.5
            dve.wait_ge(s["v_sb"], 4)

            def divide(parts, heads, o, sums, rn):
                for b, src in enumerate(parts):
                    v.tensor_tensor(o[:, b, :].rearrange("p (h c) -> p h c", c=HD),
                                    src.rearrange("p (h c) -> p h c", c=HD),
                                    rn[:, b, heads].unsqueeze(2).broadcast_to([P, 8, HD]), ALU.mult).then_inc(sums, 1)

            for h in range(HEADS + 1):
                if h < HEADS:
                    dve.wait_ge(s["mscore"], h + 1)
                    if h >= 2:
                        dve.wait_ge(s["mprobT"], h - 1)
                    k = bank[h % 2]
                    pr = prob[:, h % 2, :]
                    v.tensor_tensor_reduce(out=pr[:, 0:P], in0=k[:, 0:P], in1=causal, scale=-scale, scalar=HUGE,
                                           op0=ALU.add, op1=ALU.min, accum_out=nmax[:, 0, h:h + 1])\
                        .then_inc(s["masked"], 1)
                    v.tensor_tensor_reduce(out=pr[:, P:3 * P], in0=k[:, P:3 * P], in1=con[:, C_OPEN:C_OPEN + 2 * P],
                                           scale=-scale, scalar=HUGE, op0=ALU.add, op1=ALU.min,
                                           accum_out=nmax[:, 1, h:h + 1]).then_inc(s["masked"], 1)
                if h >= 1:
                    g = h - 1
                    dve.wait_ge(s["mprobT"], g + 1)
                    if g >= 2:
                        dve.wait_ge(s["mpv"], g - 1)
                    v.tensor_copy(probT[:, g % 2, :], bank[2 + g % 2][:, 0:3 * P]).then_inc(s["mprobT_sb"], 1)
                if h in (9, HEADS):
                    a = 0 if h == 9 else 8
                    if h == HEADS:
                        dve.wait_ge(s["mpv"], HEADS)
                    dve.wait_ge(s["mpv"], a + 8 if h == HEADS else 8)
                    dve.wait_ge(s["expd"], 2 * (a + 8))
                    link(v.reciprocal(rinv[:, :, a:a + 8], rsum[:, :, a:a + 8]))
                    divide([upper[2 * (a // 8)], upper[2 * (a // 8) + 1]], slice(a, a + 8),
                           O[:, :, a * VD:(a + 8) * VD], s["o_norm"], rinv)
            for d in range(KT):
                dve.wait_ge(s["omm"], d + 1)
                residual(d, upper[d % 4][:, 0:T], GT_M)
                ada_strip(4 + d // 4, 2 * (d % 4))
                ada_strip(4 + d // 4, 2 * (d % 4) + 1)
            mod_out(4)
            mod_out(5)
            scale_of(1, SC_F, V_FFN)
            inverse(1)
            norm(1, nT)

            def gated(j, n, job):
                dve.wait_ge(s["silu_done"], job + j + 1)
                if not (isinstance(job, int) and job + j < 2):
                    dve.wait_ge(s["downmm"], job + j - 1)
                v.tensor_tensor(hid[:, j % 2, 0:n], bank[j % 2][:, T:T + n], sg[:, j % 2, 0:n], ALU.mult)\
                    .then_inc(s["hid_ready"], 1)

            for half in range(2):
                done = 0
                for j in range(JT):
                    gated(j, T, half * JT)
                    for i in range(3 if j < JT - 1 else 2):
                        ada_strip(6 + 4 * half + done // KT, done % KT)
                        done += 1
                    if j in (4, 7, 9):
                        i = (4, 7, 9).index(j)
                        b = 6 + 4 * half + i
                        dve.wait_ge(s["ada_reduced"], b + 1)
                        v.tensor_tensor(mod[:, b * KT:(b + 1) * KT], bank[3][:, i * KT:(i + 1) * KT],
                                        bcol[:, b * KT:(b + 1) * KT], ALU.add).then_inc(s["mod_ready"], 1)
                b = 9 + 4 * half
                dve.wait_ge(s["ada_reduced"], b + 1)
                v.tensor_tensor(mod[:, b * KT:(b + 1) * KT], bank[3][:, 3 * KT:4 * KT],
                                bcol[:, b * KT:(b + 1) * KT], ALU.add).then_inc(s["mod_ready"], 1)
            dve.wait_ge(s["downmm"], 2 * JT)
            for d in range(KT):
                residual(d, wide[:, d * T:(d + 1) * T], GT_F)
            scale_of(2, KV_SC, V_KV)
            scale_of(3, L1 + SC_M, V_MIX + KT)
            scale_of(4, L1 + SC_F, V_FFN + KT)
            inverse(2)
            norm(2, nT)
            norm(3, n2T)

            for u in range(2 * SLOTS + 1):
                if u < 2 * SLOTS:
                    h, b = divmod(u, 2)
                    dve.wait_ge(s["dscore"], u + 1)
                    if b == 0:
                        dve.wait_ge(rel_in[h % 2], 16 * (h // 2 + 1))
                    if h >= 1:
                        dve.wait_ge(s["dprobT"], 3 * (h - 1) + (1 if b == 0 else 3))
                    n = (b + 1) * P
                    if b == 0:
                        src, dst = bank[0][:, 0:3 * P], pd[:, 0:3 * P]
                        parts = [(src.rearrange("p (g n) -> p g n", n=n), dst.rearrange("p (g n) -> p g n", n=n),
                                  relT[:, h % 2, :, P:2 * P])]
                    else:
                        parts = []
                        parts.append((bank[1][:, :].rearrange("p (g n) -> p g n", n=n),
                                      pd[:, 3 * P:7 * P].rearrange("p (g n) -> p g n", n=n), relT[:, h % 2, 0:2, :]))
                        parts.append((bank[2][:, 0:T], pd[:, 7 * P:9 * P], relT[:, h % 2, 2, :]))
                    for i, (a, o, bias) in enumerate(parts):
                        start = HUGE if i == 0 else npart[:, h:h + 1]
                        acc = nmax[:, b, h:h + 1] if i == len(parts) - 1 else npart[:, h:h + 1]
                        ins = v.tensor_tensor_reduce(out=o, in0=a, in1=bias, scale=-HD ** -0.5, scalar=start,
                                                     op0=ALU.add, op1=ALU.min, accum_out=acc)
                        if i < len(parts) - 1:
                            link(ins)
                    ins.then_inc(s["dmask"], 1)
                for q in {0: (), 1: (0,)}.get(u, ((3 * (u // 2) - 2, 3 * (u // 2) - 1) if u % 2 == 0
                                                  else (3 * (u // 2),))):
                    dve.wait_ge(s["dprobT"], q + 1)
                    if q >= 2:
                        dve.wait_ge(s["dpv"], q - 1)
                    v.tensor_copy(pdT[:, q % 2, :], (bank[3] if q % 2 == 0 else upper[0])[:, 0:3 * P])\
                        .then_inc(s["dprobT_sb"], 1)
            dve.wait_ge(s["dpv"], 3 * SLOTS)
            dve.wait_ge(s["dexp"], 2 * SLOTS)
            link(v.reciprocal(rinv[:, :, 0:SLOTS], rsum[:, :, 0:SLOTS]))
            divide([upper[1], upper[2]], slice(0, SLOTS), Od, s["od_norm"], rinv)
            for d in range(KT):
                dve.wait_ge(s["odmm"], d + 1)
                residual(d, upper[d % 4][:, 0:T], L1 + GT_M)
            inverse(3)
            norm(4, nT)

            dve.wait_ge(s["logit"], 1)
            sm = [small[:, i, :, 0:NE] for i in range(12)]
            chosen, gate, lg, first, second, rest, eq, tmp = sm[:8]
            one = [P, TB, NE]
            link(v.tensor_copy(lg, bank[3][:, 0:TB * NE].rearrange("p (b e) -> p b e", e=NE)))
            down_count = con[:, C_IOTA + 1:C_IOTA + 1 + NE]
            for vals, hot, best in ((lg, first, sm[9][:, :, 0:1]), (rest, second, sm[9][:, :, 1:2])):
                link(v.tensor_reduce(best, vals, AX_X, ALU.max))
                link(v.tensor_tensor(eq, vals, best.broadcast_to(one), ALU.is_equal))
                for b in range(TB):
                    link(v.scalar_tensor_tensor(out=tmp[:, b, :], in0=down_count, scalar=-9.0, in1=eq[:, b, :],
                                                op0=ALU.add, op1=ALU.mult))
                link(v.tensor_reduce(sm[9][:, :, 2:3], tmp, AX_X, ALU.min))
                link(v.tensor_tensor(hot, tmp, sm[9][:, :, 2:3].broadcast_to(one), ALU.is_equal))
                if hot is first:
                    link(v.scalar_tensor_tensor(out=rest, in0=first, scalar=-HUGE, in1=lg, op0=ALU.mult, op1=ALU.add))
            v.tensor_tensor(chosen, first, second, ALU.add).then_inc(s["routed"], 1)
            v.tensor_tensor(sm[8][:, :, 1:2], sm[9][:, :, 1:2], sm[9][:, :, 0:1], ALU.subtract)\
                .then_inc(s["routed_gap"], 1)
            dve.wait_ge(s["gap_exp"], 1)
            link(v.tensor_scalar(sm[9][:, :, 3:4], sm[8][:, :, 0:1], 1.0, None, ALU.add))
            link(v.reciprocal(sm[9][:, :, 4:5], sm[9][:, :, 3:4]))
            link(v.tensor_tensor(sm[9][:, :, 5:6], sm[9][:, :, 4:5], sm[8][:, :, 0:1], ALU.mult))
            link(v.tensor_tensor(gate, first, sm[9][:, :, 4:5].broadcast_to(one), ALU.mult))
            link(v.tensor_tensor(tmp, second, sm[9][:, :, 5:6].broadcast_to(one), ALU.mult))
            link(v.tensor_tensor(gate, gate, tmp, ALU.add))
            dve.wait_ge(s["rankmm"], 1)
            rank = sm[10]
            link(v.tensor_copy(rank, bank[2][:, 0:TB * NE].rearrange("p (b e) -> p b e", e=NE)))
            v.tensor_copy(counts[:, 0:NE], bank[2][0:1, 2 * NE:3 * NE]).then_inc(s["count_sb"], 1)
            dve.wait_ge(s["count_sb"], 1)

            def select_tokens(e):
                for b in range(TB):
                    r = small[:, 10, b, bass.ds(e, 1)]
                    v.tensor_scalar(sel[:, b, :], iota, r, small[:, 0, b, bass.ds(e, 1)], ALU.is_equal, ALU.mult)
                    ins = v.tensor_scalar(selg[:, b, :], iota, r, small[:, 1, b, bass.ds(e, 1)], ALU.is_equal, ALU.mult)
                ins.then_inc(s["selmade"], 1)

            def columns_lo(e, k, src):
                dve.wait_ge(s[f"xg_hi{k}"], e + 1)
                for i in range(2):
                    at = (slice(None), slice(4 * i, 4 * i + 4), slice(k * P, (k + 1) * P))
                    ins = v.tensor_tensor(xg_lo[at], src[i].rearrange("p (d n) -> p d n", n=P),
                                          xg_hi[at].bitcast(F32), ALU.subtract)
                ins.then_inc(s[f"xg_lo{k}"], 1)

            def second_block(e, nb):
                if nb == 2:
                    columns_lo(e, 1, bank23)
                else:
                    dve.sem_inc(s["xg_lo1"], 1)

            def add_results(e):
                dve.wait_ge(s["scatmm"], e + 1)
                for i in range(4):
                    m = moe[:, 2 * i:2 * i + 2, :]
                    ins = v.tensor_tensor(m, upper[i].rearrange("p (a t) -> p a t", t=T), m, ALU.add)
                ins.then_inc(s["moe_sum"], 1)

            def weight_lo(e, c, u):
                n = unit_size(c, u)
                dve.wait_ge(s["hi_" + UNITS[u]], e * CHUNKS + c + 1)
                v.tensor_tensor(w_lo[:, u, 0:n], slot(T_MOE + 3 * c + u)[:, 0:n], w_hi[:, u, 0:n].bitcast(F32),
                                ALU.subtract).then_inc(s["lo_" + UNITS[u]], 1)

            def expert(e, nb):
                c0 = e * CHUNKS

                def gated_hidden(c):
                    w = width(c)
                    dve.wait_ge(s["e_silu"], c0 + c + 1)
                    if c:
                        dve.wait_ge(s["e_hT"], c0 + c)
                    for k in range(nb):
                        ins = v.tensor_tensor(hidden[:, k, 0:w], bank[c % 2 if nb == 1 else k][:, w:2 * w],
                                              gate_act[:, k, 0:w], ALU.mult)
                    ins.then_inc(s["e_hid"], 1)

                def hidden_lo(c):
                    nf = width(c) // P
                    dve.wait_ge(s["hT_hi_done"], c0 + c + 1)
                    v.tensor_tensor(hT_lo[:, 0:nf, 0:nb * P], bank[2][:, 0:nf * nb * P].rearrange("p (f n) -> p f n", f=nf),
                                    hT_hi[:, 0:nf, 0:nb * P].bitcast(F32), ALU.subtract).then_inc(s["hT_lo_done"], 1)

                for c in range(1, CHUNKS):
                    weight_lo(e, c, 0)
                    gated_hidden(c - 1)
                    weight_lo(e, c, 1)
                    if c == 1:
                        add_results(e)
                    weight_lo(e, c - 1, 2)
                    hidden_lo(c - 1)
                    if c == CHUNKS // 2:
                        unless_last(dve, e, lambda: (dve.wait_ge(s["selT"], e + 1), select_tokens(e + 1)))

                def last_chunk_and_next():
                    weight_lo(e, CHUNKS, 0)
                    gated_hidden(CHUNKS - 1)
                    if nb == 1:
                        columns_lo(e + 1, 0, free23)
                    weight_lo(e, CHUNKS - 1, 2)
                    hidden_lo(CHUNKS - 1)
                    weight_lo(e, CHUNKS, 1)
                    if nb == 2:
                        columns_lo(e + 1, 0, bank23)

                def last_chunk():
                    gated_hidden(CHUNKS - 1)
                    weight_lo(e, CHUNKS - 1, 2)
                    hidden_lo(CHUNKS - 1)

                with dve.If(e < NE - 1):
                    last_chunk_and_next()
                with dve.Else():
                    last_chunk()

            bank23 = (bank[2][:, :], bank[3][:, :])
            free23 = (upper[2], upper[3])
            dve.wait_ge(s["moe_sum"], 1)
            select_tokens(0)
            weight_lo(0, 0, 0)
            weight_lo(0, 0, 1)
            columns_lo(0, 0, bank23)
            by_blocks(dve, 0, lambda nb: second_block(0, nb))
            with dve.Fori(0, NE) as e:
                by_blocks(dve, e, lambda nb: expert(e, nb))
                unless_last(dve, e, lambda: by_blocks(dve, e + 1, lambda nb: second_block(e + 1, nb)))
            add_results(NE)
            dve.wait_ge(s["moe_sum"], NE + 2)
            for d in range(KT):
                residual(d, moe[:, d, :], L1 + GT_F)
            inverse(4)
            for j in range(KT):
                v.scalar_tensor_tensor(out=nT[:, j, :], in0=hT[:, j, :], scalar=vec[:, V_FINAL + j:V_FINAL + j + 1],
                                       in1=rstd[:, 0, :], op0=ALU.mult, op1=ALU.mult).then_inc(s["scaled"], 1)
            for i in range(1, 4, 2):
                dve.wait_ge(s["finT"], i + 1)
                v.tensor_copy(otok[:, i // 2, 512:D], upper[i]).then_inc(s["fin_dve"], 1)


def constants():
    import numpy as np
    con = np.zeros((P, NCONST), np.float32)
    con[:, C_ID:C_ID + P] = np.eye(P)
    i = np.arange(ROPE // 2)
    con[NOPE + ROPE // 2 + i, C_PERM + i] = -1.0
    con[NOPE + i, C_PERM + ROPE // 2 + i] = 1.0
    q, k = np.arange(P)[:, None], np.arange(P)[None, :]
    con[:, C_CAUSAL:C_CAUSAL + P] = np.where(k <= q, 0.0, -BIG)
    con[:, C_BEFORE:C_BEFORE + P] = q < k
    con[:, C_IOTA:C_IOTA + T] = np.arange(T)
    freq = np.float32(10000.0) ** (-np.arange(0, ROPE, 2, dtype=np.float32) / np.float32(ROPE))
    con[NOPE:QK, C_FREQ] = np.concatenate([freq, freq])
    onehot = np.zeros((BUCKETS, GROUPS, NREL), np.float32)
    relmask = np.zeros((SLOTS, GROUPS, NREL), np.float32)
    exact = BUCKETS // 2
    for g, (dil, span) in enumerate(zip(DILATIONS, SPANS)):
        for m in range(NREL):
            d = T - 1 - m
            if d < 0 or d % dil or d // dil > span:
                relmask[:, g, m] = -BIG
                continue
            big = exact + int(np.log(np.float32(max(d, 1)) / np.float32(exact)) / np.float32(np.log(2048 / exact))
                              * np.float32(BUCKETS - exact))
            onehot[d if d < exact else min(big, BUCKETS - 1), g, m] = 1.0
    return con, onehot.reshape(BUCKETS, -1), relmask.reshape(SLOTS, -1)


_INS = ['x', 'c', 'positions', 'g_mix', 'g_ffn', 'w_ada', 'b_ada', 'w_mla_in', 'g_mla_q', 'w_mla_q_up', 'g_mla_kv',
        'w_mla_kv_up', 'w_mla_out', 'g_kv_b', 'w_ada_kv', 'b_ada_kv', 'w_kv_b', 'rpb_table', 'w_q_b', 'w_o_b',
        'w_ffn_gu', 'w_ffn_down', 'w_router', 'w_exp_gu', 'w_exp_down', 'g_final']


def kernel(**inputs):
    import numpy as _np
    import concourse.bacc as _bacc
    from concourse import mybir as _mybir
    from concourse.bass_utils import run_bass_kernel_spmd as _run

    nc = _bacc.Bacc("TRN2", target_bir_lowering=False, num_devices=1)
    arrays, args = {}, []
    given = [(name, _np.ascontiguousarray(inputs[name])) for name in _INS]
    given += list(zip(("consts", "onehot", "relmask"), constants()))
    for name, a in given:
        arrays[f"in_{name}"] = a
        args.append(nc.dram_tensor(f"in_{name}", a.shape, _mybir.dt.from_np(a.dtype), kind="ExternalInput").ap())
    args.append(nc.dram_tensor("out_0", (1, T, D), _mybir.dt.float32, kind="ExternalOutput").ap())
    trunk(nc, *args)
    r = _run(nc, [arrays], core_ids=[0])
    return r.results[0]["out_0"]
```

```python
from contextlib import ExitStack

import concourse.bass as bass
from concourse import mybir

F32 = mybir.dt.float32
F32R = mybir.dt.float32r
BF16 = mybir.dt.bfloat16
I32 = mybir.dt.int32
ALU = mybir.AluOpType
ACT = mybir.ActivationFunctionType
AX_X = mybir.AxisListType.X

P = 128
D = 1024
T = 256
TB = T // P
KT = D // P
FF = 2816
HALF = FF // 2
JT = HALF // P
NCH = (JT + 1) // 2
NE = 8
HEADS = 16
NOPE, ROPE, VD = 64, 32, 64
QK = NOPE + ROPE
QR, KVR = 384, 256
QRT, KVT = QR // P, KVR // P
GROUPS, SLOTS, HD = 3, 8, 64
DILATIONS = (1, 4, 16)
SPANS = (128, 128, 128)
BUCKETS = 32
DQ = SLOTS * HD
NREL = 384
EPS = 1e-6
BIG = 1e30
HUGE = 3e38
CHUNKS = 2 * NCH
LEAD = 3
RING, SLOT = 9, 2048
ADAS, BLOCKS = 4, 14
TWO_PI_HI, TWO_PI_MID = 6.28125, 0.0019350051879882812
ROUND = 12582912.0

C_ID, C_PERM, C_OPEN, C_CAUSAL, C_BEFORE, C_IOTA, C_FREQ, NCONST = 0, 128, 160, 288, 416, 544, 800, 801
V_MIX, V_FFN, V_KV, V_FINAL, V_LQ, V_LKV, NVEC = 0, 16, 32, 40, 48, 51, 53
SH_M, SC_M, GT_M, SH_F, SC_F, GT_F = range(6)
KV_SH, KV_SC, L1 = 6, 7, 8


def trunk(nc, x, c, positions, g_mix, g_ffn, w_ada, b_ada, w_mla_in, g_mla_q, w_mla_q_up, g_mla_kv,
          w_mla_kv_up, w_mla_out, g_kv_b, w_ada_kv, b_ada_kv, w_kv_b, rpb_table, w_q_b, w_o_b,
          w_ffn_gu, w_ffn_down, w_router, w_exp_gu, w_exp_down, g_final, consts, onehot, relmask, out):
    ctx = ExitStack()
    with ctx:
        def sb(name, shape, dt=F32):
            return ctx.enter_context(nc.sbuf_tensor(name, shape, dt))

        def sem(name):
            return ctx.enter_context(nc.semaphore(name))

        bank = [ctx.enter_context(nc.psum_tensor(f"bank{i}", [P, 512], F32)) for i in range(4)]
        wide = ctx.enter_context(nc.psum_tensor("wide", [P, 2048], F32))
        upper = [wide[:, 512 * i:512 * (i + 1)] for i in range(4)]

        hT = sb("hT", [P, KT, T])
        ring = sb("ring", [P, RING, SLOT])
        KB = 1024
        region0 = nc.sbuf_base
        sb("region", [P, 112 * KB // 4])

        def at(name, start, shape, dt=F32):
            return nc.alloc_sbuf_tensor_at(name, shape, dt, offset=region0 + start)

        nT = at("nT", 0, [P, KT, T])
        sqT = at("sqT", 8 * KB, [P, KT, T])
        strip = at("strip", 16 * KB, [P, ADAS, D])
        adasum = at("adasum", 32 * KB, [P, 2, D])
        arena = at("arena", 40 * KB, [P, 18432])
        adasum_c = at("adasum_c", 98 * KB, [P, D])
        nT_lo = at("nT_lo", 0, [P, KT, T], F32R)
        nT_hi = at("nT_hi", 8 * KB, [P, KT, T], F32R)
        n2_hi = at("n2_hi", 16 * KB, [P, KT, T], F32R)
        n2_lo = at("n2_lo", 80 * KB, [P, KT, T], F32R)
        ff_hi = at("ff_hi", 40 * KB, [P, 3, SLOT], F32R)
        ff_lo = at("ff_lo", 64 * KB, [P, 3, SLOT], F32R)
        hid_hi = at("hid_hi", 92 * KB, [P, 2, T], F32R)
        hid_lo = at("hid_lo", 94 * KB, [P, 2, T], F32R)
        kq_hi = [at(f"kq_hi{i}", (24 + 8 * i) * KB, [P, SLOT], F32R) for i in range(2)]
        kq_lo = [at(f"kq_lo{i}", (88 + 14 * i) * KB, [P, SLOT], F32R) for i in range(2)]
        w_hi = at("w_hi", 16 * KB, [P, 3, SLOT], F32R)
        w_lo = at("w_lo", 40 * KB, [P, 3, SLOT], F32R)
        xg_hi = at("xg_hi", 0, [P, KT, T], F32R)
        xg_lo = at("xg_lo", 8 * KB, [P, KT, T], F32R)
        hT_hi = at("hT_hi", 64 * KB, [P, 2, T], F32R)
        hT_lo = at("hT_lo", 66 * KB, [P, 2, T], F32R)
        con = sb("con", [P, NCONST])
        ones = sb("ones", [P, P])
        zeros = sb("zeros", [1, 512], BF16)
        vrows = sb("vrows", [NVEC, P])
        brows = sb("brows", [BLOCKS * KT, P])
        crow = sb("crow", [KT, P])
        vec = sb("vec", [P, NVEC])
        bcol = sb("bcol", [P, BLOCKS * KT])
        mod = sb("mod", [P, BLOCKS * KT])
        cact = sb("cact", [P, KT])
        ascale = sb("ascale", [P, 5, KT])
        eps = sb("eps", [P, 1])
        unused = sb("unused", [P, 1])
        std = sb("std", [P, 2, T])
        rstd = sb("rstd", [P, 2, T])
        trig = sb("trig", [P, 2, T])
        rsum = sb("rsum", [P, TB, HEADS])
        rinv = sb("rinv", [P, TB, HEADS])
        nmax = sb("nmax", [P, TB, HEADS])
        npart = sb("npart", [P, SLOTS])
        wrout = sb("wrout", [P, KT, NE])
        table = sb("table", [BUCKETS, GROUPS * SLOTS])
        small = sb("small", [P, 12, TB, NE + 1])
        counts = sb("counts", [1, NE + 1], I32)
        scratch = nc.dram_tensor("relbias", [SLOTS, GROUPS, P, NREL], F32, kind="Internal").ap()

        def area(at, *shape):
            size = 1
            for n in shape:
                size *= n
            a = arena[:, at:at + size]
            if len(shape) == 2:
                a = a.rearrange("p (a b) -> p a b", b=shape[1])
            if len(shape) == 3:
                a = a.rearrange("p (a b c) -> p a b c", b=shape[1], c=shape[2])
            return a

        oh = area(0, GROUPS, NREL)
        rmask = area(1152, GROUPS, NREL)
        relb = area(16384, GROUPS, NREL)
        xtok = area(16384, TB, D)
        posi = area(12288, T).bitcast(I32)
        ang = area(12544, 2, T)
        turns = area(13056, 2, T)
        lat = sqT[:, 0:5, :]
        Q = area(0, HEADS, T)
        K = area(4096, HEADS, T)
        V = area(8192, TB, D)
        O = area(10240, TB, D)
        latsq = area(10240, 5, T)
        latn = area(12288, 5, T)
        prob = area(12288, 2, 3 * P)
        probT = area(13056, 2, 3 * P)
        rt = area(14336, 2, 2 * T)
        krot = area(15360, 2, T)
        Qd = area(0, 12, T)
        Kd = area(3072, 12, T)
        Vd = area(6144, TB, 3 * DQ)
        Od = area(9216, TB, DQ)
        n2T = area(10240, KT, T)
        pds = [area(12288, 9 * P), area(15872, 9 * P)]
        pdT = area(13440, 2, 3 * P)
        relT = area(14336, 2, GROUPS, 2 * P)
        sg = area(12288, 2, T)
        hid = area(12800, 2, T)
        ntok = area(7168, TB, D)
        yslot = area(9216, TB, D)
        moe = area(11264, KT, T)
        sel = area(13312, TB, T)
        selg = area(13824, TB, T)
        selgT = area(14336, TB, T)
        gate_act = area(14848, TB, T)
        hidden = area(15360, TB, T)
        otok = area(0, TB, D)

        ident = con[:, C_ID:C_ID + P]
        perm = con[NOPE:QK, C_PERM:C_PERM + ROPE]
        causal = con[:, C_CAUSAL:C_CAUSAL + P]
        before = con[:, C_BEFORE:C_BEFORE + P]
        iota = con[:, C_IOTA:C_IOTA + T]
        freq = con[NOPE:QK, C_FREQ:C_FREQ + 1]

        names = """in_c cT in_vec in_con in_x in_misc in_pos pool_const rel_stored vecT vec_sb c_ready xT x_act
            relmm rel_ready trig_step trig_done ada_step ada_reduced mod_ready
            sq stat std_ready dve_own norm_mul norm_ready scaled
            latmm lat_sb latsq_done latstat latstd latn_ready krmm k_rot k_bcast
            qmm q_sb ropemm rope_mul rope_done kmm k_sb vmm v_sb
            mscore masked expd mprobT mprobT_sb mpv o_norm oT oT_sb omm h_ready
            gatemm upmm downmm silu_done hid_ready hid_hi_done hid_lo_done norm_lo
            dg_hi du_hi dd_hi dg_lo du_lo dd_lo kq_hi_done kq_lo_done
            kvmm kv_sb qdmm qd_sb dscore dmask dexp dprobT dprobT_sb dpv od_norm odT odT_sb odmm
            logit ntokT ntok_sb routed routed_gap gap_exp rankmm count_sb
            selmade gather0 gather1 xg_hi0 xg_hi1 xg_lo0 xg_lo1 selT selT_sb scatmm moe_sum
            hi_a hi_b hi_d lo_a lo_b lo_d lo2_a lo2_b lo2_d gua gub e_silu e_hid e_hT hT_hi_done hT_lo_done e_down y_sb
            finT fin_act fin_dve out_done""".split()
        s = {n: sem(n) for n in names}
        landed = [sem(f"landed{i}") for i in range(RING)]
        strip_in = [sem(f"strip_in{i}") for i in range(ADAS)]
        rel_in = [sem(f"rel_in{i}") for i in range(2)]

        freed = []
        freed += [(s["latmm"], 2 * i + 2) for i in range(3)]
        freed += [(s["qmm"], HEADS)] * QRT
        freed += [(s["vmm"], 4)] * KVT
        freed += [(s["omm"], 2 * i + 2) for i in range(4)]
        T_QUP, T_KVUP, T_OUT, T_FFN = 3, 6, 8, 12

        for i in range(CHUNKS):
            freed += [(s["dg_lo"], i + 1), (s["du_lo"], i + 1), (s["dd_lo"], i + 1)]
        T_KVB = len(freed)
        T_QB = T_KVB + 12
        freed += [(s["kq_lo_done"], i + 1) for i in range(18)]
        T_OB = len(freed)
        freed += [(s["odmm"], 4 * i + 4) for i in range(2)]
        T_MOE = len(freed)

        def tile_in(eng, t):
            eng.wait_ge(landed[t % RING], 16 * (t // RING + 1))

        def slot(t):
            return ring[:, t % RING, :]

        def cols(t, kt=KT, n=None):
            n = n or SLOT // kt
            return slot(t)[:, 0:kt * n].rearrange("p (k n) -> p k n", n=n)

        def by_blocks(eng, e, body):
            count = eng.value_load(counts[0:1, bass.ds(e, 1)], min_val=0, max_val=T)
            with eng.If(count < P + 1):
                body(1)
            with eng.Else():
                body(2)
            eng.nop()

        def unless_last(eng, e, body):
            with eng.If(e < NE - 1):
                body()
            with eng.Else():
                eng.nop()

        def width(c):
            return 2 * P if c % NCH < NCH - 1 else P

        UNITS = ("a", "b", "d")

        def landings(e, c, u):
            t = T_MOE + 3 * c + u
            per = 1 if u == 2 else 2
            before = len([x for x in range(T_MOE) if x % RING == t % RING])
            return e * (16 * per * CHUNKS // LEAD) + 16 * (before + per * (c // LEAD + 1))

        def dve_share(c, u):
            return unit_size(c, u) * 11 // 16

        def unit_size(c, u):
            return width(c) * (2 * KT // 2 if u < 2 else D // P)

        def ada_sum(b):
            i = b % 2 if b < 4 else (b + 2) % 3
            return adasum_c[:, :] if i == 2 else adasum[:, i, :]

        block = ctx.enter_context(nc.Block())

        @block.sync
        def _(sp):
            def rows(ap, r0, n):
                return ap[r0:r0 + n, :]

            vlist = [(V_MIX, g_mix.rearrange("a (j p) -> (a j) p", p=P)),
                     (V_FFN, g_ffn.rearrange("a (j p) -> (a j) p", p=P)),
                     (V_KV, g_kv_b.rearrange("(j p) -> j p", p=P)), (V_FINAL, g_final.rearrange("(j p) -> j p", p=P)),
                     (V_LQ, g_mla_q.rearrange("a (j p) -> (a j) p", p=P)),
                     (V_LKV, g_mla_kv.rearrange("a (j p) -> (a j) p", p=P))]
            sp.dma_start(crow[:, :], c.rearrange("a (j p) -> (a j) p", p=P)).then_inc(s["in_c"], 16)
            for at, ap in vlist:
                sp.dma_start(vrows[at:at + ap.shape[0], :], ap).then_inc(s["in_vec"], 16)
            ba = b_ada.rearrange("l (j p) -> (l j) p", p=P)
            sp.dma_start(brows[0:48, :], ba[0:48, :]).then_inc(s["in_vec"], 16)
            sp.dma_start(brows[48:64, :], b_ada_kv.rearrange("(j p) -> j p", p=P)).then_inc(s["in_vec"], 16)
            sp.dma_start(brows[64:112, :], ba[48:96, :]).then_inc(s["in_vec"], 16)

            def load(t, dst, src):
                if t >= RING:
                    sp.wait_ge(*freed[t - RING])
                sp.dma_start(dst, src).then_inc(landed[t % RING], 16)

            strips = "(k p) n -> p k n"
            sp.wait_ge(s["ada_step"], KT + 5)
            for i, (a, b) in enumerate(((0, 256), (256, 512), (512, 672))):
                load(i, cols(i, KT, b - a), w_mla_in[0][:, a:b].rearrange(strips, p=P))
            for k in range(QRT):
                load(T_QUP + k, slot(T_QUP + k)[:, 0:HEADS * QK], w_mla_q_up[0][k * P:(k + 1) * P, :])
            for k in range(KVT):
                load(T_KVUP + k, slot(T_KVUP + k), w_mla_kv_up[0][k * P:(k + 1) * P, :])
            for i in range(4):
                load(T_OUT + i, cols(T_OUT + i), w_mla_out[0][:, 256 * i:256 * (i + 1)].rearrange(strips, p=P))
            for half in range(2):
                for ch in range(NCH):
                    t = T_FFN + 3 * (NCH * half + ch)
                    f0, n = half * HALF + ch * 256, min(256, HALF - ch * 256)
                    load(t, cols(t, KT, n), w_ffn_gu[0][:, f0:f0 + n].rearrange(strips, p=P))
                    load(t + 1, cols(t + 1, KT, n), w_ffn_gu[0][:, FF + f0:FF + f0 + n].rearrange(strips, p=P))
                    load(t + 2, cols(t + 2, n // P, D), w_ffn_down[0][f0:f0 + n, :].rearrange(strips, p=P))
            for i in range(12):
                load(T_KVB + i, cols(T_KVB + i), w_kv_b[:, 256 * i:256 * (i + 1)].rearrange(strips, p=P))
            for i in range(6):
                load(T_QB + i, cols(T_QB + i), w_q_b[0][:, 256 * i:256 * (i + 1)].rearrange(strips, p=P))
            for i in range(2):
                load(T_OB + i, cols(T_OB + i, 4), w_o_b[0][:, 512 * i:512 * (i + 1)].rearrange(strips, p=P))

            gu_rows = w_exp_gu[0].rearrange("e d n -> (e d) n").rearrange("r (i f) -> r i f", i=2)
            down_rows = w_exp_down[0].rearrange("e f n -> (e f) n")
            with sp.Fori(0, NE) as e:
                for ch in range(CHUNKS):
                    n = width(ch)
                    f0 = (ch // NCH) * HALF + (ch % NCH) * 2 * P
                    for u in range(3):
                        if ch < LEAD:
                            sp.wait_ge(*freed[T_MOE - RING + 3 * ch + u])
                        sp.wait_ge(s["lo_" + UNITS[u]], e * CHUNKS + ch + 1)
                        sp.wait_ge(s["lo2_" + UNITS[u]], e * CHUNKS + ch + 1)
                        to = slot(T_MOE + 3 * ch + u)[:, 0:unit_size(ch, u)]
                        if u < 2:
                            src = gu_rows[bass.ds(e * D + u * (D // 2), D // 2), :, f0:f0 + n]
                            for i in range(2):
                                sp.dma_start(to.rearrange("p (k i n) -> p k i n", i=2, n=n)[:, :, i, :],
                                             src[:, i, :].rearrange(strips, p=P))\
                                    .then_inc(landed[(T_MOE + 3 * ch + u) % RING], 16)
                        else:
                            src = down_rows[bass.ds(e * FF + f0, n), :].rearrange(strips, p=P)
                            sp.dma_start(to.rearrange("p (k n) -> p k n", n=D), src)\
                                .then_inc(landed[(T_MOE + 3 * ch + u) % RING], 16)
            ov = out[0].rearrange("(b p) d -> p b d", p=P)
            for b in range(TB):
                sp.wait_ge(s["fin_act"], b + 1)
                sp.wait_ge(s["fin_dve"], b + 1)
                sp.dma_start(ov[:, b, :], otok[:, b, :]).then_inc(s["out_done"], 16)
            sp.wait_ge(s["out_done"], 16 * TB)

        @block.gpsimd
        def _(pool):
            nc.gpsimd.memset(ones[:, :], 1.0).then_inc(s["pool_const"], 1)
            nc.gpsimd.memset(eps[:, :], EPS).then_inc(s["pool_const"], 1)
            nc.gpsimd.memset(zeros[:, :], 0.0).then_inc(s["pool_const"], 1)
            nc.gpsimd.memset(small[:, :, :, :], 0.0).then_inc(s["pool_const"], 1)
            nc.gpsimd.memset(counts[:, :], 0).then_inc(s["pool_const"], 1)

            for u in UNITS:
                pool.sem_inc(s["lo_" + u], LEAD)
                pool.sem_inc(s["lo2_" + u], LEAD)

            def blocks(first, w, col):
                for k in range(KT):
                    n = first * KT + k
                    if not (isinstance(n, int) and n < ADAS):
                        pool.wait_ge(s["ada_step"], n - ADAS + 1)
                    pool.dma_start(strip[:, k % ADAS, :], w[k * P:(k + 1) * P, col])\
                        .then_inc(strip_in[k % ADAS], 16)

            blocks(0, w_ada[0], slice(0, D))
            with pool.Fori(1, 4) as b:
                blocks(b, w_ada[0], bass.ds(b * D, D))
            pool.wait_ge(s["k_rot"], 1)
            nc.gpsimd.tensor_copy(K[NOPE:QK, :, :], krot[NOPE:QK, 1:2, :].broadcast_to([ROPE, HEADS, T]))\
                .then_inc(s["k_bcast"], 1)
            with pool.Fori(4, 6) as b:
                blocks(b, w_ada[0], bass.ds(b * D, D))
            with pool.Fori(0, 2) as b:
                blocks(b + KV_SH, w_ada_kv, bass.ds(b * D, D))
            pool.wait_ge(s["rel_ready"], GROUPS)
            for g in range(GROUPS):
                pool.dma_start(scratch[:, g, :, :], relb[0:SLOTS, g:g + 1, :].broadcast_to([SLOTS, P, NREL]))\
                    .then_inc(s["rel_stored"], 16)
            with pool.Fori(0, 6) as b:
                blocks(b + L1, w_ada[1], bass.ds(b * D, D))
            pool.wait_ge(s["rel_stored"], 16 * GROUPS)
            pool.wait_ge(s["mpv"], HEADS)
            pool.wait_ge(s["rope_done"], SLOTS)
            pool.wait_ge(s["mod_ready"], BLOCKS)
            for h in range(SLOTS):
                if h >= 2:
                    pool.wait_ge(s["dmask"], 2 * (h - 1))
                src = bass.AP(scratch.tensor, h * GROUPS * P * NREL + P - 1,
                              [[NREL - 1, P], [P * NREL, GROUPS], [1, 2 * P]])
                pool.dma_start(relT[:, h % 2, :, :], src).then_inc(rel_in[h % 2], 16)
            pool.wait_ge(s["odT"], 4)
            nc.gpsimd.memset(moe[:, :, :], 0.0).then_inc(s["moe_sum"], 1)

            def weight_lo(e, c, u):
                a, n = dve_share(c, u), unit_size(c, u)
                pool.wait_ge(s["hi_" + UNITS[u]], e * CHUNKS + c + 1)
                nc.gpsimd.tensor_tensor(w_lo[:, u, a:n], slot(T_MOE + 3 * c + u)[:, a:n],
                                        w_hi[:, u, a:n].bitcast(F32), ALU.subtract).then_inc(s["lo2_" + UNITS[u]], 1)

            weight_lo(0, 0, 0)
            weight_lo(0, 0, 1)
            with pool.Fori(0, NE) as e:
                for ch in range(1, CHUNKS):
                    weight_lo(e, ch, 0)
                    weight_lo(e, ch, 1)
                    weight_lo(e, ch - 1, 2)
                unless_last(pool, e, lambda: weight_lo(e, CHUNKS, 0))
                weight_lo(e, CHUNKS - 1, 2)
                unless_last(pool, e, lambda: weight_lo(e, CHUNKS, 1))

        @block.tensor
        def _(pe):
            mm, tr = nc.tensor.matmul, nc.tensor.transpose

            def turn(o, a, first):
                return mm(o, a, ident, start=True, stop=True) if first else tr(o, a, ident)

            def product(o, pairs):
                n = len(pairs)
                for i, (w, r) in enumerate(pairs):
                    last = mm(o, w, r, start=(i == 0), stop=(i == n - 1))
                return last

            def ada_reduce(b, i=None, dyn=0, to=None):
                i = b if i is None else i
                pe.wait_ge(s["ada_step"], dyn * KT + KT * (b + 1))
                if b >= 1 and to is None:
                    pe.wait_ge(s["mod_ready"], dyn + b)
                for j in range(KT):
                    last = mm((to or bank[3])[:, KT * i + j:KT * i + j + 1], ada_sum(b)[:, j * P:(j + 1) * P],
                              ones[:, 0:1], start=True, stop=True)
                last.then_inc(s["ada_reduced"], 1)

            def norm_stat(k):
                for j in range(KT):
                    pe.wait_ge(s["sq"], KT * k + j + 1)
                    last = mm(bank[2][:, 0:T], ones[:, :], sqT[:, j, :], start=(j == 0), stop=(j == KT - 1))
                last.then_inc(s["stat"], 1)

            pe.wait_ge(s["in_c"], 16)
            pe.wait_ge(s["in_con"], 16)
            tr(bank[2][:, 0:KT], crow[:, :], ident[0:KT, 0:KT]).then_inc(s["cT"], 1)
            pe.wait_ge(s["in_vec"], 16 * 9)
            pe.wait_ge(s["in_con"], 16)
            tr(bank[0][:, 0:NVEC], vrows[:, :], ident[0:NVEC, 0:NVEC]).then_inc(s["vecT"], 1)
            nb = BLOCKS * KT
            tr(bank[1][:, 0:nb], brows[:, :], ident[0:nb, 0:nb]).then_inc(s["vecT"], 1)
            pe.wait_ge(s["in_x"], 16)
            for d in range(KT):
                if d >= 4:
                    pe.wait_ge(s["x_act"], d - 3)
                for b in range(TB):
                    last = tr(upper[d % 4][:, b * P:(b + 1) * P], xtok[:, b, d * P:(d + 1) * P], ident)
                last.then_inc(s["xT"], 1)
            pe.wait_ge(s["pool_const"], 5)
            norm_stat(0)
            ada_reduce(0)
            pe.wait_ge(s["in_misc"], 16 * 4)
            pe.wait_ge(s["vec_sb"], 2)
            for g in range(GROUPS):
                mm((bank[0], bank[1], upper[0])[g][0:SLOTS, 0:NREL], table[:, g * SLOTS:(g + 1) * SLOTS], oh[0:BUCKETS, g, :],
                   start=True, stop=True).then_inc(s["relmm"], 1)
            ada_reduce(1)
            pe.wait_ge(s["rel_ready"], GROUPS)

            for i in range(6):
                if i % 2 == 0:
                    tile_in(pe, i // 2)
                if i >= 4:
                    pe.wait_ge(s["latsq_done"], i - 3)
                w = cols(i // 2, KT, 256 if i < 4 else 160)
                o = upper[i % 4][:, 0:T] if i < 5 else upper[1][NOPE:QK, 0:T]
                n = P if i < 5 else ROPE
                for k in range(KT):
                    if i == 0:
                        pe.wait_ge(s["norm_ready"], k + 1)
                    last = mm(o, w[:, k, (i % 2) * P:(i % 2) * P + n], nT[:, k, :], start=(k == 0), stop=(k == KT - 1))
                last.then_inc(s["latmm"], 1)
            pe.wait_ge(s["latsq_done"], 5)
            product(bank[2][:, 0:T], [(ones[:, :], latsq[:, i, :]) for i in range(QRT)]).then_inc(s["latstat"], 1)
            product(bank[1][:, 0:T], [(ones[:, :], latsq[:, QRT + i, :]) for i in range(KVT)])\
                .then_inc(s["latstat"], 1)
            pe.wait_ge(s["lat_sb"], 6)
            mm(bank[0][NOPE:QK, 0:T], perm, krot[NOPE:QK, 0, :], start=True, stop=True).then_inc(s["krmm"], 1)

            for k in range(QRT):
                tile_in(pe, T_QUP + k)
            for h in range(HEADS):
                if h >= 4:
                    pe.wait_ge(s["q_sb"], h - 3)
                if h == 0:
                    pe.wait_ge(s["latn_ready"], QRT)
                product(upper[h % 4][0:QK, 0:T], [(slot(T_QUP + k)[:, h * QK:(h + 1) * QK], latn[:, k, :])
                                                  for k in range(QRT)]).then_inc(s["qmm"], 1)
            pe.wait_ge(s["latn_ready"], 5)
            pe.wait_ge(s["k_rot"], 1)
            for k in range(KVT):
                tile_in(pe, T_KVUP + k)
            for p in range(HEADS // 2):
                if p >= 2:
                    pe.wait_ge(s["rope_mul"], p - 1)
                pe.wait_ge(s["q_sb"], min(2 * p + 6, HEADS))
                mm(bank[p % 2][NOPE:QK, 0:2 * T], perm, Q[NOPE:QK, 2 * p:2 * p + 2, :],
                   start=True, stop=True).then_inc(s["ropemm"], 1)
                for h in (2 * p, 2 * p + 1):
                    if h >= 4:
                        pe.wait_ge(s["k_sb"], h - 3)
                    if h == 0:
                        pe.wait_ge(s["q_sb"], HEADS)
                    product(upper[h % 4][0:NOPE, 0:T], [(slot(T_KVUP + k)[:, h * P:h * P + NOPE], latn[:, QRT + k, :])
                                                        for k in range(KVT)]).then_inc(s["kmm"], 1)
            for i in range(4):
                b, half = i // 2, i % 2
                pe.wait_ge(s["k_sb"], HEADS - 3 + i)
                product(upper[i], [(latn[:, QRT + k, b * P:(b + 1) * P],
                                    slot(T_KVUP + k).rearrange("p (h c) -> p h c", c=P)[:, half * 8:half * 8 + 8, NOPE:P])
                                   for k in range(KVT)]).then_inc(s["vmm"], 1)
            ada_reduce(2)
            ada_reduce(3)

            pe.wait_ge(s["rope_done"], HEADS // 2)
            pe.wait_ge(s["k_bcast"], 1)
            pe.wait_ge(s["v_sb"], 4)
            pe.wait_ge(s["mod_ready"], 4)
            for i in range(HEADS + 2):
                if i < HEADS:
                    h = i
                    if h >= 2:
                        pe.wait_ge(s["masked"], 2 * (h - 1))
                    mm(bank[h % 2][:, 0:P], Q[0:QK, h, 0:P], K[0:QK, h, 0:P], start=True, stop=True)
                    mm(bank[h % 2][:, P:3 * P], Q[0:QK, h, P:T], K[0:QK, h, :], start=True, stop=True)\
                        .then_inc(s["mscore"], 1)
                if 1 <= i <= HEADS:
                    h = i - 1
                    pe.wait_ge(s["expd"], 2 * (h + 1))
                    if h >= 2:
                        pe.wait_ge(s["mprobT_sb"], h - 1)
                    for j in range(3):
                        last = tr(bank[2 + h % 2][:, j * P:(j + 1) * P], prob[:, h % 2, j * P:(j + 1) * P], ident)
                    last.then_inc(s["mprobT"], 1)
                if i >= 2:
                    h = i - 2
                    pe.wait_ge(s["mprobT_sb"], h + 1)
                    o = upper[2 * (h // 8)][:, (h % 8) * VD:(h % 8 + 1) * VD]
                    mm(o, probT[:, h % 2, 0:P], V[:, 0, h * VD:(h + 1) * VD], start=True, stop=True)
                    o = upper[2 * (h // 8) + 1][:, (h % 8) * VD:(h % 8 + 1) * VD]
                    product(o, [(probT[:, h % 2, (b + 1) * P:(b + 2) * P], V[:, b, h * VD:(h + 1) * VD])
                                for b in range(TB)]).then_inc(s["mpv"], 1)
            ada_reduce(4)
            for d in range(KT):
                pe.wait_ge(s["o_norm"], 2 * (d // 4 + 1))
                if d >= 2:
                    pe.wait_ge(s["oT_sb"], d - 1)
                for b in range(TB):
                    last = tr(bank[d % 2][:, b * P:(b + 1) * P], O[:, b, d * P:(d + 1) * P], ident)
                last.then_inc(s["oT"], 1)
            pe.wait_ge(s["oT_sb"], KT)
            for d in range(KT):
                if d % 2 == 0:
                    tile_in(pe, T_OUT + d // 2)
                if d >= 4:
                    pe.wait_ge(s["h_ready"], d - 3)
                product(upper[d % 4][:, 0:T], [(cols(T_OUT + d // 2)[:, k, (d % 2) * P:(d % 2 + 1) * P], nT[:, k, :])
                                               for k in range(KT)]).then_inc(s["omm"], 1)
            norm_stat(1)
            ada_reduce(5, to=bank[1])
            pe.wait_ge(s["std_ready"], 2)
            ada_reduce(6, to=bank[2])
            ada_reduce(7, to=bank[3])

            def split_products(out, pairs, first, final, ready=None):
                n = 3 * len(pairs)
                for i, ((xh, xl), (wh, wl)) in enumerate(pairs):
                    if ready is not None:
                        pe.wait_ge(s["norm_lo"], ready + i + 1)
                    for j, (x_, w_) in enumerate(((xh, wh), (xh, wl), (xl, wh))):
                        at = 3 * i + j
                        last = mm(out, x_, w_, start=(first and at == 0), stop=(final and at == n - 1),
                                  skip_group_check=True)
                return last

            def open_sums(n):
                for i in range(n):
                    last = mm(upper[i], zeros[:, 0:P], zeros[:, :], start=True, stop=False, skip_group_check=True)
                return last

            def dense_half(half):
                c0 = half * NCH

                def hidden_products(c, u, o):
                    n = width(c)
                    for j in range(n // P):
                        at = [kt * n + j * P for kt in range(KT)]
                        last = split_products(o[:, j * T:(j + 1) * T],
                                              [((ff_hi[:, u, a:a + P], ff_lo[:, u, a:a + P]),
                                                (nT_hi[:, kt, :], nT_lo[:, kt, :])) for kt, a in enumerate(at)],
                                              True, True, 0 if c == u == j == 0 else None)
                    return last

                def down(c):
                    pe.wait_ge(s["dd_lo"], c0 + c + 1)
                    pe.wait_ge(s["hid_lo_done"], c0 + c + 1)
                    for j in range(width(c) // P):
                        for d in range(KT):
                            at = j * D + d * P
                            last = split_products(wide[:, d * T:(d + 1) * T],
                                                  [((ff_hi[:, 2, at:at + P], ff_lo[:, 2, at:at + P]),
                                                    (hid_hi[:, j, :], hid_lo[:, j, :]))], False, False)
                    last.then_inc(s["downmm"], 1)

                for c in range(NCH):
                    if c:
                        pe.wait_ge(s["silu_done"], c0 + c)
                    pe.wait_ge(s["dg_lo"], c0 + c + 1)
                    hidden_products(c, 0, bank[0]).then_inc(s["gatemm"], 1)
                    if c:
                        down(c - 1)
                    if c == 0:
                        pe.wait_ge(s["mod_ready"], 8)
                    pe.wait_ge(s["du_lo"], c0 + c + 1)
                    hidden_products(c, 1, bank[1]).then_inc(s["upmm"], 1)
                    if c in (2, 4):
                        ada_reduce(8 + c // 2 - 1, c // 2 - 1, half * 3)
                ada_reduce(10, 2, half * 3)
                down(NCH - 1)

            pe.wait_ge(s["h_ready"], KT)
            pe.wait_ge(s["oT_sb"], KT)
            open_sums(4)
            with pe.Fori(0, 2) as half:
                dense_half(half)

            norm_stat(2)
            for i in range(24):
                if i % 2 == 0:
                    pe.wait_ge(s["kq_lo_done"], i // 2 + 1)
                if i == 0:
                    pe.wait_ge(s["h_ready"], 2 * KT)
                if i >= 4:
                    pe.wait_ge(s["kv_sb"], i - 3)
                hi, lo = kq_hi[i // 2 % 2], kq_lo[i // 2 % 2]
                if (i // 2) % 4 < 2:
                    at = [k * T + (i % 2) * P for k in range(KT)]
                    pairs = [((hi[:, a:a + P], lo[:, a:a + P]), (nT_hi[:, k, :], nT_lo[:, k, :])) for k, a in enumerate(at)]
                else:
                    b = slice((i % 2) * P, (i % 2 + 1) * P)
                    pairs = [((nT_hi[:, k, b], nT_lo[:, k, b]), (hi[:, k * T:(k + 1) * T], lo[:, k * T:(k + 1) * T]))
                             for k in range(KT)]
                split_products(upper[i % 4][:, 0:T], pairs, True, True, KT if i == 0 else None).then_inc(s["kvmm"], 1)
            pe.wait_ge(s["norm_lo"], 3 * KT)
            for i in range(12):
                if i % 2 == 0:
                    pe.wait_ge(s["kq_lo_done"], 12 + i // 2 + 1)
                if i < 4:
                    pe.wait_ge(s["kv_sb"], 21 + i)
                else:
                    pe.wait_ge(s["qd_sb"], i - 3)
                hi, lo = kq_hi[i // 2 % 2], kq_lo[i // 2 % 2]
                at = [k * T + (i % 2) * P for k in range(KT)]
                split_products(upper[i % 4][:, 0:T],
                               [((hi[:, a:a + P], lo[:, a:a + P]), (n2_hi[:, k, :], n2_lo[:, k, :]))
                                for k, a in enumerate(at)], True, True).then_inc(s["qdmm"], 1)

            pe.wait_ge(s["qd_sb"], 12)

            def dscores(u):
                h, b = divmod(u, 2)
                if u >= 2:
                    pe.wait_ge(s["dmask"], u - 1)
                p0 = (h % 2) * HD
                for g in range(GROUPS):
                    t = 4 * g + h // 2
                    n = (b + 1) * P
                    o = bank[0][:, g * P:(g + 1) * P] if b == 0 else bank[1 + g // 2][:, (g % 2) * T:(g % 2) * T + T]
                    last = mm(o, Qd[p0:p0 + HD, t, b * P:(b + 1) * P], Kd[p0:p0 + HD, t, 0:n], start=True, stop=True)
                last.then_inc(s["dscore"], 1)

            def dtranspose(q):
                h, r = divmod(q, 3)
                pe.wait_ge(s["dexp"], 2 * h + (1 if r == 0 else 2))
                if q >= 2:
                    pe.wait_ge(s["dprobT_sb"], q - 1)
                o = bank[3] if q % 2 == 0 else upper[0]
                for j in range(3):
                    last = tr(o[:, j * P:(j + 1) * P], pds[h % 2][:, (3 * r + j) * P:(3 * r + j + 1) * P], ident)
                last.then_inc(s["dprobT"], 1)

            def dvalues(q):
                h, r = divmod(q, 3)
                pe.wait_ge(s["dprobT_sb"], q + 1)
                o = upper[1 if r == 0 else 2][:, h * HD:(h + 1) * HD]
                for j in range(3):
                    g, kb = (j, 0) if r == 0 else divmod(3 * (r - 1) + j, 2)
                    first = j == 0 and r < 2
                    last = mm(o, pdT[:, q % 2, j * P:(j + 1) * P], Vd[:, kb, g * DQ + h * HD:g * DQ + (h + 1) * HD],
                              start=first, stop=(j == 2 and r != 1))
                last.then_inc(s["dpv"], 1)

            dscores(0)
            dscores(1)
            for h in range(SLOTS):
                for r in range(3):
                    q = 3 * h + r
                    dtranspose(q)
                    if q >= 1:
                        dvalues(q - 1)
                    if h + 1 < SLOTS and r in (0, 1):
                        dscores(2 * h + 2 + r)
            dvalues(3 * SLOTS - 1)
            for d in range(4):
                pe.wait_ge(s["od_norm"], TB)
                if d >= 2:
                    pe.wait_ge(s["odT_sb"], d - 1)
                for b in range(TB):
                    last = tr(bank[d % 2][:, b * P:(b + 1) * P], Od[:, b, d * P:(d + 1) * P], ident)
                last.then_inc(s["odT"], 1)
            pe.wait_ge(s["odT_sb"], 4)
            for d in range(KT):
                if d % 4 == 0:
                    tile_in(pe, T_OB + d // 4)
                if d >= 4:
                    pe.wait_ge(s["h_ready"], 2 * KT + d - 3)
                product(upper[d % 4][:, 0:T], [(cols(T_OB + d // 4, 4)[:, k, (d % 4) * P:(d % 4 + 1) * P], nT[:, k, :])
                                               for k in range(4)]).then_inc(s["odmm"], 1)
            norm_stat(3)

            for k in range(KT):
                pe.wait_ge(s["norm_ready"], 4 * KT + k + 1)
                for b in range(TB):
                    last = mm(bank[2 + b][:, 0:NE], nT[:, k, b * P:(b + 1) * P], wrout[:, k, :],
                              start=(k == 0), stop=(k == KT - 1))
            last.then_inc(s["logit"], 1)
            for i in range(4):
                b, half = i // 2, i % 2
                for j in range(4):
                    d = 4 * half + j
                    last = tr(upper[i][:, j * P:(j + 1) * P], nT[:, d, b * P:(b + 1) * P], ident)
                last.then_inc(s["ntokT"], 1)
            pe.wait_ge(s["routed"], 1)
            chosen = small[:, 0, :, 0:NE]
            mm(bank[2][:, 0:NE], before, chosen[:, 0, :], start=True, stop=True)
            product(bank[2][:, NE:2 * NE], [(ones[:, :], chosen[:, 0, :]), (before, chosen[:, 1, :])])
            product(bank[2][:, 2 * NE:3 * NE], [(ones[:, :], chosen[:, 0, :]), (ones[:, :], chosen[:, 1, :])])\
                .then_inc(s["rankmm"], 1)
            pe.wait_ge(s["count_sb"], 1)
            pe.wait_ge(s["ntok_sb"], 4)

            def gather(e, k, to):
                pe.wait_ge(s["selmade"], e + 1)
                for d in range(KT):
                    last = product(to[d // 4][:, (d % 4) * P:(d % 4 + 1) * P],
                                   [(ntok[:, b, d * P:(d + 1) * P], sel[:, b, k * P:(k + 1) * P]) for b in range(TB)])
                last.then_inc(s[f"gather{k}"], 1)

            def turn_gates(e, nb):
                pe.wait_ge(s[f"xg_lo{nb - 1}"], e + 1)
                for k in range(nb):
                    for b in range(TB):
                        last = tr(bank[3][:, k * T + b * P:k * T + (b + 1) * P], selg[:, b, k * P:(k + 1) * P], ident)
                last.then_inc(s["selT"], 1)

            def gate_up(e, nb, c, u):
                n = 2 * width(c)
                pe.wait_ge(s["lo_" + UNITS[u]], e * CHUNKS + c + 1 + LEAD)
                pe.wait_ge(s["lo2_" + UNITS[u]], e * CHUNKS + c + 1 + LEAD)
                if u == 0 and c > 2 - nb:
                    pe.wait_ge(s["e_hid"], e * CHUNKS + (c - 1 if nb == 1 else c))
                for k in range(nb):
                    o = bank[c % 2 if nb == 1 else k][:, 0:n]
                    xs = [(xg_hi[:, 4 * u + i, k * P:(k + 1) * P], xg_lo[:, 4 * u + i, k * P:(k + 1) * P])
                          for i in range(4)]
                    ws = [(w_hi[:, u, i * n:(i + 1) * n], w_lo[:, u, i * n:(i + 1) * n]) for i in range(4)]
                    last = split_products(o, list(zip(xs, ws)), u == 0, u == 1)
                last.then_inc(s["gua" if u == 0 else "gub"], 1)

            def start(e, nb, prior):
                pe.wait_ge(s["xg_lo0"], e + 1)
                if nb == 2:
                    if prior:
                        pe.wait_ge(s["selT_sb"], e)
                    gather(e, 1, bank[2:4])
                    pe.wait_ge(s["xg_lo1"], e + 1)
                else:
                    pe.sem_inc(s["gather1"], 1)
                gate_up(e, nb, 0, 0)
                gate_up(e, nb, 0, 1)

            def expert(e, nb):
                c0 = e * CHUNKS

                def turn_hidden(c):
                    pe.wait_ge(s["e_hid"], c0 + c + 1)
                    for f in range(width(c) // P):
                        for k in range(nb):
                            j = f * nb + k
                            last = tr(bank[2][:, j * P:(j + 1) * P], hidden[:, k, f * P:(f + 1) * P], ident)
                    last.then_inc(s["e_hT"], 1)

                def down(c):
                    if c == 0:
                        pe.wait_ge(s["moe_sum"], e + 2)
                        open_sums(2 * nb)
                    pe.wait_ge(s["lo_d"], c0 + c + 1 + LEAD)
                    pe.wait_ge(s["lo2_d"], c0 + c + 1 + LEAD)
                    pe.wait_ge(s["hT_lo_done"], c0 + c + 1)
                    for k in range(nb):
                        for half in range(2):
                            o = wide[:, k * D + half * 512:k * D + (half + 1) * 512]
                            at = [f * D + half * 512 for f in range(width(c) // P)]
                            last = split_products(o, [((hT_hi[:, f, k * P:(k + 1) * P], hT_lo[:, f, k * P:(k + 1) * P]),
                                                       (w_hi[:, 2, a:a + 512], w_lo[:, 2, a:a + 512]))
                                                      for f, a in enumerate(at)], False, False)
                    last.then_inc(s["e_down"], 1)

                for c in range(1, CHUNKS):
                    gate_up(e, nb, c, 0)
                    turn_hidden(c - 1)
                    gate_up(e, nb, c, 1)
                    down(c - 1)
                    if nb == 1 and c == CHUNKS - 2:
                        unless_last(pe, e, lambda: gather(e + 1, 0, upper[2:4]))
                turn_hidden(CHUNKS - 1)
                down(CHUNKS - 1)
                if nb == 2:
                    unless_last(pe, e, lambda: (pe.wait_ge(s["selT_sb"], e + 1),
                                                gather(e + 1, 0, bank[2:4])))

            def scatter(e, nb):
                pe.wait_ge(s["y_sb"], e + 1)
                for d in range(KT):
                    last = product(wide[:, d * T:(d + 1) * T],
                                   [(yslot[:, k, d * P:(d + 1) * P], selgT[:, k, :]) for k in range(nb)])
                last.then_inc(s["scatmm"], 1)

            open_sums(4).then_inc(s["scatmm"], 1)
            gather(0, 0, bank[2:4])
            by_blocks(pe, 0, lambda nb: start(0, nb, False))
            by_blocks(pe, 0, lambda nb: turn_gates(0, nb))
            with pe.Fori(0, NE) as e:
                by_blocks(pe, e, lambda nb: expert(e, nb))
                unless_last(pe, e, lambda: by_blocks(pe, e + 1, lambda nb: start(e + 1, nb, True)))
                by_blocks(pe, e, lambda nb: scatter(e, nb))
                unless_last(pe, e, lambda: by_blocks(pe, e + 1, lambda nb: turn_gates(e + 1, nb)))

            norm_stat(4)
            pe.wait_ge(s["scaled"], KT)
            for i in range(4):
                b, half = i // 2, i % 2
                for j in range(4):
                    last = tr(upper[i][:, j * P:(j + 1) * P], nT[:, 4 * half + j, b * P:(b + 1) * P], ident)
                last.then_inc(s["finT"], 1)

        @block.scalar
        def _(act):
            go = nc.scalar.activation
            act.dma_start(con[:, :], consts).then_inc(s["in_con"], 16)
            act.dma_start(xtok, x[0].rearrange("(b p) d -> p b d", p=P)).then_inc(s["in_x"], 16)
            act.dma_start(oh[0:BUCKETS, :, :], onehot.rearrange("b (g m) -> b g m", g=GROUPS)).then_inc(s["in_misc"], 16)
            act.dma_start(rmask[0:SLOTS, :, :], relmask.rearrange("b (g m) -> b g m", g=GROUPS)).then_inc(s["in_misc"], 16)
            act.dma_start(table[:, :], rpb_table).then_inc(s["in_misc"], 16)
            act.dma_start(wrout[:, :, :], w_router[0].rearrange("(k p) e -> p k e", p=P)).then_inc(s["in_misc"], 16)
            pos_all = bass.AP(positions.tensor, 0, [[0, ROPE], [1, T]])
            act.dma_start(posi[NOPE:QK, :], pos_all).then_inc(s["in_pos"], 16)

            act.wait_ge(s["cT"], 1)
            go(cact[:, :], bank[2][:, 0:KT], ACT.Silu).then_inc(s["c_ready"], 1)
            for d in range(KT):
                act.wait_ge(s["xT"], d + 1)
                go(hT[:, d, :], upper[d % 4][:, 0:T], ACT.Copy).then_inc(s["x_act"], 1)

            def load_table(f):
                go(unused[:, :], eps[:, 0:1], f)

            def squares(k, ready):
                load_table(ACT.Sqrt)
                for j in range(KT):
                    ready(j)
                    go(sqT[:, j, :], hT[:, j, :], ACT.Square).then_inc(s["sq"], 1)
                act.wait_ge(s["stat"], k + 1)
                go(std[:, 0, :], bank[2][:, 0:T], ACT.Sqrt, bias=eps[:, 0:1], scale=1.0 / D)\
                    .then_inc(s["std_ready"], 1)

            def shifts(m, b, dst, hi=None):
                act.wait_ge(s["mod_ready"], b + 1)
                for j in range(KT):
                    act.wait_ge(s["norm_mul"], m * KT + j + 1)
                    go((hi if hi is not None else dst)[:, j, :], dst[:, j, :], ACT.Identity,
                       bias=mod[:, b * KT + j:b * KT + j + 1]).then_inc(s["norm_ready"], 1)

            act.wait_ge(s["pool_const"], 5)

            def x_ready(j):
                act.wait_ge(s["x_act"], j + 1)
            squares(0, x_ready)
            shifts(0, SH_M, nT)
            act.wait_ge(s["trig_step"], 1)
            go(trig[NOPE:QK, :, :], ang[NOPE:QK, :, :], ACT.Sin).then_inc(s["trig_done"], 1)

            act.wait_ge(s["stat"], 1)
            for i in range(6):
                act.wait_ge(s["latmm"], i + 1)
                if i < 5:
                    go(lat[:, i, :], upper[i % 4][:, 0:T], ACT.Copy).then_inc(s["lat_sb"], 1)
                    go(latsq[:, i, :], upper[i % 4][:, 0:T], ACT.Square).then_inc(s["latsq_done"], 1)
                else:
                    go(krot[NOPE:QK, 0, :], upper[1][NOPE:QK, 0:T], ACT.Copy).then_inc(s["lat_sb"], 1)
            act.wait_ge(s["latstat"], 1)
            go(std[:, 0, :], bank[2][:, 0:T], ACT.Sqrt, bias=eps[:, 0:1], scale=1.0 / QR).then_inc(s["latstd"], 1)
            act.wait_ge(s["latstat"], 2)
            go(std[:, 1, :], bank[1][:, 0:T], ACT.Sqrt, bias=eps[:, 0:1], scale=1.0 / KVR).then_inc(s["latstd"], 1)
            load_table(ACT.Exp)
            for h in range(HEADS):
                act.wait_ge(s["qmm"], h + 1)
                go(Q[0:QK, h, :], upper[h % 4][0:QK, 0:T], ACT.Copy).then_inc(s["q_sb"], 1)
            for h in range(HEADS):
                act.wait_ge(s["kmm"], h + 1)
                go(K[0:NOPE, h, :], upper[h % 4][0:NOPE, 0:T], ACT.Copy).then_inc(s["k_sb"], 1)
            for i in range(4):
                act.wait_ge(s["vmm"], i + 1)
                go(V[:, i // 2, (i % 2) * 512:(i % 2 + 1) * 512], upper[i], ACT.Copy).then_inc(s["v_sb"], 1)
            for h in range(HEADS + 1):
                if h >= 1:
                    g = h - 1
                    act.wait_ge(s["mprobT"], g + 1)
                    if g >= 2:
                        act.wait_ge(s["mpv"], g - 1)
                    go(probT[:, g % 2, :], bank[2 + g % 2][:, 0:3 * P], ACT.Copy).then_inc(s["mprobT_sb"], 1)
                for b in range(TB if h < HEADS else 0):
                    act.wait_ge(s["masked"], 2 * h + b + 1)
                    pr = prob[:, h % 2, 0:P] if b == 0 else prob[:, h % 2, P:3 * P]
                    go(pr, pr, ACT.Exp, bias=nmax[:, b, h:h + 1], scale=-1.0,
                       accum_out=rsum[:, b, h:h + 1]).then_inc(s["expd"], 1)
            for d in range(KT):
                act.wait_ge(s["oT"], d + 1)
                go(nT[:, d, :], bank[d % 2][:, 0:T], ACT.Copy).then_inc(s["oT_sb"], 1)

            def h_ready(base):
                return lambda j: act.wait_ge(s["h_ready"], base + j + 1)

            def dense_hi(c, u):
                t = T_FFN + 3 * c + u
                tile_in(act, t)
                if c:
                    act.wait_ge(s[("gatemm", "upmm", "downmm")[u]], c)
                n = width(c) * KT
                go(ff_hi[:, u, 0:n], slot(t)[:, 0:n], ACT.Copy).then_inc(s[("dg_hi", "du_hi", "dd_hi")[u]], 1)

            def dense_hidden_hi(c):
                n = width(c) // P
                act.wait_ge(s["hid_ready"], c + 1)
                go(hid_hi[:, 0:n, :], hid[:, 0:n, :], ACT.Copy).then_inc(s["hid_hi_done"], 1)

            for u in range(3):
                dense_hi(0, u)
            squares(1, h_ready(0))
            shifts(1, SH_F, nT, nT_hi)
            for c in range(CHUNKS):
                if c:
                    dense_hidden_hi(c - 1)
                    dense_hi(c, 1)
                act.wait_ge(s["gatemm"], c + 1)
                n = width(c) // P
                go(sg[:, 0:n, :], bank[0][:, 0:n * T].rearrange("p (j t) -> p j t", t=T), ACT.Silu)\
                    .then_inc(s["silu_done"], 1)
                if c < CHUNKS - 1:
                    dense_hi(c + 1, 0)
                if c:
                    dense_hi(c, 2)
            dense_hidden_hi(CHUNKS - 1)

            def kq_split_hi(i):
                tile_in(act, T_KVB + i)
                if i >= 2:
                    j = i - 2
                    act.wait_ge(*((s["kvmm"], 2 * j + 2) if j < 12 else (s["qdmm"], 2 * (j - 12) + 2)))
                go(kq_hi[i % 2][:, :], slot(T_KVB + i), ACT.Copy).then_inc(s["kq_hi_done"], 1)

            act.wait_ge(s["mod_ready"], BLOCKS)
            kq_split_hi(0)
            kq_split_hi(1)
            squares(2, h_ready(KT))
            shifts(2, KV_SH, nT, nT_hi)
            shifts(3, L1 + SH_M, n2T, n2_hi)
            load_table(ACT.Exp)
            for i in range(24):
                act.wait_ge(s["kvmm"], i + 1)
                m, r = divmod(i, 2)
                g, q = divmod(m, 4)
                dst = Kd[:, 4 * g + 2 * q + r, :] if q < 2 else Vd[:, r, g * DQ + (q - 2) * T:g * DQ + (q - 1) * T]
                go(dst, upper[i % 4][:, 0:T], ACT.Copy).then_inc(s["kv_sb"], 1)
                if i % 2:
                    kq_split_hi(i // 2 + 2)
            for i in range(12):
                act.wait_ge(s["qdmm"], i + 1)
                go(Qd[:, i, :], upper[i % 4][:, 0:T], ACT.Copy).then_inc(s["qd_sb"], 1)
                if i % 2 and i < 8:
                    kq_split_hi(12 + i // 2 + 2)
            for u in range(2 * SLOTS):
                h, b = divmod(u, 2)
                act.wait_ge(s["dmask"], u + 1)
                pr = pds[h % 2][:, 0:3 * P] if b == 0 else pds[h % 2][:, 3 * P:9 * P]
                go(pr, pr, ACT.Exp, bias=nmax[:, b, h:h + 1], scale=-1.0,
                   accum_out=rsum[:, b, h:h + 1]).then_inc(s["dexp"], 1)
            for d in range(4):
                act.wait_ge(s["odT"], d + 1)
                go(nT[:, d, :], bank[d % 2][:, 0:T], ACT.Copy).then_inc(s["odT_sb"], 1)
            def weight_hi(e, c, u):
                t = T_MOE + 3 * c + u
                act.wait_ge(landed[t % RING], landings(e, c, u))
                if c:
                    act.wait_ge(s[("gua", "gub", "e_down")[u]], e * CHUNKS + c)
                n = unit_size(c, u)
                go(w_hi[:, u, 0:n], slot(t)[:, 0:n], ACT.Copy).then_inc(s["hi_" + UNITS[u]], 1)

            weight_hi(0, 0, 0)
            weight_hi(0, 0, 1)
            squares(3, h_ready(2 * KT))
            shifts(4, L1 + SH_F, nT)
            load_table(ACT.Exp)
            act.wait_ge(s["logit"], 1)
            act.wait_ge(s["dexp"], 2 * SLOTS)
            for i in range(4):
                act.wait_ge(s["ntokT"], i + 1)
                go(ntok[:, i // 2, (i % 2) * 512:(i % 2 + 1) * 512], upper[i], ACT.Copy).then_inc(s["ntok_sb"], 1)
            act.wait_ge(s["routed_gap"], 1)
            go(small[:, 8, :, 0:1], small[:, 8, :, 1:2], ACT.Exp).then_inc(s["gap_exp"], 1)
            act.wait_ge(s["count_sb"], 1)

            def columns_hi(e, k, src):
                act.wait_ge(s[f"gather{k}"], e + 1)
                for i in range(2):
                    ins = go(xg_hi[:, 4 * i:4 * i + 4, k * P:(k + 1) * P],
                             src[i].rearrange("p (d n) -> p d n", n=P), ACT.Copy)
                ins.then_inc(s[f"xg_hi{k}"], 1)

            def second_block(e, nb):
                if nb == 2:
                    columns_hi(e, 1, bank23)
                else:
                    act.sem_inc(s["xg_hi1"], 1)

            def expert(e, nb):
                c0 = e * CHUNKS

                def silu(c):
                    w = width(c)
                    act.wait_ge(s["gub"], c0 + c + 1)
                    if c:
                        act.wait_ge(s["e_hid"], c0 + c)
                    for k in range(nb):
                        ins = go(gate_act[:, k, 0:w], bank[c % 2 if nb == 1 else k][:, 0:w], ACT.Silu)
                    ins.then_inc(s["e_silu"], 1)

                def hidden_hi(c):
                    nf = width(c) // P
                    act.wait_ge(s["e_hT"], c0 + c + 1)
                    go(hT_hi[:, 0:nf, 0:nb * P], bank[2][:, 0:nf * nb * P].rearrange("p (f n) -> p f n", f=nf), ACT.Copy)\
                        .then_inc(s["hT_hi_done"], 1)

                def results():
                    act.wait_ge(s["e_down"], c0 + CHUNKS)
                    go(yslot[:, 0:nb, :], wide[:, 0:nb * D].rearrange("p (k d) -> p k d", d=D), ACT.Copy)\
                        .then_inc(s["y_sb"], 1)

                for c in range(1, CHUNKS):
                    weight_hi(e, c, 0)
                    silu(c - 1)
                    weight_hi(e, c, 1)
                    if c == 1:
                        act.wait_ge(s["selT"], e + 1)
                        go(selgT[:, 0:nb, :], bank[3][:, 0:nb * T].rearrange("p (k t) -> p k t", t=T), ACT.Copy)\
                            .then_inc(s["selT_sb"], 1)
                    weight_hi(e, c - 1, 2)
                    hidden_hi(c - 1)

                def last_chunk_and_next():
                    weight_hi(e, CHUNKS, 0)
                    silu(CHUNKS - 1)
                    if nb == 1:
                        act.wait_ge(s["gub"], c0 + CHUNKS)
                        columns_hi(e + 1, 0, free23)
                    weight_hi(e, CHUNKS - 1, 2)
                    hidden_hi(CHUNKS - 1)
                    weight_hi(e, CHUNKS, 1)
                    results()
                    if nb == 2:
                        columns_hi(e + 1, 0, bank23)

                def last_chunk():
                    silu(CHUNKS - 1)
                    weight_hi(e, CHUNKS - 1, 2)
                    hidden_hi(CHUNKS - 1)
                    results()

                with act.If(e < NE - 1):
                    last_chunk_and_next()
                with act.Else():
                    last_chunk()

            bank23 = (bank[2][:, :], bank[3][:, :])
            free23 = (upper[2], upper[3])
            columns_hi(0, 0, bank23)
            by_blocks(act, 0, lambda nb: second_block(0, nb))
            with act.Fori(0, NE) as e:
                by_blocks(act, e, lambda nb: expert(e, nb))
                unless_last(act, e, lambda: by_blocks(act, e + 1, lambda nb: second_block(e + 1, nb)))
            squares(4, h_ready(3 * KT))
            for i in range(0, 4, 2):
                act.wait_ge(s["finT"], i + 1)
                go(otok[:, i // 2, 0:512], upper[i], ACT.Copy).then_inc(s["fin_act"], 1)

        @block.vector
        def _(dve):
            v = nc.vector
            own = [0]

            def link(ins):
                own[0] += 1
                ins.then_inc(s["dve_own"], 1)
                dve.wait_ge(s["dve_own"], own[0])

            def ada_strip(b, k, dyn=0):
                n = KT * b + k
                m = n % ADAS
                turn = n // ADAS + 1
                dve.wait_ge(strip_in[m], dyn * (16 * KT // ADAS) + 16 * turn)
                if k == 0:
                    if b >= 2 and b != 6:
                        dve.wait_ge(s["ada_reduced"], dyn + (b - 1 if b < 6 else b - 2))
                    v.tensor_scalar(ada_sum(b), strip[:, m, :], cact[:, 0:1], None, ALU.mult)\
                        .then_inc(s["ada_step"], 1)
                else:
                    dve.wait_ge(s["ada_step"], dyn * KT + n)
                    v.scalar_tensor_tensor(out=ada_sum(b), in0=strip[:, m, :], scalar=cact[:, k:k + 1],
                                           in1=ada_sum(b), op0=ALU.mult, op1=ALU.add)\
                        .then_inc(s["ada_step"], 1)

            def ada(b):
                for k in range(KT):
                    ada_strip(b, k)

            def mod_out(b, at=bank[3]):
                dve.wait_ge(s["ada_reduced"], b + 1)
                v.tensor_tensor(mod[:, b * KT:(b + 1) * KT], at[:, b * KT:(b + 1) * KT],
                                bcol[:, b * KT:(b + 1) * KT], ALU.add).then_inc(s["mod_ready"], 1)

            def scale_of(m, b, g):
                dve.wait_ge(s["mod_ready"], b + 1)
                link(v.scalar_tensor_tensor(out=ascale[:, m, :], in0=mod[:, b * KT:(b + 1) * KT], scalar=1.0,
                                            in1=vec[:, g:g + KT], op0=ALU.add, op1=ALU.mult))

            def norm(m, dst):
                for j in range(KT):
                    v.scalar_tensor_tensor(out=dst[:, j, :], in0=hT[:, j, :], scalar=ascale[:, m, j:j + 1],
                                           in1=rstd[:, 0, :], op0=ALU.mult, op1=ALU.mult)\
                        .then_inc(s["norm_mul"], 1)

            def norm_split(m, b, dst, hi, lo):
                for j in range(KT + 2):
                    if j < KT:
                        v.scalar_tensor_tensor(out=dst[:, j, :], in0=hT[:, j, :], scalar=ascale[:, m, j:j + 1],
                                               in1=rstd[:, 0, :], op0=ALU.mult, op1=ALU.mult)\
                            .then_inc(s["norm_mul"], 1)
                    if j >= 2:
                        i = j - 2
                        dve.wait_ge(s["norm_ready"], m * KT + i + 1)
                        v.scalar_tensor_tensor(out=lo[:, i, :], in0=dst[:, i, :],
                                               scalar=mod[:, b * KT + i:b * KT + i + 1],
                                               in1=hi[:, i, :].bitcast(F32), op0=ALU.add, op1=ALU.subtract)\
                            .then_inc(s["norm_lo"], 1)

            def inverse(k):
                dve.wait_ge(s["std_ready"], k + 1)
                link(v.reciprocal(rstd[:, 0, :], std[:, 0, :]))

            def residual(j, src, b):
                v.scalar_tensor_tensor(out=hT[:, j, :], in0=src, scalar=mod[:, b * KT + j:b * KT + j + 1],
                                       in1=hT[:, j, :], op0=ALU.mult, op1=ALU.add).then_inc(s["h_ready"], 1)

            dve.wait_ge(s["c_ready"], 1)
            ada(0)
            dve.wait_ge(s["vecT"], 1)
            v.tensor_copy(vec[:, :], bank[0][:, 0:NVEC]).then_inc(s["vec_sb"], 1)
            dve.wait_ge(s["vecT"], 2)
            v.tensor_copy(bcol[:, :], bank[1][:, 0:BLOCKS * KT]).then_inc(s["vec_sb"], 1)
            for k in range(KT):
                ada_strip(1, k)
                if k in (3, 5, 7):
                    g = (k - 3) // 2
                    dve.wait_ge(s["relmm"], g + 1)
                    v.scalar_tensor_tensor(out=relb[0:SLOTS, g, :], in0=(bank[0], bank[1], upper[0])[g][0:SLOTS, 0:NREL],
                                           scalar=HD ** 0.5, in1=rmask[0:SLOTS, g, :], op0=ALU.mult, op1=ALU.add)\
                        .then_inc(s["rel_ready"], 1)
            mod_out(0)
            mod_out(1)
            scale_of(0, SC_M, V_MIX)
            inverse(0)
            norm(0, nT)
            R = slice(NOPE, QK)
            dve.wait_ge(s["in_pos"], 16)
            dve.wait_ge(s["in_con"], 16)
            link(v.tensor_copy(ang[R, 1, :], posi[R, :]))
            link(v.tensor_scalar(ang[R, 0, :], ang[R, 1, :], freq, None, ALU.mult))
            link(v.tensor_scalar(turns[R, 0, :], ang[R, 0, :], 0.15915494309189535, 0.25, ALU.mult, ALU.add))
            link(v.tensor_scalar(turns[R, 1, :], ang[R, 0, :], 0.15915494309189535, None, ALU.mult))
            link(v.tensor_copy(ang[R, 1, :], ang[R, 0, :]))
            link(v.tensor_scalar(turns[R, :, :], turns[R, :, :], ROUND, None, ALU.add))
            link(v.tensor_scalar(turns[R, :, :], turns[R, :, :], ROUND, None, ALU.subtract))
            two_pi_lo = 6.283185307179586 - TWO_PI_HI - TWO_PI_MID
            for part in (TWO_PI_HI, TWO_PI_MID, two_pi_lo):
                link(v.scalar_tensor_tensor(out=ang[R, :, :], in0=turns[R, :, :], scalar=-part, in1=ang[R, :, :],
                                            op0=ALU.mult, op1=ALU.add))
            link(v.tensor_scalar(ang[R, 0, :], ang[R, 0, :], 1.5707963267948966, None, ALU.add))
            v.tensor_scalar(ang[R, :, :], ang[R, :, :], 3.1415925, -3.1415925, ALU.min, ALU.max)\
                .then_inc(s["trig_step"], 1)


            for i, (a, n, g) in enumerate(((0, QRT, V_LQ), (QRT, KVT, V_LKV))):
                dve.wait_ge(s["latstd"], i + 1)
                dve.wait_ge(s["lat_sb"], 5)
                link(v.reciprocal(rstd[:, i, :], std[:, i, :]))
                if i == 0:
                    dve.wait_ge(s["trig_done"], 1)
                for j in range(n):
                    v.scalar_tensor_tensor(out=latn[:, a + j, :], in0=lat[:, a + j, :], scalar=vec[:, g + j:g + j + 1],
                                           in1=rstd[:, i, :], op0=ALU.mult, op1=ALU.mult)\
                        .then_inc(s["latn_ready"], 1)
            cos, sin = trig[R, 0:1, :], trig[R, 1:2, :]
            dve.wait_ge(s["krmm"], 1)
            dve.wait_ge(s["lat_sb"], 6)
            link(v.tensor_tensor(rt[R, 0, 0:T], bank[0][R, 0:T], trig[R, 1, :], ALU.mult))
            link(v.tensor_tensor(rt[R, 1, 0:T], krot[R, 0, :], trig[R, 0, :], ALU.mult))
            v.tensor_tensor(krot[R, 1, :], rt[R, 0, 0:T], rt[R, 1, 0:T], ALU.add).then_inc(s["k_rot"], 1)
            ada(2)
            ada(3)
            dve.wait_ge(s["k_rot"], 1)
            for p in range(HEADS // 2):
                two = [ROPE, 2, T]
                dve.wait_ge(s["ropemm"], p + 1)
                q2 = Q[R, 2 * p:2 * p + 2, :]
                r0 = rt[R, 0, :].rearrange("p (a t) -> p a t", t=T)
                r1 = rt[R, 1, :].rearrange("p (a t) -> p a t", t=T)
                if p:
                    dve.wait_ge(s["rope_done"], p)
                v.tensor_tensor(r0, bank[p % 2][R, :].rearrange("p (a t) -> p a t", t=T), sin.broadcast_to(two),
                                ALU.mult).then_inc(s["rope_mul"], 1)
                dve.wait_ge(s["rope_mul"], p + 1)
                link(v.tensor_tensor(r1, q2, cos.broadcast_to(two), ALU.mult))
                v.tensor_tensor(q2, r0, r1, ALU.add).then_inc(s["rope_done"], 1)
            mod_out(2)
            mod_out(3)

            scale = QK ** -0.5
            dve.wait_ge(s["v_sb"], 4)

            def divide(parts, heads, o, sums, rn):
                for b, src in enumerate(parts):
                    v.tensor_tensor(o[:, b, :].rearrange("p (h c) -> p h c", c=HD),
                                    src.rearrange("p (h c) -> p h c", c=HD),
                                    rn[:, b, heads].unsqueeze(2).broadcast_to([P, 8, HD]), ALU.mult).then_inc(sums, 1)

            for h in range(HEADS + 1):
                if h < HEADS:
                    dve.wait_ge(s["mscore"], h + 1)
                    if h >= 2:
                        dve.wait_ge(s["mprobT"], h - 1)
                    k = bank[h % 2]
                    pr = prob[:, h % 2, :]
                    v.tensor_tensor_reduce(out=pr[:, 0:P], in0=k[:, 0:P], in1=causal, scale=-scale, scalar=HUGE,
                                           op0=ALU.add, op1=ALU.min, accum_out=nmax[:, 0, h:h + 1])\
                        .then_inc(s["masked"], 1)
                    v.tensor_tensor_reduce(out=pr[:, P:3 * P], in0=k[:, P:3 * P], in1=con[:, C_OPEN:C_OPEN + 2 * P],
                                           scale=-scale, scalar=HUGE, op0=ALU.add, op1=ALU.min,
                                           accum_out=nmax[:, 1, h:h + 1]).then_inc(s["masked"], 1)
                if h >= 1:
                    g = h - 1
                    for i in range(3 * g // 2, 3 * (g + 1) // 2):
                        ada_strip(4 + i // KT, i % KT)
                if h in (9, HEADS):
                    a = 0 if h == 9 else 8
                    if h == HEADS:
                        dve.wait_ge(s["mpv"], HEADS)
                    dve.wait_ge(s["mpv"], a + 8 if h == HEADS else 8)
                    dve.wait_ge(s["expd"], 2 * (a + 8))
                    link(v.reciprocal(rinv[:, :, a:a + 8], rsum[:, :, a:a + 8]))
                    divide([upper[2 * (a // 8)], upper[2 * (a // 8) + 1]], slice(a, a + 8),
                           O[:, :, a * VD:(a + 8) * VD], s["o_norm"], rinv)
            mod_out(4)
            scale_of(1, SC_F, V_FFN)

            def dense_lo(c, u):
                n = width(c) * KT
                dve.wait_ge(s[("dg_hi", "du_hi", "dd_hi")[u]], c + 1)
                v.tensor_tensor(ff_lo[:, u, 0:n], slot(T_FFN + 3 * c + u)[:, 0:n], ff_hi[:, u, 0:n].bitcast(F32),
                                ALU.subtract).then_inc(s[("dg_lo", "du_lo", "dd_lo")[u]], 1)

            def dense_hidden(c):
                n = width(c) // P
                dve.wait_ge(s["silu_done"], c + 1)
                dve.wait_ge(s["upmm"], c + 1)
                v.tensor_tensor(hid[:, 0:n, :], bank[1][:, 0:n * T].rearrange("p (j t) -> p j t", t=T),
                                sg[:, 0:n, :], ALU.mult).then_inc(s["hid_ready"], 1)

            def dense_hidden_lo(c):
                n = width(c) // P
                dve.wait_ge(s["hid_hi_done"], c + 1)
                v.tensor_tensor(hid_lo[:, 0:n, :], hid[:, 0:n, :], hid_hi[:, 0:n, :].bitcast(F32),
                                ALU.subtract).then_inc(s["hid_lo_done"], 1)

            for u in range(3):
                dense_lo(0, u)
            for d in range(KT):
                dve.wait_ge(s["omm"], d + 1)
                residual(d, upper[d % 4][:, 0:T], GT_M)
                if d < KT - 1:
                    ada_strip(7, d if d == 0 else d + 1)
                if d == 0:
                    ada_strip(7, 1)
            inverse(1)
            norm_split(1, SH_F, nT, nT_hi, nT_lo)
            mod_out(5, bank[1])
            mod_out(6, bank[2])
            mod_out(7, bank[3])

            def mod_out_half(b):
                i = (b - 8) % 3
                dve.wait_ge(s["ada_reduced"], b + 1)
                v.tensor_tensor(mod[:, b * KT:(b + 1) * KT], bank[3][:, i * KT:(i + 1) * KT],
                                bcol[:, b * KT:(b + 1) * KT], ALU.add).then_inc(s["mod_ready"], 1)

            strips_done = 0

            def add_strips(n):
                nonlocal strips_done
                for i in range(strips_done, strips_done + n):
                    ada_strip(8 + i // KT, i % KT)
                strips_done += n

            for c in range(CHUNKS):
                if c:
                    dense_hidden(c - 1)
                    add_strips(1)
                    dense_hidden_lo(c - 1)
                    dense_lo(c, 1)
                else:
                    add_strips(1)
                add_strips(1)
                if c < CHUNKS - 1:
                    dense_lo(c + 1, 0)
                add_strips(1)
                if c:
                    dense_lo(c, 2)
                add_strips(1)
                if c in (3, 5, 6, 9, 11):
                    mod_out_half({3: 8, 5: 9, 6: 10, 9: 11, 11: 12}[c])
            dense_hidden(CHUNKS - 1)
            dense_hidden_lo(CHUNKS - 1)
            mod_out_half(13)
            scale_of(2, KV_SC, V_KV)
            scale_of(3, L1 + SC_M, V_MIX + KT)
            scale_of(4, L1 + SC_F, V_FFN + KT)
            dve.wait_ge(s["downmm"], CHUNKS)
            for d in range(KT):
                residual(d, wide[:, d * T:(d + 1) * T], GT_F)

            def kq_split_lo(i):
                dve.wait_ge(s["kq_hi_done"], i + 1)
                v.tensor_tensor(kq_lo[i % 2][:, :], slot(T_KVB + i), kq_hi[i % 2][:, :].bitcast(F32),
                                ALU.subtract).then_inc(s["kq_lo_done"], 1)

            kq_split_lo(0)
            inverse(2)
            norm_split(2, KV_SH, nT, nT_hi, nT_lo)
            dve.wait_ge(s["rel_stored"], 16 * GROUPS)
            kq_split_lo(1)
            norm_split(3, L1 + SH_M, n2T, n2_hi, n2_lo)
            for i in range(2, 18):
                kq_split_lo(i)

            for u in range(2 * SLOTS + 1):
                if u < 2 * SLOTS:
                    h, b = divmod(u, 2)
                    dve.wait_ge(s["dscore"], u + 1)
                    if b == 0:
                        dve.wait_ge(rel_in[h % 2], 16 * (h // 2 + 1))
                    if h >= 2:
                        dve.wait_ge(s["dprobT"], 3 * (h - 2) + (1 if b == 0 else 3))
                    pd = pds[h % 2]
                    n = (b + 1) * P
                    if b == 0:
                        src, dst = bank[0][:, 0:3 * P], pd[:, 0:3 * P]
                        parts = [(src.rearrange("p (g n) -> p g n", n=n), dst.rearrange("p (g n) -> p g n", n=n),
                                  relT[:, h % 2, :, P:2 * P])]
                    else:
                        parts = []
                        parts.append((bank[1][:, :].rearrange("p (g n) -> p g n", n=n),
                                      pd[:, 3 * P:7 * P].rearrange("p (g n) -> p g n", n=n), relT[:, h % 2, 0:2, :]))
                        parts.append((bank[2][:, 0:T], pd[:, 7 * P:9 * P], relT[:, h % 2, 2, :]))
                    for i, (a, o, bias) in enumerate(parts):
                        start = HUGE if i == 0 else npart[:, h:h + 1]
                        acc = nmax[:, b, h:h + 1] if i == len(parts) - 1 else npart[:, h:h + 1]
                        ins = v.tensor_tensor_reduce(out=o, in0=a, in1=bias, scale=-HD ** -0.5, scalar=start,
                                                     op0=ALU.add, op1=ALU.min, accum_out=acc)
                        if i < len(parts) - 1:
                            link(ins)
                    ins.then_inc(s["dmask"], 1)
                for q in {0: (), 1: (0,)}.get(u, ((3 * (u // 2) - 2, 3 * (u // 2) - 1) if u % 2 == 0
                                                  else (3 * (u // 2),))):
                    dve.wait_ge(s["dprobT"], q + 1)
                    if q >= 2:
                        dve.wait_ge(s["dpv"], q - 1)
                    v.tensor_copy(pdT[:, q % 2, :], (bank[3] if q % 2 == 0 else upper[0])[:, 0:3 * P])\
                        .then_inc(s["dprobT_sb"], 1)
            dve.wait_ge(s["dpv"], 3 * SLOTS)
            dve.wait_ge(s["dexp"], 2 * SLOTS)
            link(v.reciprocal(rinv[:, :, 0:SLOTS], rsum[:, :, 0:SLOTS]))
            divide([upper[1], upper[2]], slice(0, SLOTS), Od, s["od_norm"], rinv)
            def weight_lo(e, c, u):
                n = dve_share(c, u)
                dve.wait_ge(s["hi_" + UNITS[u]], e * CHUNKS + c + 1)
                v.tensor_tensor(w_lo[:, u, 0:n], slot(T_MOE + 3 * c + u)[:, 0:n], w_hi[:, u, 0:n].bitcast(F32),
                                ALU.subtract).then_inc(s["lo_" + UNITS[u]], 1)

            weight_lo(0, 0, 0)
            weight_lo(0, 0, 1)
            for d in range(KT):
                dve.wait_ge(s["odmm"], d + 1)
                residual(d, upper[d % 4][:, 0:T], L1 + GT_M)
            inverse(3)
            norm(4, nT)

            dve.wait_ge(s["logit"], 1)
            sm = [small[:, i, :, 0:NE] for i in range(12)]
            chosen, gate, lg, first, second, rest, eq, tmp = sm[:8]
            one = [P, TB, NE]
            for b in range(TB):
                link(v.tensor_copy(lg[:, b, :], bank[2 + b][:, 0:NE]))
            down_count = con[:, C_IOTA + 1:C_IOTA + 1 + NE]
            for vals, hot, best in ((lg, first, sm[9][:, :, 0:1]), (rest, second, sm[9][:, :, 1:2])):
                link(v.tensor_reduce(best, vals, AX_X, ALU.max))
                link(v.tensor_tensor(eq, vals, best.broadcast_to(one), ALU.is_equal))
                for b in range(TB):
                    link(v.scalar_tensor_tensor(out=tmp[:, b, :], in0=down_count, scalar=-9.0, in1=eq[:, b, :],
                                                op0=ALU.add, op1=ALU.mult))
                link(v.tensor_reduce(sm[9][:, :, 2:3], tmp, AX_X, ALU.min))
                link(v.tensor_tensor(hot, tmp, sm[9][:, :, 2:3].broadcast_to(one), ALU.is_equal))
                if hot is first:
                    link(v.scalar_tensor_tensor(out=rest, in0=first, scalar=-HUGE, in1=lg, op0=ALU.mult, op1=ALU.add))
            v.tensor_tensor(chosen, first, second, ALU.add).then_inc(s["routed"], 1)
            v.tensor_tensor(sm[8][:, :, 1:2], sm[9][:, :, 1:2], sm[9][:, :, 0:1], ALU.subtract)\
                .then_inc(s["routed_gap"], 1)
            dve.wait_ge(s["gap_exp"], 1)
            link(v.tensor_scalar(sm[9][:, :, 3:4], sm[8][:, :, 0:1], 1.0, None, ALU.add))
            link(v.reciprocal(sm[9][:, :, 4:5], sm[9][:, :, 3:4]))
            link(v.tensor_tensor(sm[9][:, :, 5:6], sm[9][:, :, 4:5], sm[8][:, :, 0:1], ALU.mult))
            link(v.tensor_tensor(gate, first, sm[9][:, :, 4:5].broadcast_to(one), ALU.mult))
            link(v.tensor_tensor(tmp, second, sm[9][:, :, 5:6].broadcast_to(one), ALU.mult))
            link(v.tensor_tensor(gate, gate, tmp, ALU.add))
            dve.wait_ge(s["rankmm"], 1)
            rank = sm[10]
            link(v.tensor_copy(rank, bank[2][:, 0:TB * NE].rearrange("p (b e) -> p b e", e=NE)))
            v.tensor_copy(counts[:, 0:NE], bank[2][0:1, 2 * NE:3 * NE]).then_inc(s["count_sb"], 1)
            dve.wait_ge(s["count_sb"], 1)

            def select_tokens(e):
                for b in range(TB):
                    r = small[:, 10, b, bass.ds(e, 1)]
                    v.tensor_scalar(sel[:, b, :], iota, r, small[:, 0, b, bass.ds(e, 1)], ALU.is_equal, ALU.mult)
                    ins = v.tensor_scalar(selg[:, b, :], iota, r, small[:, 1, b, bass.ds(e, 1)], ALU.is_equal, ALU.mult)
                ins.then_inc(s["selmade"], 1)

            def columns_lo(e, k, src):
                dve.wait_ge(s[f"xg_hi{k}"], e + 1)
                for i in range(2):
                    at = (slice(None), slice(4 * i, 4 * i + 4), slice(k * P, (k + 1) * P))
                    ins = v.tensor_tensor(xg_lo[at], src[i].rearrange("p (d n) -> p d n", n=P),
                                          xg_hi[at].bitcast(F32), ALU.subtract)
                ins.then_inc(s[f"xg_lo{k}"], 1)

            def second_block(e, nb):
                if nb == 2:
                    columns_lo(e, 1, bank23)
                else:
                    dve.sem_inc(s["xg_lo1"], 1)

            def add_results(e):
                dve.wait_ge(s["scatmm"], e + 1)
                for i in range(4):
                    m = moe[:, 2 * i:2 * i + 2, :]
                    ins = v.tensor_tensor(m, upper[i].rearrange("p (a t) -> p a t", t=T), m, ALU.add)
                ins.then_inc(s["moe_sum"], 1)

            def expert(e, nb):
                c0 = e * CHUNKS

                def gated_hidden(c):
                    w = width(c)
                    dve.wait_ge(s["e_silu"], c0 + c + 1)
                    if c:
                        dve.wait_ge(s["e_hT"], c0 + c)
                    for k in range(nb):
                        ins = v.tensor_tensor(hidden[:, k, 0:w], bank[c % 2 if nb == 1 else k][:, w:2 * w],
                                              gate_act[:, k, 0:w], ALU.mult)
                    ins.then_inc(s["e_hid"], 1)

                def hidden_lo(c):
                    nf = width(c) // P
                    dve.wait_ge(s["hT_hi_done"], c0 + c + 1)
                    v.tensor_tensor(hT_lo[:, 0:nf, 0:nb * P], bank[2][:, 0:nf * nb * P].rearrange("p (f n) -> p f n", f=nf),
                                    hT_hi[:, 0:nf, 0:nb * P].bitcast(F32), ALU.subtract).then_inc(s["hT_lo_done"], 1)

                for c in range(1, CHUNKS):
                    weight_lo(e, c, 0)
                    gated_hidden(c - 1)
                    weight_lo(e, c, 1)
                    if c == 1:
                        add_results(e)
                    weight_lo(e, c - 1, 2)
                    hidden_lo(c - 1)
                    if c == CHUNKS // 2:
                        unless_last(dve, e, lambda: (dve.wait_ge(s["selT"], e + 1), select_tokens(e + 1)))

                def last_chunk_and_next():
                    gated_hidden(CHUNKS - 1)
                    weight_lo(e, CHUNKS, 0)
                    weight_lo(e, CHUNKS - 1, 2)
                    hidden_lo(CHUNKS - 1)
                    if nb == 1:
                        columns_lo(e + 1, 0, free23)
                    weight_lo(e, CHUNKS, 1)
                    if nb == 2:
                        columns_lo(e + 1, 0, bank23)

                def last_chunk():
                    gated_hidden(CHUNKS - 1)
                    weight_lo(e, CHUNKS - 1, 2)
                    hidden_lo(CHUNKS - 1)

                with dve.If(e < NE - 1):
                    last_chunk_and_next()
                with dve.Else():
                    last_chunk()

            bank23 = (bank[2][:, :], bank[3][:, :])
            free23 = (upper[2], upper[3])
            dve.wait_ge(s["moe_sum"], 1)
            select_tokens(0)
            columns_lo(0, 0, bank23)
            by_blocks(dve, 0, lambda nb: second_block(0, nb))
            with dve.Fori(0, NE) as e:
                by_blocks(dve, e, lambda nb: expert(e, nb))
                unless_last(dve, e, lambda: by_blocks(dve, e + 1, lambda nb: second_block(e + 1, nb)))
            add_results(NE)
            dve.wait_ge(s["moe_sum"], NE + 2)
            for d in range(KT):
                residual(d, moe[:, d, :], L1 + GT_F)
            inverse(4)
            for j in range(KT):
                v.scalar_tensor_tensor(out=nT[:, j, :], in0=hT[:, j, :], scalar=vec[:, V_FINAL + j:V_FINAL + j + 1],
                                       in1=rstd[:, 0, :], op0=ALU.mult, op1=ALU.mult).then_inc(s["scaled"], 1)
            for i in range(1, 4, 2):
                dve.wait_ge(s["finT"], i + 1)
                v.tensor_copy(otok[:, i // 2, 512:D], upper[i]).then_inc(s["fin_dve"], 1)


def constants():
    import numpy as np
    con = np.zeros((P, NCONST), np.float32)
    con[:, C_ID:C_ID + P] = np.eye(P)
    i = np.arange(ROPE // 2)
    con[NOPE + ROPE // 2 + i, C_PERM + i] = -1.0
    con[NOPE + i, C_PERM + ROPE // 2 + i] = 1.0
    q, k = np.arange(P)[:, None], np.arange(P)[None, :]
    con[:, C_CAUSAL:C_CAUSAL + P] = np.where(k <= q, 0.0, -BIG)
    con[:, C_BEFORE:C_BEFORE + P] = q < k
    con[:, C_IOTA:C_IOTA + T] = np.arange(T)
    freq = np.float32(10000.0) ** (-np.arange(0, ROPE, 2, dtype=np.float32) / np.float32(ROPE))
    con[NOPE:QK, C_FREQ] = np.concatenate([freq, freq])
    onehot = np.zeros((BUCKETS, GROUPS, NREL), np.float32)
    relmask = np.zeros((SLOTS, GROUPS, NREL), np.float32)
    exact = BUCKETS // 2
    for g, (dil, span) in enumerate(zip(DILATIONS, SPANS)):
        for m in range(NREL):
            d = T - 1 - m
            if d < 0 or d % dil or d // dil > span:
                relmask[:, g, m] = -BIG
                continue
            big = exact + int(np.log(np.float32(max(d, 1)) / np.float32(exact)) / np.float32(np.log(2048 / exact))
                              * np.float32(BUCKETS - exact))
            onehot[d if d < exact else min(big, BUCKETS - 1), g, m] = 1.0
    return con, onehot.reshape(BUCKETS, -1), relmask.reshape(SLOTS, -1)


_INS = ['x', 'c', 'positions', 'g_mix', 'g_ffn', 'w_ada', 'b_ada', 'w_mla_in', 'g_mla_q', 'w_mla_q_up', 'g_mla_kv',
        'w_mla_kv_up', 'w_mla_out', 'g_kv_b', 'w_ada_kv', 'b_ada_kv', 'w_kv_b', 'rpb_table', 'w_q_b', 'w_o_b',
        'w_ffn_gu', 'w_ffn_down', 'w_router', 'w_exp_gu', 'w_exp_down', 'g_final']


def kernel(**inputs):
    import numpy as _np
    import concourse.bacc as _bacc
    from concourse import mybir as _mybir
    from concourse.bass_utils import run_bass_kernel_spmd as _run

    nc = _bacc.Bacc("TRN2", target_bir_lowering=False, num_devices=1)
    arrays, args = {}, []
    given = [(name, _np.ascontiguousarray(inputs[name])) for name in _INS]
    given += list(zip(("consts", "onehot", "relmask"), constants()))
    for name, a in given:
        arrays[f"in_{name}"] = a
        args.append(nc.dram_tensor(f"in_{name}", a.shape, _mybir.dt.from_np(a.dtype), kind="ExternalInput").ap())
    args.append(nc.dram_tensor("out_0", (1, T, D), _mybir.dt.float32, kind="ExternalOutput").ap())
    trunk(nc, *args)
    r = _run(nc, [arrays], core_ids=[0])
    return r.results[0]["out_0"]
```
